# Optimizing a Trainium2 kernel written in Bass

```python
import math
import jax, jax.numpy as jnp
from jax import lax
import numpy as np

D_MODEL = 1024
BATCH = 1
SEQ = 512
DEPTH = 2

EPS = 1e-6
N_BRANCHES = 3

POOL_WINDOWS = (2, 4, 8, 16)
POOL_GROUP = 128
POOL_WIDTH = POOL_GROUP * len(POOL_WINDOWS)

SSM_GROUP = 16
SSM_GROUPS = 32
SSM_WIDTH = SSM_GROUP * SSM_GROUPS
SSM_STATE = 64

HEAD_DIM = 64
HEADS_PER_GROUP = 4
ATTN_PATTERNS = ((128, 1), (512, 4), (2048, 16))
ATTN_HEADS = HEADS_PER_GROUP * len(ATTN_PATTERNS)
ATTN_WIDTH = ATTN_HEADS * HEAD_DIM
ATTN_OUT = HEADS_PER_GROUP * HEAD_DIM
ATTN_BLOCK = 128
ROPE_THETA = 10000.0

IN_SPLITS = (POOL_WIDTH, SSM_WIDTH, ATTN_WIDTH, ATTN_WIDTH, ATTN_WIDTH, N_BRANCHES * D_MODEL)
IN_COLS = sum(IN_SPLITS)

PEER_HEADS = 8
PEER_NKEYS = 128
PEER_EXPERTS = PEER_NKEYS * PEER_NKEYS
PEER_QDIM = 256
PEER_TOPK = 16
PEER_CHUNK = 128

kernel_name = "hybrid_pool_s5_dilated_attn_peer"

F32 = jnp.float32

def rmsnorm(x, g):
    xf = x.astype(F32)
    y = xf * lax.rsqrt(jnp.mean(xf * xf, axis=-1, keepdims=True) + EPS)
    return (y * g.astype(F32)).astype(x.dtype)

def pool_branch(u, w, scale):
    B, L, _ = u.shape
    uf = u.astype(F32)
    cs = jnp.concatenate([jnp.zeros((B, 1, POOL_WIDTH), F32), jnp.cumsum(uf, axis=1)], axis=1)
    t = jnp.arange(L)
    outs = []
    for gi, win in enumerate(POOL_WINDOWS):
        sl = slice(gi * POOL_GROUP, (gi + 1) * POOL_GROUP)
        start = jnp.maximum(t + 1 - win, 0)
        count = (t + 1 - start).astype(F32)[None, :, None]
        outs.append((cs[:, 1:, sl] - cs[:, start, sl]) / count - uf[:, :, sl])
    pooled = jnp.stack(outs, axis=2)
    mixed = jnp.einsum('blgc,gcd->blgd', pooled, w.astype(F32)).reshape(B, L, POOL_WIDTH)
    return (mixed * scale.astype(F32)).astype(u.dtype)

def diag_linear_scan(a_re, a_im, b_re, b_im):
    def combine(left, right):
        lar, lai, lbr, lbi = left
        rar, rai, rbr, rbi = right
        return (lar * rar - lai * rai,
                lar * rai + lai * rar,
                rar * lbr - rai * lbi + rbr,
                rar * lbi + rai * lbr + rbi)
    _, _, s_re, s_im = lax.associative_scan(combine, (a_re, a_im, b_re, b_im), axis=0)
    return s_re, s_im

def ssm_branch(u, a_re, a_im, log_dt, b_re, b_im, c_re, c_im, d_skip, w_glu):
    B, L, _ = u.shape
    uf = u.astype(F32).reshape(B, L, SSM_GROUPS, SSM_GROUP)
    dt = jnp.exp(log_dt.astype(F32))[:, None]
    ar, ai = a_re.astype(F32), a_im.astype(F32)
    decay = jnp.exp(ar * dt)
    abar_re = decay * jnp.cos(ai * dt)
    abar_im = decay * jnp.sin(ai * dt)
    den = ar * ar + ai * ai
    nr = abar_re - 1.0
    k_re = (nr * ar + abar_im * ai) / den
    k_im = (abar_im * ar - nr * ai) / den
    br, bi = b_re.astype(F32), b_im.astype(F32)
    bbar_re = k_re[:, :, None] * br - k_im[:, :, None] * bi
    bbar_im = k_re[:, :, None] * bi + k_im[:, :, None] * br
    x_re = jnp.einsum('blgp,gnp->blgn', uf, bbar_re)
    x_im = jnp.einsum('blgp,gnp->blgn', uf, bbar_im)
    a_seq_re = jnp.broadcast_to(abar_re, (L,) + abar_re.shape)
    a_seq_im = jnp.broadcast_to(abar_im, (L,) + abar_im.shape)
    s_re, s_im = jax.vmap(diag_linear_scan, in_axes=(None, None, 0, 0))(a_seq_re, a_seq_im, x_re, x_im)
    y = (jnp.einsum('blgn,gpn->blgp', s_re, c_re.astype(F32))
         - jnp.einsum('blgn,gpn->blgp', s_im, c_im.astype(F32))
         + d_skip.astype(F32).reshape(SSM_GROUPS, SSM_GROUP) * uf)
    y = jax.nn.gelu(y.reshape(B, L, SSM_WIDTH))
    val, gate = jnp.split(y @ w_glu.astype(F32), 2, axis=-1)
    return (val * jax.nn.sigmoid(gate)).astype(u.dtype)

def rope(x, positions):
    half = HEAD_DIM // 2
    inv_freq = ROPE_THETA ** (-jnp.arange(half, dtype=F32) / half)
    ang = positions.astype(F32)[..., None] * inv_freq
    cos = jnp.cos(ang)[:, :, None, :]
    sin = jnp.sin(ang)[:, :, None, :]
    x1, x2 = x[..., :half], x[..., half:]
    return jnp.concatenate([x1 * cos - x2 * sin, x2 * cos + x1 * sin], axis=-1)

def dilated_window_attention(q, k, v, dilation, n_back):
    B, L, H, Dh = q.shape
    span = dilation * ATTN_BLOCK
    Lp = -(-L // span) * span
    pad = Lp - L
    M = Lp // dilation
    nb = M // ATTN_BLOCK

    def to_blocks(a):
        a = jnp.pad(a, ((0, 0), (0, pad), (0, 0), (0, 0)))
        a = a.reshape(B, M, dilation, H, Dh).transpose(0, 2, 3, 1, 4)
        return a.reshape(B, dilation, H, nb, ATTN_BLOCK, Dh)

    def with_prev(a):
        prev = jnp.pad(a, ((0, 0), (0, 0), (0, 0), (1, 0), (0, 0), (0, 0)))[:, :, :, :-1]
        return jnp.concatenate([prev, a], axis=4)

    qb = to_blocks(q)
    kc = with_prev(to_blocks(k))
    vc = with_prev(to_blocks(v))
    s = jnp.einsum('brhnqd,brhnkd->brhnqk', qb, kc) * (Dh ** -0.5)
    qi = jnp.arange(ATTN_BLOCK)[:, None] + ATTN_BLOCK
    ki = jnp.arange(2 * ATTN_BLOCK)[None, :]
    dist = qi - ki
    band = (dist >= 0) & (dist <= n_back)
    has_prev = (jnp.arange(nb)[:, None, None] > 0) | (ki[None] >= ATTN_BLOCK)
    mask = band[None] & has_prev
    s = jnp.where(mask, s, -jnp.inf)
    m = jnp.max(s, axis=-1, keepdims=True)
    p = jnp.exp(s - m)
    den = jnp.sum(p, axis=-1, keepdims=True)
    o = jnp.einsum('brhnqk,brhnkd->brhnqd', p, vc) / den
    lse = (m + jnp.log(den))[..., 0]
    o = o.reshape(B, dilation, H, M, Dh).transpose(0, 3, 1, 2, 4).reshape(B, Lp, H, Dh)[:, :L]
    lse = lse.reshape(B, dilation, H, M).transpose(0, 3, 1, 2).reshape(B, Lp, H)[:, :L]
    return o, lse

def attention_branch(q, k, v, positions):
    B, L, _ = q.shape
    q = rope(q.astype(F32).reshape(B, L, ATTN_HEADS, HEAD_DIM), positions)
    k = rope(k.astype(F32).reshape(B, L, ATTN_HEADS, HEAD_DIM), positions)
    v = v.astype(F32).reshape(B, L, ATTN_HEADS, HEAD_DIM)
    outs, lses = [], []
    for gi, (window, dil) in enumerate(ATTN_PATTERNS):
        hs = slice(gi * HEADS_PER_GROUP, (gi + 1) * HEADS_PER_GROUP)
        o, lse = dilated_window_attention(q[:, :, hs], k[:, :, hs], v[:, :, hs], dil, window // dil)
        outs.append(o)
        lses.append(lse)
    w = jax.nn.softmax(jnp.stack(lses), axis=0)
    out = jnp.einsum('gblh,gblhd->blhd', w, jnp.stack(outs))
    return out.reshape(B, L, ATTN_OUT)

def peer_ffn(h, wq, k1, k2, u_tab, v_tab):
    B, L, D = h.shape
    q = (h @ wq).astype(F32).reshape(B, L, PEER_HEADS, 2, PEER_QDIM // 2)
    s1 = jnp.einsum('blhc,kc->blhk', q[..., 0, :], k1.astype(F32))
    s2 = jnp.einsum('blhc,kc->blhk', q[..., 1, :], k2.astype(F32))
    v1, i1 = lax.top_k(s1, PEER_TOPK)
    v2, i2 = lax.top_k(s2, PEER_TOPK)
    cand_s = (v1[..., :, None] + v2[..., None, :]).reshape(B, L, PEER_HEADS, PEER_TOPK * PEER_TOPK)
    cand_i = (i1[..., :, None] * PEER_NKEYS + i2[..., None, :]).reshape(B, L, PEER_HEADS, PEER_TOPK * PEER_TOPK)
    top_s, pos = lax.top_k(cand_s, PEER_TOPK)
    expert = jnp.take_along_axis(cand_i, pos, axis=-1)
    gate = jax.nn.softmax(top_s, axis=-1)
    n_chunks = (B * L) // PEER_CHUNK
    hc = h.reshape(n_chunks, PEER_CHUNK, D)
    ec = expert.reshape(n_chunks, PEER_CHUNK, PEER_HEADS * PEER_TOPK)
    gc = gate.reshape(n_chunks, PEER_CHUNK, PEER_HEADS * PEER_TOPK).astype(h.dtype)

    def eval_chunk(args):
        hx, e, g = args
        a = jnp.einsum('cd,ckd->ck', hx, u_tab[e])
        return jnp.einsum('ck,ckd->cd', g * jax.nn.gelu(a), v_tab[e])

    out = lax.map(eval_chunk, (hc, ec, gc))
    return out.reshape(B, L, D)

def setup_inputs(seed: int = 0) -> dict:
    key = jax.random.key(seed)
    ks = list(jax.random.split(key, 32))

    def nrm(i, shape, scale):
        return jax.random.normal(ks[i], shape, F32) * scale

    n_idx = jnp.arange(SSM_STATE, dtype=F32)
    x = nrm(0, (BATCH, SEQ, D_MODEL), 1.0)
    positions = (jnp.arange(SEQ, dtype=jnp.int32)[None, :]
                 + jax.random.randint(ks[1], (BATCH, 1), 0, 1024, dtype=jnp.int32))
    norm1_g = 1.0 + nrm(2, (DEPTH, D_MODEL), 0.02)
    w_in = nrm(3, (DEPTH, D_MODEL, IN_COLS), D_MODEL ** -0.5)
    pool_w = nrm(4, (DEPTH, len(POOL_WINDOWS), POOL_GROUP, POOL_GROUP), POOL_GROUP ** -0.5)
    pool_scale = 1.0 + nrm(5, (DEPTH, POOL_WIDTH), 0.02)
    pool_proj = nrm(6, (DEPTH, POOL_WIDTH, D_MODEL), POOL_WIDTH ** -0.5)
    ssm_a_re = -0.5 + nrm(7, (DEPTH, SSM_GROUPS, SSM_STATE), 0.01)
    ssm_a_im = math.pi * n_idx + nrm(8, (DEPTH, SSM_GROUPS, SSM_STATE), 0.01)
    ssm_log_dt = jax.random.uniform(ks[9], (DEPTH, SSM_GROUPS), F32, math.log(1e-3), math.log(1e-1))
    b_scale = (2.0 * SSM_GROUP) ** -0.5
    ssm_b_re = nrm(10, (DEPTH, SSM_GROUPS, SSM_STATE, SSM_GROUP), b_scale)
    ssm_b_im = nrm(11, (DEPTH, SSM_GROUPS, SSM_STATE, SSM_GROUP), b_scale)
    c_scale = (2.0 * SSM_STATE) ** -0.5 * 4.0
    ssm_c_re = nrm(12, (DEPTH, SSM_GROUPS, SSM_GROUP, SSM_STATE), c_scale)
    ssm_c_im = nrm(13, (DEPTH, SSM_GROUPS, SSM_GROUP, SSM_STATE), c_scale)
    ssm_d = nrm(14, (DEPTH, SSM_WIDTH), 1.0)
    ssm_glu = nrm(15, (DEPTH, SSM_WIDTH, 2 * SSM_WIDTH), SSM_WIDTH ** -0.5)
    ssm_proj = nrm(16, (DEPTH, SSM_WIDTH, D_MODEL), SSM_WIDTH ** -0.5)
    attn_proj = nrm(17, (DEPTH, ATTN_OUT, D_MODEL), ATTN_OUT ** -0.5)
    w_out = nrm(18, (DEPTH, D_MODEL, D_MODEL), D_MODEL ** -0.5)
    norm2_g = 1.0 + nrm(19, (DEPTH, D_MODEL), 0.02)
    peer_wq = nrm(20, (DEPTH, D_MODEL, PEER_HEADS * PEER_QDIM), D_MODEL ** -0.5)
    peer_k1 = nrm(21, (DEPTH, PEER_NKEYS, PEER_QDIM // 2), (PEER_QDIM // 2) ** -0.5)
    peer_k2 = nrm(22, (DEPTH, PEER_NKEYS, PEER_QDIM // 2), (PEER_QDIM // 2) ** -0.5)
    peer_u = nrm(23, (DEPTH, PEER_EXPERTS, D_MODEL), D_MODEL ** -0.5)
    peer_v = nrm(24, (DEPTH, PEER_EXPERTS, D_MODEL), PEER_HEADS ** -0.5)
    final_g = 1.0 + nrm(25, (D_MODEL,), 0.02)
    return {"x": x, "positions": positions, "norm1_g": norm1_g, "w_in": w_in,
            "pool_w": pool_w, "pool_scale": pool_scale, "pool_proj": pool_proj,
            "ssm_a_re": ssm_a_re, "ssm_a_im": ssm_a_im, "ssm_log_dt": ssm_log_dt,
            "ssm_b_re": ssm_b_re, "ssm_b_im": ssm_b_im, "ssm_c_re": ssm_c_re, "ssm_c_im": ssm_c_im,
            "ssm_d": ssm_d, "ssm_glu": ssm_glu, "ssm_proj": ssm_proj, "attn_proj": attn_proj,
            "w_out": w_out, "norm2_g": norm2_g, "peer_wq": peer_wq, "peer_k1": peer_k1,
            "peer_k2": peer_k2, "peer_u": peer_u, "peer_v": peer_v, "final_g": final_g}

def reference(x, positions, norm1_g, w_in, pool_w, pool_scale, pool_proj,
              ssm_a_re, ssm_a_im, ssm_log_dt, ssm_b_re, ssm_b_im, ssm_c_re, ssm_c_im,
              ssm_d, ssm_glu, ssm_proj, attn_proj, w_out, norm2_g, peer_wq, peer_k1,
              peer_k2, peer_u, peer_v, final_g):
    B, L, D = x.shape
    offsets = [int(o) for o in np.cumsum(IN_SPLITS)[:-1]]
    for l in range(DEPTH):
        h = rmsnorm(x, norm1_g[l])
        z = h @ w_in[l]
        u_pool, u_ssm, q, k, v, gate_logits = jnp.split(z, offsets, axis=-1)
        y_pool = pool_branch(u_pool, pool_w[l], pool_scale[l]) @ pool_proj[l]
        y_ssm = ssm_branch(u_ssm, ssm_a_re[l], ssm_a_im[l], ssm_log_dt[l], ssm_b_re[l], ssm_b_im[l],
                           ssm_c_re[l], ssm_c_im[l], ssm_d[l], ssm_glu[l]) @ ssm_proj[l]
        y_attn = attention_branch(q, k, v, positions).astype(x.dtype) @ attn_proj[l]
        g = jax.nn.sigmoid(gate_logits).reshape(B, L, N_BRANCHES, D)
        merged = g[:, :, 0] * y_pool + g[:, :, 1] * y_ssm + g[:, :, 2] * y_attn
        x = x + merged @ w_out[l]
        h2 = rmsnorm(x, norm2_g[l])
        x = x + peer_ffn(h2, peer_wq[l], peer_k1[l], peer_k2[l], peer_u[l], peer_v[l])
    return rmsnorm(x, final_g)


_drawn_inputs = setup_inputs


def setup_inputs(seed=0):
    import zlib

    import numpy as np

    out = dict(_drawn_inputs(seed))
    spreads = {}
    factors = {}
    for name, (base, spread) in spreads.items():
        noise = np.random.default_rng([zlib.crc32(name.encode()), seed]).standard_normal(out[name].shape)
        drawn = base * np.exp(spread * noise) if base else spread * noise
        out[name] = __import__('jax').numpy.asarray(drawn.astype(out[name].dtype))
    for name, factor in factors.items():
        out[name] = (out[name] * factor).astype(out[name].dtype)
    return out
```

```python
import math
from contextlib import ExitStack

import numpy as np

import concourse.bass as bass
from concourse import mybir

F32 = mybir.dt.float32
I32 = mybir.dt.int32
U32 = mybir.dt.uint32
ALU = mybir.AluOpType
ACT = mybir.ActivationFunctionType
AX = mybir.AxisListType

P = 128
L = 512
D = 1024
DEPTH = 2
KD = D // P
NT = L // P
EPS = 1e-6

POOL_WINDOWS = (2, 4, 8, 16)
PAIRS = 16
PER_TILE = 4
HEAD = 64
SLOTS = 4
KEYS = L + 2 * P
SCALE = HEAD ** -0.5
NEG = -1e30
LOWEST = -3.0e38

W_IN_MAIN = 3328
CHUNK = 17 * P
RING = 4
C_POOL, C_SSM, C_Q, C_K, C_V, C_MIX, C_GLU, C_MERGE, C_OUT, C_WQ, CHUNKS = 0, 2, 4, 7, 10, 13, 14, 16, 32, 36, 44

PH = 8
TOPK = 16
NKEYS = 128
EXPERTS = NKEYS * NKEYS
PICKS = PH * TOPK
NB = 8
ROUNDS = PICKS // NB

V_G1, V_G2, V_PSCALE, V_D, V_ARE, V_AIM, V_END = 0, 8, 16, 20, 24, 40, 56

TWO_PI_HI = 6.28125
TWO_PI_MID = 0.0019350051879882812
TWO_PI_LO = 2 * math.pi - TWO_PI_HI - TWO_PI_MID
ROUND = 1.5 * 2.0 ** 23
PI_SAFE = 3.1415925
LN2_HI = 0.693359375
LN2_LO = math.log(2.0) - LN2_HI


class Steps:

    def __init__(self, eng, sem):
        self.eng, self.sem, self.n = eng, sem, 0

    def step(self, ins):
        ins.then_inc(self.sem, 1)
        self.n += 1

    def settle(self):
        self.eng.wait_ge(self.sem, self.n)

    def link(self, ins):
        self.step(ins)
        self.settle()


def mixer_order():
    head = [("tile", "pool_u", m) for m in range(4)] + [("tile", "ssm_u", m) for m in range(4)]
    dense = []
    for which in ("q", "k"):
        for m in range(6):
            dense.append(("tile", which, m))
            if m:
                dense.append(("tile", which + "swap", m - 1))
        dense.append(("tile", which + "swap", 5))
    dense += [("tile", "v", c, b) for c in range(3) for b in range(NT)]
    dense += [("tile", "mix", g) for g in range(4)]
    out, pair = list(head), 0
    for n, item in enumerate(dense):
        out.append(item)
        if n >= 2 and pair < PAIRS and (n - 2) % 2 == 0:
            out.append(("pair", pair))
            pair += 1
    out += [("pair", p) for p in range(pair, PAIRS)]
    out.append(("pairs_end",))
    for i in range(2):
        for j in range(2):
            out += [("tile", "glu_gate", 2 * i + j), ("tile", "glu_val", 2 * i + j)]
    out.append(("attention",))
    for m in range(KD):
        for b in range(3):
            out += [("tile", "branch", m, b), ("tile", "gate", m, b)]
    out += [("tile", "out", m) for m in range(KD)]
    out.append(("norm2",))
    out += [("tile", "wq", m) for m in range(16)]
    out += [("tile", "h_tok", t, half) for t in range(NT) for half in range(2)]
    out += [("tile", "score", t, quarter) for t in range(NT) for quarter in range(4)]
    return out


ORDER = mixer_order()
TILES = [item for item in ORDER if item[0] == "tile"]
TILE_NUMBER = {item: n for n, item in enumerate(TILES)}
BRANCH_START = {(0, 0): 0, (0, 1): 4, (1, 0): 12, (1, 1): 16, (2, 0): 24, (2, 1): 26}
BRANCH_K = {0: 4, 1: 4, 2: 2}


def chunk_last_tile():
    last = {}
    for item in TILES:
        n, kind = TILE_NUMBER[item], item[1]
        first = {"pool_u": C_POOL, "ssm_u": C_SSM, "q": C_Q, "k": C_K, "out": C_OUT, "wq": C_WQ}.get(kind)
        if first is not None:
            last[first + item[2] // 2] = n
        elif kind == "v":
            last[C_V + item[2]] = n
        elif kind == "mix":
            last[C_MIX] = n
        elif kind in ("glu_gate", "glu_val"):
            last[C_GLU + item[2] // 2] = n
        elif kind in ("branch", "gate"):
            m, b = item[2], item[3]
            at = BRANCH_START[(b, kind == "gate")]
            end = at + (8 if kind == "gate" else BRANCH_K[b]) - 1
            for j in {at // 17, end // 17}:
                last[C_MERGE + 2 * m + j] = n
    return last


CHUNK_LAST_TILE = chunk_last_tile()


def trunk(nc, x_cm, positions, inv_freq, weights, keys, vecs, log_dt, ssm_bc, table_u, table_v, final_g, out_cm):
    with ExitStack() as ctx:
        def sb(name, shape, dt=F32):
            return ctx.enter_context(nc.sbuf_tensor(name, shape, dt))

        sems = []
        land = [ctx.enter_context(nc.semaphore(f"row_landed{j}")) for j in range(NB)]

        def sem(name):
            s = ctx.enter_context(nc.semaphore(name))
            sems.append(s)
            return s

        xT = sb("xT", [P, KD, L])
        hT = sb("hT", [P, KD, L])
        wring = sb("wring", [P, RING, CHUNK])
        cosT = sb("cosT", [P, L])
        sinT = sb("sinT", [P, L])
        mask = sb("mask", [P, NT, KEYS])
        ident = sb("ident", [P, P])
        mean_ones = sb("mean_ones", [P, P])
        swap = sb("swap", [P, P])
        vec = sb("vec", [P, V_END])
        keysT = sb("keysT", [P, 2 * NKEYS])
        eps = sb("eps", [P, 1])
        layer_base = sb("layer_base", [P, 1])
        iota16 = sb("iota16", [P, TOPK])

        ARENA = 31488
        arena = sb("arena", [P, ARENA])

        def carve(at, n):
            assert at + n <= ARENA, (at, n)
            return arena[:, at:at + n]

        qT = carve(0, 3072).rearrange("p (m t) -> p m t", t=L)
        kT = carve(3072, 3072).rearrange("p (m t) -> p m t", t=L)
        vtok = carve(6144, 3072).rearrange("p (b c) -> p b c", b=NT)
        merged = carve(0, 4096).rearrange("p (m t) -> p m t", t=L)
        pool_in = carve(9216, 2048).rearrange("p (g t) -> p g t", t=L)
        pool_sum = carve(11264, 2048).rearrange("p (g t) -> p g t", t=L)
        mixT = pool_sum
        gluT = pool_in
        ssmT = carve(13312, 2048).rearrange("p (m t) -> p m t", t=L)
        pool_scratch = carve(15360, 1024).rearrange("p (i t) -> p i t", t=L)
        attnT = carve(27392, 1024).rearrange("p (m t) -> p m t", t=L)
        bbarT = carve(16384, 1024).rearrange("p (s m n) -> p s m n", s=2, m=4)
        c_blocks = carve(17408, 1536).rearrange("p (s g c) -> p s g c", s=3, g=PAIRS)
        pow_b = carve(18944, 1024).rearrange("p (s g t) -> p s g t", s=2, g=PAIRS)
        pow_a = carve(19968, 512).rearrange("p (s g t) -> p s g t", s=2, g=PAIRS)
        small = carve(20480, 544).rearrange("p (i g) -> p i g", g=PAIRS)
        raw = carve(21248, 1024).rearrange("p (i t) -> p i t", t=L)
        rope_t = carve(22272, 1024).rearrange("p (i t) -> p i t", t=L)
        tabs = carve(23296, 2048).rearrange("p (i s t) -> p i s t", i=2, s=2)
        rotin = carve(25344, 2048).rearrange("p (s t) -> p s t", t=L)
        scanned = carve(27392, 2048).rearrange("p (i s t) -> p i s t", i=2, s=2)
        prods = [carve(29440 + i * L, L) for i in range(4)]
        pow_tmp = carve(25344, 1024).rearrange("p (s g t) -> p s g t", s=2, g=PAIRS)
        bc_in = carve(23296, 1024).rearrange("p (s g c) -> p s g c", s=4, g=PAIRS)
        b_blocks = carve(27392, 1024).rearrange("p (s g c) -> p s g c", s=2, g=PAIRS)
        bbar = carve(28416, 1024).rearrange("p (s g c) -> p s g c", s=2, g=PAIRS)
        bb_tmp = carve(24320, 1024).rearrange("p (s g c) -> p s g c", s=2, g=PAIRS)
        srow = carve(23296, 1536).rearrange("p (i k) -> p i k", i=2)
        pT = carve(24832, 1536).rearrange("p (i k) -> p i k", i=2)
        otok = carve(26368, 512).rearrange("p (i c) -> p i c", i=2)
        stats = carve(26880, 64)
        sig = carve(23296, 1024).rearrange("p (i t) -> p i t", t=L)
        gated = carve(24320, 1024).rearrange("p (i t) -> p i t", t=L)
        rms = carve(30000, L)
        rstd = carve(30512, L)
        scores = carve(0, 8192).rearrange("p (t j k) -> p t j k", t=NT, j=16)
        out_tok = carve(0, 4096).rearrange("p (t d) -> p t d", t=NT)
        qpT = carve(8192, 8192).rearrange("p (j t) -> p j t", t=L)
        rows = carve(8192, NB * D).rearrange("p (j d) -> p j d", d=D)
        h_tok = carve(16384, 4096).rearrange("p (t d) -> p t d", t=NT)
        diag = carve(20480, NB * P).rearrange("p (j c) -> p j c", c=P)
        junk = carve(21504, D)
        h_now = carve(22528, D)
        topv = carve(23552, 256).rearrange("p (j k) -> p j k", k=TOPK)
        topi = carve(23808, 256).bitcast(U32).rearrange("p (j k) -> p j k", k=TOPK)
        topif = carve(24064, 256).rearrange("p (j k) -> p j k", k=TOPK)
        candv = carve(24320, 128).rearrange("p (h k) -> p h k", k=TOPK)
        candp = carve(24448, 128).bitcast(U32).rearrange("p (h k) -> p h k", k=TOPK)
        halfp = carve(24576, 256).bitcast(U32).rearrange("p (s n) -> p s n", s=2)
        halff = carve(24832, 256).rearrange("p (s n) -> p s n", s=2)
        picked = carve(25088, 256).rearrange("p (s n) -> p s n", s=2)
        gate_e = carve(25344, 128).rearrange("p (h k) -> p h k", k=TOPK)
        gate_s = carve(25472, 16)
        expert = carve(25600, NT * PICKS).bitcast(U32).rearrange("p (t n) -> p t n", t=NT)
        gates = carve(26112, NT * PICKS).rearrange("p (t n) -> p t n", t=NT)
        expert_f = carve(26624, 128)
        act_all = carve(26752, PICKS)
        gelu_all = carve(26880, PICKS)
        w_all = carve(27008, PICKS)
        act_stage = carve(27136, NB)
        w_stage = carve(27144, NB)
        idx_stage = carve(27152, 2 * NB).bitcast(U32).rearrange("p (i n) -> p i n", i=2)
        zeros = carve(27168, P)
        fing = carve(27296, KD)
        cand = hT[:, 0:4, :].rearrange("p a t -> p (a t)")
        scratch = hT[:, 4:8, :].rearrange("p a t -> p (a t)")

        ps = ctx.enter_context(nc.psum_tensor("ps", [P, 8, L], F32))

        s_load = sem("s_load")
        s_const = sem("s_const")
        s_masks = sem("s_masks")
        s_modmask = sem("s_modmask")
        s_angle = sem("s_angle")
        s_dve = sem("s_dve")
        residue = carve(0, P)
        posi = carve(128, L).bitcast(I32)
        freq = carve(1700, 1)
        angle = carve(2048, L)
        turns = carve(2560, L)
        ang_c = carve(3072, L)
        wrap = carve(3584, L)

        def reduce_angle(dve, st, ang, k, cos_ang, tmp):
            st.link(dve.tensor_scalar(k, ang, 1 / (2 * math.pi), ROUND, ALU.mult, ALU.add))
            st.link(dve.tensor_scalar(k, k, -ROUND, None, ALU.add))
            for part in (TWO_PI_HI, TWO_PI_MID, TWO_PI_LO):
                st.link(dve.scalar_tensor_tensor(ang, k, -part, ang, ALU.mult, ALU.add))
            st.link(dve.tensor_scalar(cos_ang, ang, math.pi / 2, None, ALU.add))
            st.link(dve.tensor_scalar(tmp, cos_ang, math.pi, -2 * math.pi, ALU.is_gt, ALU.mult))
            st.link(dve.tensor_tensor(cos_ang, cos_ang, tmp, ALU.add))
            st.link(dve.tensor_scalar(cos_ang, cos_ang, PI_SAFE, -PI_SAFE, ALU.min, ALU.max))
            st.link(dve.tensor_scalar(ang, ang, PI_SAFE, -PI_SAFE, ALU.min, ALU.max))

        with nc.Block() as block:
            @block.sync
            def _(sp):
                sp.dma_start(xT[:].rearrange("p a t -> p (a t)"), x_cm).then_inc(s_load, 16)
                sp.dma_start(posi, positions.broadcast_to([P, L])).then_inc(s_load, 16)
                sp.dma_start(freq, inv_freq).then_inc(s_load, 16)

            @block.gpsimd
            def _(pool):
                st = Steps(pool, s_const)
                st.step(pool.memset(ident[:], 0.0))
                st.step(pool.memset(mean_ones[:], 1.0 / D))
                st.step(pool.memset(swap[:], 0.0))
                st.step(pool.memset(residue[0:4, :], 0.0))
                st.step(pool.memset(eps[:], EPS))
                st.step(pool.memset(layer_base[:], 0.0))
                st.step(pool.memset(mask[:], 0.0))
                st.settle()
                st.step(pool.iota(iota16[:], [[1, TOPK]], base=0, channel_multiplier=0,
                                  allow_small_or_imprecise_dtypes=True))
                st.step(pool.affine_select(out=ident[:], in_=ident[:], compare_op=ALU.not_equal, fill=1.0, base=0,
                                           pattern=[[-1, P]], channel_multiplier=1))
                st.step(pool.affine_select(out=residue[0:4, :].rearrange("p (m c) -> p m c", c=4),
                                           in_=residue[0:4, :].rearrange("p (m c) -> p m c", c=4),
                                           compare_op=ALU.not_equal, fill=1.0, base=0,
                                           pattern=[[0, P // 4], [-1, 4]], channel_multiplier=1))
                sw = swap[:].rearrange("p (h s j) -> p h s j", h=2, s=2)
                st.step(pool.affine_select(out=sw[:, :, 0, :], in_=sw[:, :, 0, :], compare_op=ALU.not_equal, fill=-1.0,
                                           base=-32, pattern=[[-64, 2], [-1, 32]], channel_multiplier=1))
                st.settle()
                st.step(pool.affine_select(out=sw[:, :, 1, :], in_=sw[:, :, 1, :], compare_op=ALU.not_equal, fill=1.0,
                                           base=0, pattern=[[-64, 2], [-1, 32]], channel_multiplier=1))
                for b in range(NT):
                    near = mask[:, b, 0:L].rearrange("p (b i) -> p b i", b=NT)
                    st.link(pool.affine_select(out=near, in_=near, compare_op=ALU.is_ge, fill=NEG, base=b,
                                               pattern=[[-1, NT], [-4, P]], channel_multiplier=4))
                    st.step(pool.affine_select(out=near, in_=near, compare_op=ALU.is_ge, fill=NEG, base=P - b,
                                               pattern=[[1, NT], [4, P]], channel_multiplier=-4))
                far = mask[:, :, L:KEYS].rearrange("p b (s i) -> p b s i", s=2)
                st.link(pool.affine_select(out=far, in_=far, compare_op=ALU.is_ge, fill=NEG, base=0,
                                           pattern=[[0, NT], [0, 2], [-1, P]], channel_multiplier=1))
                pool.sem_inc(s_masks, 1)

            @block.tensor
            def _(pe):
                pe.wait_ge(s_masks, 1)
                pe.matmul(ps[:, 0, 0:P], residue[0:4, :], residue[0:4, :], start=True, stop=True).then_inc(s_modmask, 1)

            @block.vector
            def _(dve):
                st = Steps(dve, s_dve)
                dve.wait_ge(s_load, 48)
                st.link(dve.tensor_copy(angle, posi))
                st.link(dve.tensor_scalar(angle, angle, freq, None, ALU.mult))
                reduce_angle(dve, st, angle, turns, ang_c, wrap)
                dve.sem_inc(s_angle, 1)
                dve.wait_ge(s_modmask, 1)
                st.link(dve.tensor_scalar(wrap[:, 0:P], ps[:, 0, 0:P], -1.0, -NEG, ALU.add, ALU.mult))
                for b in range(NT):
                    st.step(dve.tensor_tensor(mask[:, b, L + P:KEYS], mask[:, b, L + P:KEYS], wrap[:, 0:P], ALU.add))

            @block.scalar
            def _(act):
                act.wait_ge(s_angle, 1)
                act.activation(sinT[:], angle, ACT.Sin)
                act.activation(cosT[:], ang_c, ACT.Sin)

        layer_sems_from = len(sems)
        w_landed = [sem(f"w_landed{i}") for i in range(RING)]
        small_landed = sem("small_landed")
        tiles_done = sem("tiles_done")
        bank_free = [sem(f"bank_free{i}") for i in range(4)]
        squares = sem("squares")
        mean_done = sem("mean_done")
        root_done = sem("root_done")
        normed = sem("normed")
        act_steps = sem("act_steps")
        dve_steps = sem("dve_steps")
        pool_steps = sem("pool_steps")
        raw_ready = sem("raw_ready")
        roped = sem("roped")
        pool_in_ready = sem("pool_in_ready")
        pooled_ready = sem("pooled_ready")
        mixed = sem("mixed")
        ssm_in_ready = sem("ssm_in_ready")
        blocks_ready = sem("blocks_ready")
        poles_ready = sem("poles_ready")
        bbar_ready = sem("bbar_ready")
        bbarT_done = sem("bbarT_done")
        bbarT_ready = sem("bbarT_ready")
        tab_ready = sem("tab_ready")
        x_done = sem("x_done")
        x_free = sem("x_free")
        scan_done = sem("scan_done")
        prod_dve = sem("prod_dve")
        prod_pool = sem("prod_pool")
        y_done = sem("y_done")
        y_taken = sem("y_taken")
        y_gelu = sem("y_gelu")
        v_ready = sem("v_ready")
        glu_sig = sem("glu_sig")
        glu_ready = sem("glu_ready")
        sc_done = sem("sc_done")
        sc_max = sem("sc_max")
        exp_done = sem("exp_done")
        pt_done = sem("pt_done")
        pt_copied = sem("pt_copied")
        pv_done = sem("pv_done")
        o_done = sem("o_done")
        ot_done = sem("ot_done")
        ot_copied = sem("ot_copied")
        gate_sig = sem("gate_sig")
        gate_used = sem("gate_used")
        x_mixed = sem("x_mixed")
        wq_copied = sem("wq_copied")
        mix_evac = sem("mix_evac")
        out_stored = sem("out_stored")

        def norm_squares(act, base):
            for k in range(KD):
                act.activation(hT[:, k, :], xT[:, k, :], ACT.Square).then_inc(squares, 1)

        def norm_mean(pe, which):
            for k in range(KD):
                pe.wait_ge(squares, KD * which + k + 1)
                mm = pe.matmul(ps[:, 0, :], mean_ones[:], hT[:, k, :], start=(k == 0), stop=(k == KD - 1))
            mm.then_inc(mean_done, 1)

        def norm_root(act, which):
            act.wait_ge(mean_done, which + 1)
            act.activation(rms, ps[:, 0, :], ACT.Sqrt, bias=eps[:, 0:1]).then_inc(root_done, 1)

        def norm_scale(dve, which, gain, dst):
            dve.wait_ge(root_done, which + 1)
            dve.reciprocal(rstd, rms).then_inc(normed, 1)
            dve.wait_ge(normed, which * (KD + 1) + 1)
            for k in range(KD):
                dve.scalar_tensor_tensor(dst[:, k, :], xT[:, k, :], gain[:, k:k + 1], rstd, ALU.mult,
                                         ALU.mult).then_inc(normed, 1)

        def chunk_weight(c, at, n=P):
            return wring[:, c % RING, at:at + n]

        def mixer(layer):
            def attend_out(dve, st, i):
                b, h = i // SLOTS, i % SLOTS
                dve.wait_ge(pv_done, i + 1)
                st.link(dve.reciprocal(stats[:, 48 + i % 2:49 + i % 2], stats[:, 32 + i:33 + i]))
                dve.tensor_scalar(otok[:, b % 2, h * HEAD:(h + 1) * HEAD], ps[:, 2 + i % 2, 0:HEAD],
                                  stats[:, 48 + i % 2:49 + i % 2], None, ALU.mult).then_inc(o_done, 1)
                if h == 0 and b:
                    move_home(dve, b - 1)
                if i == 15:
                    move_home(dve, b)

            def move_home(dve, b):
                dve.wait_ge(ot_done, b + 1)
                dve.tensor_copy(attnT[:, :, :].rearrange("p m (i b) -> p m b i", b=NT)[:, :, b, :],
                                ps[:, 1, 0:256].rearrange("p (m i) -> p m i", m=2)).then_inc(ot_copied, 1)

            with nc.Block() as block:
                @block.sync
                def _(sp):
                    sp.dma_start(vec[:], vecs[bass.ts(layer, P), :]).then_inc(small_landed, 16)
                    for half in range(2):
                        sp.dma_start(small[64 * half:64 * half + 64, 0, :],
                                     log_dt[bass.ds(layer * 2 + half, 1), :].broadcast_to([64, PAIRS])).then_inc(small_landed, 16)
                    sp.dma_start(bc_in.rearrange("p s g c -> p (s g c)"), ssm_bc[bass.ts(layer, P), :]).then_inc(small_landed, 16)
                    sp.dma_start(keysT[:], keys[bass.ts(layer, P), :]).then_inc(small_landed, 16)
                    for c in range(CHUNKS):
                        if c >= RING:
                            sp.wait_ge(tiles_done, CHUNK_LAST_TILE[c - RING] + 1)
                        sp.dma_start(wring[:, c % RING, :],
                                     weights[bass.ts(layer * CHUNKS + c, P), :]).then_inc(w_landed[c % RING], 16)

                @block.gpsimd
                def _(pool):
                    st = Steps(pool, pool_steps)
                    st.step(pool.memset(b_blocks, 0.0))
                    st.step(pool.memset(c_blocks, 0.0))
                    pool.wait_ge(small_landed, 80)
                    st.settle()
                    for g in range(2):
                        rows_g, cols_g = slice(64 * g, 64 * g + 64), slice(16 * g, 16 * g + 16)
                        st.step(pool.tensor_copy(b_blocks[rows_g, :, :, cols_g], bc_in[rows_g, 0:2, :, :]))
                        st.step(pool.tensor_copy(c_blocks[rows_g, 0, :, cols_g], bc_in[rows_g, 2, :, :]))
                        st.step(pool.tensor_scalar(c_blocks[rows_g, 1, :, cols_g], bc_in[rows_g, 2, :, :], -1.0, None, ALU.mult))
                        st.step(pool.tensor_scalar(c_blocks[rows_g, 2, :, cols_g], bc_in[rows_g, 3, :, :], -1.0, None, ALU.mult))
                    st.settle()
                    pool.sem_inc(blocks_ready, 1)

                    pool.wait_ge(poles_ready, 1)
                    pool.wait_ge(bbar_ready, 1)
                    st.step(pool.memset(pow_b[:, 0, :, 0:1], 1.0))
                    st.step(pool.memset(pow_b[:, 1, :, 0:1], 0.0))
                    st.step(pool.memset(pow_a[:, 0, :, 0:1], 1.0))
                    st.step(pool.memset(pow_a[:, 1, :, 0:1], 0.0))
                    st.settle()
                    w_re, w_im, t0, t1 = small[:, 30, :], small[:, 31, :], small[:, 32, :], small[:, 33, :]
                    for table, count in ((pow_b, 5), (pow_a, 4)):
                        for e in range(count):
                            d = 1 << e
                            lo = lambda s: table[:, s, :, 0:d]
                            hi = lambda s: table[:, s, :, d:2 * d]
                            bc = lambda w: w.unsqueeze(2).broadcast_to([P, PAIRS, d])
                            ta, tb = pow_tmp[:, 0, :, 0:d], pow_tmp[:, 1, :, 0:d]
                            st.step(pool.tensor_tensor(hi(0), lo(0), bc(w_re), ALU.mult))
                            st.step(pool.tensor_tensor(hi(1), lo(1), bc(w_re), ALU.mult))
                            st.step(pool.tensor_tensor(ta, lo(1), bc(w_im), ALU.mult))
                            st.step(pool.tensor_tensor(tb, lo(0), bc(w_im), ALU.mult))
                            st.settle()
                            st.step(pool.tensor_tensor(hi(0), hi(0), ta, ALU.subtract))
                            st.step(pool.tensor_tensor(hi(1), hi(1), tb, ALU.add))
                            st.step(pool.tensor_tensor(t0, w_im, w_im, ALU.mult))
                            st.step(pool.tensor_tensor(t1, w_re, w_im, ALU.mult))
                            st.settle()
                            st.link(pool.tensor_tensor(w_re, w_re, w_re, ALU.mult))
                            st.step(pool.tensor_tensor(w_re, w_re, t0, ALU.subtract))
                            st.step(pool.tensor_tensor(w_im, t1, t1, ALU.add))
                            st.settle()

                    def table_of(p):
                        a = lambda s: pow_a[:, s, p, :].unsqueeze(2).broadcast_to([P, 16, 32])
                        b = lambda s: pow_b[:, s, p, :].unsqueeze(1).broadcast_to([P, 16, 32])
                        o = lambda s: tabs[:, p % 2, s, :].rearrange("p (a b) -> p a b", b=32)
                        ta = pool_scratch[:, 0, :].rearrange("p (a b) -> p a b", b=32)
                        tb = pool_scratch[:, 1, :].rearrange("p (a b) -> p a b", b=32)
                        st.step(pool.tensor_tensor(o(0), a(0), b(0), ALU.mult))
                        st.step(pool.tensor_tensor(ta, a(1), b(1), ALU.mult))
                        st.step(pool.tensor_tensor(o(1), a(1), b(0), ALU.mult))
                        st.step(pool.tensor_tensor(tb, a(0), b(1), ALU.mult))
                        st.settle()
                        st.step(pool.tensor_tensor(o(0), o(0), ta, ALU.subtract))
                        st.link(pool.tensor_tensor(o(1), o(1), tb, ALU.add))
                        pool.sem_inc(tab_ready, 1)

                    table_of(0)
                    table_of(1)

                    def windows():
                        pool.wait_ge(pool_in_ready, 4)
                        for g, win in enumerate(POOL_WINDOWS):
                            src = pool_in[:, g, :]
                            bufs = [pool_sum[:, g, :], pool_scratch[:, 0, :]]
                            cur, shift, n = src, 1, 0
                            while shift < win:
                                left = int(math.log2(win // shift)) - 1
                                dst = bufs[left % 2]
                                st.step(pool.tensor_copy(dst[:, 0:shift], cur[:, 0:shift]))
                                st.step(pool.tensor_tensor(dst[:, shift:L], cur[:, shift:L], cur[:, 0:L - shift], ALU.add))
                                st.settle()
                                cur, shift = dst, shift * 2
                            st.step(pool.tensor_scalar(cur[:, win - 1:L], cur[:, win - 1:L], 1.0 / win, None, ALU.mult))
                            for t in range(1, win - 1):
                                st.step(pool.tensor_scalar(cur[:, t:t + 1], cur[:, t:t + 1], 1.0 / (t + 1), None, ALU.mult))
                            st.settle()
                            st.link(pool.tensor_tensor(src, cur, src, ALU.subtract))
                            pool.sem_inc(pooled_ready, 1)

                    windows()
                    for p in range(PAIRS):
                        pool.wait_ge(scan_done, 2 * (p + 1))
                        if p:
                            pool.wait_ge(y_done, p)
                        st.step(pool.tensor_tensor(prods[2], scanned[:, p % 2, 1, :], tabs[:, p % 2, 0, :], ALU.mult))
                        st.link(pool.tensor_tensor(prods[3], scanned[:, p % 2, 0, :], tabs[:, p % 2, 1, :], ALU.mult))
                        pool.sem_inc(prod_pool, 1)
                        if p + 2 < PAIRS:
                            pool.wait_ge(prod_dve, 2 * (p + 1))
                            table_of(p + 2)

                @block.tensor
                def _(pe):
                    norm_mean(pe, 0)
                    pe.wait_ge(normed, KD + 1)

                    def need_chunk(c):
                        pe.wait_ge(w_landed[c % RING], 16 * (c // RING + 1))

                    def product(n, lhs, rhs, width=L, chunk_at=None):
                        for k in range(len(lhs)):
                            if chunk_at and k in chunk_at:
                                need_chunk(chunk_at[k])
                            mm = pe.matmul(ps[:, n % 4, 0:width], lhs[k], rhs[k], start=(k == 0), stop=(k == len(lhs) - 1))
                        return mm

                    def tile(item):
                        n, kind = TILE_NUMBER[item], item[1]
                        if n >= 4:
                            pe.wait_ge(bank_free[n % 4], n // 4)
                        first = {"pool_u": C_POOL, "ssm_u": C_SSM, "q": C_Q, "k": C_K, "out": C_OUT, "wq": C_WQ}.get(kind)
                        if first is not None:
                            m = item[2]
                            c = first + m // 2
                            src = merged if kind == "out" else hT
                            if kind == "out" and m == 0:
                                pe.wait_ge(gate_used, 3 * KD)
                            if kind == "wq" and m == 0:
                                pe.wait_ge(normed, 2 * (KD + 1))
                            mm = product(n, [chunk_weight(c, k * 256 + (m % 2) * P) for k in range(KD)],
                                         [src[:, k, :] for k in range(KD)], chunk_at={0: c})
                        elif kind in ("qswap", "kswap"):
                            pe.wait_ge(raw_ready, item[2] + 1 + (6 if kind == "kswap" else 0))
                            mm = product(n, [swap[:]], [raw[:, item[2] % 2, :]])
                        elif kind == "v":
                            c, b = C_V + item[2], item[3]
                            mm = product(n, [hT[:, k, :].rearrange("p (i b) -> p b i", b=NT)[:, b, :] for k in range(KD)],
                                         [chunk_weight(c, k * 256, 256) for k in range(KD)], width=256, chunk_at={0: c})
                        elif kind == "mix":
                            g = item[2]
                            pe.wait_ge(pooled_ready, g + 1)
                            mm = product(n, [chunk_weight(C_MIX, g * P)], [pool_in[:, g, :]], chunk_at={0: C_MIX})
                        elif kind in ("glu_gate", "glu_val"):
                            m = item[2]
                            c = C_GLU + m // 2
                            pe.wait_ge(y_gelu, 4)
                            at = (m % 2) * P + (256 if kind == "glu_gate" else 0)
                            mm = product(n, [chunk_weight(c, k * 512 + at) for k in range(4)],
                                         [ssmT[:, k, :] for k in range(4)], chunk_at={0: c})
                        elif kind in ("branch", "gate"):
                            m, b = item[2], item[3]
                            at = BRANCH_START[(b, kind == "gate")]
                            rows_n = 8 if kind == "gate" else BRANCH_K[b]
                            src = hT if kind == "gate" else (mixT, gluT, attnT)[b]
                            if kind == "branch" and m == 0:
                                pe.wait_ge((mixed, glu_ready, ot_copied)[b], 4)
                            where = [(C_MERGE + 2 * m + (at + k) // 17, (at + k) % 17) for k in range(rows_n)]
                            mm = product(n, [chunk_weight(c, j * P) for c, j in where],
                                         [src[:, k, :] for k in range(rows_n)],
                                         chunk_at={k: c for k, (c, j) in enumerate(where) if k == 0 or c != where[k - 1][0]})
                        elif kind == "h_tok":
                            t, half = item[2], item[3]
                            for k in range(4):
                                mm = pe.transpose(ps[:, n % 4, k * P:(k + 1) * P], hT[:, 4 * half + k, t * P:(t + 1) * P], ident[:])
                        elif kind == "score":
                            t, quarter = item[2], item[3]
                            if (t, quarter) == (0, 0):
                                pe.wait_ge(wq_copied, 16)
                            for k in range(4):
                                j = 4 * quarter + k
                                mm = pe.matmul(ps[:, n % 4, k * P:(k + 1) * P], qpT[:, j, t * P:(t + 1) * P],
                                               keysT[:, (j % 2) * NKEYS:(j % 2 + 1) * NKEYS], start=True, stop=True)
                        mm.then_inc(tiles_done, 1)

                    def pair_in(p):
                        m, a = p // PER_TILE, p % PER_TILE
                        part = slice(32 * a, 32 * a + 32)
                        if p == 0:
                            pe.wait_ge(bbar_ready, 1)
                            for s in range(2):
                                for mm_ in range(4):
                                    blk = bbar[:, s, 4 * mm_:4 * mm_ + 4, :].rearrange("p g c -> p (g c)")
                                    last = pe.transpose(ps[:, 4 + s, mm_ * P:(mm_ + 1) * P], blk, ident[:])
                            last.then_inc(bbarT_done, 1)
                            pe.wait_ge(ssm_in_ready, 4)
                            pe.wait_ge(bbarT_ready, 2)
                        else:
                            pe.wait_ge(x_free, p)
                        for s in range(2):
                            mm = pe.matmul(ps[:, 4 + s, :], bbarT[part, s, m, :], ssmT[part, m, :], start=True, stop=True)
                        mm.then_inc(x_done, 1)

                    def pair_out(p):
                        m, a = p // PER_TILE, p % PER_TILE
                        if p == 0:
                            pe.wait_ge(blocks_ready, 1)
                        if a == 0 and m >= 2:
                            pe.wait_ge(y_taken, m - 1)
                        pe.wait_ge(prod_dve, 2 * (p + 1))
                        pe.wait_ge(prod_pool, p + 1)
                        for i, c in enumerate((0, 1, 2, 2)):
                            mm = pe.matmul(ps[32 * a:32 * a + 32, 6 + m % 2, :], c_blocks[:, c, p, :], prods[i],
                                           start=(i == 0), stop=(i == 3))
                        mm.then_inc(y_done, 1)

                    def attention():
                        for b in range(4):
                            done = len([i for i in range(TILE_NUMBER[("tile", "branch", 0, 0)]) if i % 4 == b])
                            pe.wait_ge(bank_free[b], done)
                        pe.wait_ge(y_taken, 4)
                        pe.wait_ge(roped, 12)
                        pe.wait_ge(v_ready, 12)
                        its = [(b, h) for b in range(NT) for h in range(SLOTS)]

                        def rows_of(t, h, g):
                            m = 2 * g + h // 2
                            return t[HEAD * (h % 2):HEAD * (h % 2) + HEAD, m, :].rearrange("p (i b) -> p b i", b=NT)

                        def score(i):
                            b, h = its[i]
                            bank = 4 + 2 * (i % 2)
                            if i >= 2:
                                pe.wait_ge(sc_max, i - 1)
                            pe.matmul(ps[:, bank, :], rows_of(qT, h, 0)[:, b, :], rows_of(kT, h, 0), start=True, stop=True)
                            for g in (1, 2):
                                mm = pe.matmul(ps[:, bank + 1, (g - 1) * P:g * P], rows_of(qT, h, g)[:, b, :],
                                               rows_of(kT, h, g)[:, b, :], start=True, stop=True)
                            mm.then_inc(sc_done, 1)

                        def turn(i):
                            pe.wait_ge(exp_done, i + 1)
                            if i:
                                pe.wait_ge(pt_copied, i)
                            if i > 1 and (i - 1) % SLOTS == 0:
                                pe.wait_ge(ot_copied, (i - 1) // SLOTS)
                            for j in range(6):
                                mm = pe.transpose(ps[:, j // 4, (j % 4) * P:(j % 4 + 1) * P],
                                                  srow[:, i % 2, j * P:(j + 1) * P], ident[:])
                            mm.then_inc(pt_done, 1)

                        def weigh(i):
                            b, h = its[i]
                            pe.wait_ge(pt_copied, i + 1)
                            if i >= 2:
                                pe.wait_ge(o_done, i - 1)
                            for j in range(6):
                                g, kb = (0, j) if j < 4 else (j - 3, b)
                                mm = pe.matmul(ps[:, 2 + i % 2, 0:HEAD], pT[:, i % 2, j * P:(j + 1) * P],
                                               vtok[:, kb, (4 * g + h) * HEAD:(4 * g + h + 1) * HEAD],
                                               start=(j == 0), stop=(j == 5))
                            mm.then_inc(pv_done, 1)
                            if h == SLOTS - 1:
                                return b
                            return None

                        def turn_out(b):
                            pe.wait_ge(o_done, 4 * (b + 1))
                            for j in range(2):
                                mm = pe.transpose(ps[:, 1, j * P:(j + 1) * P], otok[:, b % 2, j * P:(j + 1) * P], ident[:])
                            mm.then_inc(ot_done, 1)

                        score(0)
                        pending = None
                        for i in range(len(its)):
                            if i + 1 < len(its):
                                score(i + 1)
                            turn(i)
                            last_b = weigh(i)
                            if pending is not None:
                                turn_out(pending)
                            pending = last_b
                        turn_out(pending)
                        pe.wait_ge(ot_copied, 4)

                    for item in ORDER:
                        if item[0] == "tile":
                            tile(item)
                        elif item[0] == "pair":
                            pair_in(item[1])
                            if item[1]:
                                pair_out(item[1] - 1)
                        elif item[0] == "pairs_end":
                            pair_out(PAIRS - 1)
                        elif item[0] == "attention":
                            attention()
                        elif item[0] == "norm2":
                            for b in range(4):
                                done = len([i for i in range(TILE_NUMBER[("tile", "wq", 0)]) if i % 4 == b])
                                pe.wait_ge(bank_free[b], done)
                            norm_mean(pe, 1)
                            pe.wait_ge(root_done, 2)

                @block.scalar
                def _(act):
                    norm_squares(act, 0)
                    norm_root(act, 0)
                    st = Steps(act, act_steps)
                    act.wait_ge(poles_angle, 1)
                    act.activation(small[:, 12, :], small[:, 4, :], ACT.Sin).then_inc(poles_sincos, 1)
                    act.activation(small[:, 13, :], small[:, 6, :], ACT.Sin).then_inc(poles_sincos, 1)
                    glu_n = gate_n = raw_n = 0
                    for item in ORDER:
                        kind = item[1] if item[0] == "tile" else item[0]
                        if item[0] == "tile":
                            n = TILE_NUMBER[item]
                            src = ps[:, n % 4, :]
                            free = bank_free[n % 4]
                        if kind in ("pool_u", "ssm_u"):
                            act.wait_ge(tiles_done, n + 1)
                            dst, ready = (pool_in, pool_in_ready) if kind == "pool_u" else (ssmT, ssm_in_ready)
                            st.step(act.copy(dst[:, item[2], :], src))
                            st.settle()
                            act.sem_inc(ready, 1)
                            act.sem_inc(free, 1)
                        elif kind in ("q", "k"):
                            act.wait_ge(tiles_done, n + 1)
                            if raw_n >= 2:
                                act.wait_ge(roped, raw_n - 1)
                            st.link(act.copy(raw[:, item[2] % 2, :], src))
                            act.sem_inc(raw_ready, 1)
                            act.sem_inc(free, 1)
                            raw_n += 1
                        elif kind == "v":
                            act.wait_ge(tiles_done, n + 1)
                            st.link(act.copy(vtok[:, item[3], 256 * item[2]:256 * item[2] + 256], src[:, 0:256]))
                            act.sem_inc(v_ready, 1)
                            act.sem_inc(free, 1)
                        elif kind == "pair" and item[1] == 0:
                            act.wait_ge(bbarT_done, 1)
                            for s in range(2):
                                act.copy(bbarT[:, s, :, :], ps[:, 4 + s, :].rearrange("p (m n) -> p m n", m=4)).then_inc(bbarT_ready, 1)
                        elif kind == "mix":
                            act.wait_ge(tiles_done, n + 1)
                            g = item[2]
                            st.link(act.activation(mixT[:, g, :], src, ACT.Copy, scale=vec[:, V_PSCALE + g:V_PSCALE + g + 1]))
                            act.sem_inc(mixed, 1)
                            act.sem_inc(free, 1)
                        elif kind == "pairs_end":
                            for m in range(4):
                                act.wait_ge(y_taken, m + 1)
                                act.activation(ssmT[:, m, :], ssmT[:, m, :], ACT.Gelu_apprx_tanh).then_inc(y_gelu, 1)
                        elif kind == "glu_gate":
                            act.wait_ge(tiles_done, n + 1)
                            if glu_n >= 2:
                                act.wait_ge(glu_ready, glu_n - 1)
                            st.link(act.activation(rope_t[:, glu_n % 2, :], src, ACT.Sigmoid))
                            act.sem_inc(glu_sig, 1)
                            act.sem_inc(free, 1)
                            glu_n += 1
                        elif kind == "gate":
                            act.wait_ge(tiles_done, n + 1)
                            if gate_n >= 2:
                                act.wait_ge(gate_used, gate_n - 1)
                            st.link(act.activation(sig[:, gate_n % 2, :], src, ACT.Sigmoid))
                            act.sem_inc(gate_sig, 1)
                            act.sem_inc(free, 1)
                            gate_n += 1
                        elif kind == "attention":
                            for i in range(16):
                                act.wait_ge(sc_max, i + 1)
                                act.activation(srow[:, i % 2, :], srow[:, i % 2, :], ACT.Exp, bias=stats[:, 16 + i:17 + i],
                                               scale=SCALE, accum_out=stats[:, 32 + i:33 + i]).then_inc(exp_done, 1)
                                act.wait_ge(pt_done, i + 1)
                                if i >= 2:
                                    act.wait_ge(pv_done, i - 1)
                                act.copy(pT[:, i % 2, :], ps[:, 0:2, :].rearrange("p a t -> p (a t)")[:, 0:KEYS]).then_inc(pt_copied, 1)
                        elif kind == "norm2":
                            act.wait_ge(x_mixed, KD)
                            norm_squares(act, 1)
                            norm_root(act, 1)
                        elif kind == "wq":
                            act.wait_ge(tiles_done, n + 1)
                            st.link(act.copy(qpT[:, item[2], :], src))
                            act.sem_inc(wq_copied, 1)
                            act.sem_inc(free, 1)
                        elif kind == "h_tok":
                            act.wait_ge(tiles_done, n + 1)
                            st.step(act.copy(h_tok[:, item[2], 512 * item[3]:512 * item[3] + 512], src))
                            st.settle()
                            act.sem_inc(free, 1)
                        elif kind == "score":
                            act.wait_ge(tiles_done, n + 1)
                            st.link(act.copy(scores[:, item[2], 4 * item[3]:4 * item[3] + 4, :],
                                             src.rearrange("p (j k) -> p j k", j=4)))
                            act.sem_inc(free, 1)

                @block.vector
                def _(dve):
                    st = Steps(dve, dve_steps)

                    def own_exp(x, out, k, r, q):
                        st.link(dve.tensor_scalar(k, x, 1 / math.log(2.0), ROUND, ALU.mult, ALU.add))
                        st.link(dve.tensor_scalar(k, k, -ROUND, -126.0, ALU.add, ALU.max))
                        st.link(dve.scalar_tensor_tensor(r, k, -LN2_HI, x, ALU.mult, ALU.add))
                        st.link(dve.scalar_tensor_tensor(r, k, -LN2_LO, r, ALU.mult, ALU.add))
                        st.link(dve.tensor_scalar(q, r, 1 / 5040.0, None, ALU.mult))
                        for c in (1 / 720.0, 1 / 120.0, 1 / 24.0, 1 / 6.0, 0.5, 1.0):
                            st.link(dve.scalar_tensor_tensor(q, q, c, r, ALU.add, ALU.mult))
                        st.link(dve.tensor_scalar(k.bitcast(I32), k, 127.0, 2.0 ** 23, ALU.add, ALU.mult))
                        st.link(dve.scalar_tensor_tensor(out, q, 1.0, k, ALU.add, ALU.mult))

                    def tt(out, a, b, op):
                        st.link(dve.tensor_tensor(out, a, b, op))

                    S = lambda i: small[:, i, :]
                    log_dt_, dt, x, decay, theta, kk, theta_c, tmp = (S(i) for i in range(8))
                    r_, q_ = S(8), S(9)
                    sin_, cos_ = S(12), S(13)
                    a_re, a_im = vec[:, V_ARE:V_ARE + PAIRS], vec[:, V_AIM:V_AIM + PAIRS]
                    ab_re, ab_im, den, k_re, k_im, nr = S(14), S(15), S(16), S(17), S(18), S(19)
                    dve.wait_ge(small_landed, 80)
                    own_exp(log_dt_, dt, kk, r_, q_)
                    tt(x, a_re, dt, ALU.mult)
                    own_exp(x, decay, kk, r_, q_)
                    tt(theta, a_im, dt, ALU.mult)
                    reduce_angle(dve, st, theta, kk, theta_c, tmp)
                    dve.sem_inc(poles_angle, 1)
                    norm_scale(dve, 0, vec[:, V_G1:V_G1 + KD], hT)
                    dve.wait_ge(poles_sincos, 2)
                    tt(ab_re, decay, cos_, ALU.mult)
                    tt(ab_im, decay, sin_, ALU.mult)
                    tt(den, a_re, a_re, ALU.mult)
                    tt(tmp, a_im, a_im, ALU.mult)
                    tt(den, den, tmp, ALU.add)
                    st.link(dve.reciprocal(den, den))
                    st.link(dve.tensor_scalar(nr, ab_re, -1.0, None, ALU.add))
                    tt(k_re, nr, a_re, ALU.mult)
                    tt(tmp, ab_im, a_im, ALU.mult)
                    tt(k_re, k_re, tmp, ALU.add)
                    tt(k_re, k_re, den, ALU.mult)
                    tt(k_im, ab_im, a_re, ALU.mult)
                    tt(tmp, nr, a_im, ALU.mult)
                    tt(k_im, k_im, tmp, ALU.subtract)
                    tt(k_im, k_im, den, ALU.mult)
                    st.step(dve.tensor_copy(S(30), cos_))
                    st.link(dve.tensor_copy(S(31), sin_))
                    dve.sem_inc(poles_ready, 1)
                    dve.wait_ge(blocks_ready, 1)
                    wide = lambda v: v.unsqueeze(2).broadcast_to([P, PAIRS, 32])
                    tt(bbar[:, 0, :, :], b_blocks[:, 0, :, :], wide(k_re), ALU.mult)
                    tt(bb_tmp[:, 0, :, :], b_blocks[:, 1, :, :], wide(k_im), ALU.mult)
                    tt(bbar[:, 0, :, :], bbar[:, 0, :, :], bb_tmp[:, 0, :, :], ALU.subtract)
                    tt(bbar[:, 1, :, :], b_blocks[:, 1, :, :], wide(k_re), ALU.mult)
                    tt(bb_tmp[:, 0, :, :], b_blocks[:, 0, :, :], wide(k_im), ALU.mult)
                    tt(bbar[:, 1, :, :], bbar[:, 1, :, :], bb_tmp[:, 0, :, :], ALU.add)
                    dve.sem_inc(bbar_ready, 1)

                    def pair(p):
                        cs, sn = tabs[:, p % 2, 0, :], tabs[:, p % 2, 1, :]
                        xr, xi = ps[:, 4, :], ps[:, 5, :]
                        m1, m2, m3, m4 = (rotin[:, i, :] for i in range(4))
                        dve.wait_ge(tab_ready, p + 1)
                        dve.wait_ge(x_done, p + 1)
                        dve.tensor_tensor(m1, xr, cs, ALU.mult)
                        dve.tensor_tensor(m2, xi, sn, ALU.mult)
                        dve.tensor_tensor(m3, xi, cs, ALU.mult)
                        dve.tensor_tensor(m4, xr, sn, ALU.mult).then_inc(x_free, 1)
                        dve.wait_ge(x_free, p + 1)
                        st.step(dve.tensor_tensor(m1, m1, m2, ALU.add))
                        st.step(dve.tensor_tensor(m3, m3, m4, ALU.subtract))
                        if p >= 2:
                            dve.wait_ge(prod_pool, p - 1)
                        st.settle()
                        rate = decay[:, p:p + 1].broadcast_to([P, L])
                        for s, v in enumerate((m1, m3)):
                            dve.tensor_tensor_scan(scanned[:, p % 2, s, :], rate, v, 0.0, ALU.mult, ALU.add).then_inc(scan_done, 1)
                        dve.wait_ge(scan_done, 2 * (p + 1))
                        if p:
                            dve.wait_ge(y_done, p)
                        dve.tensor_tensor(prods[0], scanned[:, p % 2, 0, :], cs, ALU.mult).then_inc(prod_dve, 1)
                        dve.tensor_tensor(prods[1], scanned[:, p % 2, 1, :], sn, ALU.mult).then_inc(prod_dve, 1)

                    def take_y(m):
                        dve.wait_ge(y_done, PER_TILE * (m + 1))
                        dve.scalar_tensor_tensor(ssmT[:, m, :], ssmT[:, m, :], vec[:, V_D + m:V_D + m + 1], ps[:, 6 + m % 2, :],
                                                 ALU.mult, ALU.add).then_inc(y_taken, 1)

                    rope_n = glu_n = gate_n = 0
                    for item in ORDER:
                        kind = item[1] if item[0] == "tile" else item[0]
                        if item[0] == "tile":
                            n = TILE_NUMBER[item]
                            src = ps[:, n % 4, :]
                            free = bank_free[n % 4]
                        if kind in ("qswap", "kswap"):
                            dst = (qT if kind == "qswap" else kT)[:, item[2], :]
                            dve.wait_ge(raw_ready, rope_n + 1)
                            st.step(dve.tensor_tensor(rope_t[:, 0, :], raw[:, item[2] % 2, :], cosT[:], ALU.mult))
                            dve.wait_ge(tiles_done, n + 1)
                            st.link(dve.tensor_tensor(rope_t[:, 1, :], src, sinT[:], ALU.mult))
                            dve.sem_inc(free, 1)
                            dve.tensor_tensor(dst, rope_t[:, 0, :], rope_t[:, 1, :], ALU.add).then_inc(roped, 1)
                            rope_n += 1
                            dve.wait_ge(roped, rope_n)
                        elif kind == "pair":
                            pair(item[1])
                            if item[1] and item[1] % PER_TILE == 0:
                                take_y(item[1] // PER_TILE - 1)
                        elif kind == "pairs_end":
                            take_y(3)
                        elif kind == "glu_val":
                            dve.wait_ge(tiles_done, n + 1)
                            dve.wait_ge(glu_sig, glu_n + 1)
                            dve.tensor_tensor(gluT[:, item[2], :], src, rope_t[:, glu_n % 2, :], ALU.mult).then_inc(glu_ready, 1)
                            glu_n += 1
                            dve.wait_ge(glu_ready, glu_n)
                            dve.sem_inc(free, 1)
                        elif kind == "attention":
                            for i in range(16):
                                b, h = i // SLOTS, i % SLOTS
                                bank = 4 + 2 * (i % 2)
                                dve.wait_ge(sc_done, i + 1)
                                if i >= 2:
                                    dve.wait_ge(pt_done, i - 1)
                                st.link(dve.tensor_tensor_reduce(
                                    srow[:, i % 2, :], ps[:, bank:bank + 2, :].rearrange("p a t -> p (a t)")[:, 0:KEYS],
                                    mask[:, b, :], 1.0, LOWEST, ALU.add, ALU.max, stats[:, i:i + 1]))
                                dve.tensor_scalar(stats[:, 16 + i:17 + i], stats[:, i:i + 1], -SCALE, None, ALU.mult).then_inc(sc_max, 1)
                                if i:
                                    attend_out(dve, st, i - 1)
                            attend_out(dve, st, 15)
                        elif kind == "gate":
                            m, b = item[2], item[3]
                            ny = TILE_NUMBER[("tile", "branch", m, b)]
                            y = ps[:, ny % 4, :]
                            dve.wait_ge(tiles_done, ny + 1)
                            dve.wait_ge(gate_sig, gate_n + 1)
                            if b == 0:
                                dve.tensor_tensor(merged[:, m, :], y, sig[:, gate_n % 2, :], ALU.mult).then_inc(gate_used, 1)
                            else:
                                st.link(dve.tensor_tensor(gated[:, 0, :], y, sig[:, gate_n % 2, :], ALU.mult))
                                dve.wait_ge(gate_used, gate_n)
                                dve.tensor_tensor(merged[:, m, :], merged[:, m, :], gated[:, 0, :], ALU.add).then_inc(gate_used, 1)
                            gate_n += 1
                            dve.wait_ge(gate_used, gate_n)
                            dve.sem_inc(bank_free[ny % 4], 1)
                        elif kind == "out":
                            dve.wait_ge(tiles_done, n + 1)
                            dve.tensor_tensor(xT[:, item[2], :], xT[:, item[2], :], src, ALU.add).then_inc(x_mixed, 1)
                            dve.wait_ge(x_mixed, item[2] + 1)
                            dve.sem_inc(free, 1)
                        elif kind == "norm2":
                            norm_scale(dve, 1, vec[:, V_G2:V_G2 + KD], hT)

        poles_angle = sem("poles_angle")
        poles_sincos = sem("poles_sincos")
        freed = [sem(f"row_free{j}") for j in range(NB)]
        picks_ready = sem("picks_ready")
        exp_ready = sem("exp_ready")
        shifted = sem("shifted")
        peer_dve = sem("peer_dve")
        idx_staged = sem("idx_staged")
        act_copied = sem("act_copied")
        acts_ready = sem("acts_ready")
        gelu_ready = sem("gelu_ready")
        w_ready = sem("w_ready")
        w_staged = sem("w_staged")
        diag_ready = sem("diag_ready")
        acc_open = sem("acc_open")
        acc_done = sem("acc_done")
        acc_free = sem("acc_free")
        back_done = sem("back_done")
        back_taken = sem("back_taken")
        h_copied = sem("h_copied")
        zeroed = sem("zeroed")
        pool_turn = sem("pool_turn")
        dve_turn = sem("dve_turn")

        def peer(layer):
            with nc.Block() as block:
                @block.gpsimd
                def _(pool):
                    for j in range(NB):
                        pool.sem_inc(freed[j], 1)
                    pool.wait_ge(picks_ready, NT)
                    with pool.Fori(0, NT) as t:
                        for half, table in enumerate((table_u, table_v)):
                            with pool.Fori(0, ROUNDS // 2) as i2:
                                for par in range(2):
                                    rnd = t * (2 * ROUNDS) + half * ROUNDS + i2 * 2 + par
                                    stage = idx_stage[:, par, :]
                                    for j in range(NB):
                                        pool.wait_ge(freed[j], rnd + 1)
                                        if j == 0:
                                            pool.tensor_copy(stage, expert.rearrange("p t n -> p (t n)")[
                                                :, bass.ds(t * PICKS + (i2 * 2 + par) * NB, NB)]).then_inc(idx_staged, 1)
                                            pool.wait_ge(idx_staged, rnd + 1)
                                        pool.sem_inc(pool_turn, 1)
                                        pool.indirect_dma_start(rows[:, j, :], None, table,
                                                                bass.IndirectOffsetOnAxis(stage[:, j:j + 1], 0)).then_inc(land[j], 16)

                @block.vector
                def _(dve):
                    st = Steps(dve, peer_dve)
                    dve.memset(zeros, 0.0).then_inc(zeroed, 1)
                    eq = scratch.rearrange("p (n k) -> p n k", k=TOPK)
                    eq4 = scratch.rearrange("p (h n k) -> p h n k", h=PH, k=TOPK)
                    for t in range(NT):
                        left = scratch.rearrange("p (j k) -> p j k", j=16)
                        for j in range(16):
                            st.step(dve.max(topv[:, j, 0:8], scores[:, t, j, :]))
                        st.settle()
                        for j in range(16):
                            st.step(dve.max_index(topi[:, j, 0:8], topv[:, j, 0:8], scores[:, t, j, :]))
                            st.step(dve.match_replace(left[:, j, :], topv[:, j, 0:8], scores[:, t, j, :], LOWEST))
                        st.settle()
                        for j in range(16):
                            st.step(dve.max(topv[:, j, 8:16], left[:, j, :]))
                        st.settle()
                        for j in range(16):
                            st.step(dve.max_index(topi[:, j, 8:16], topv[:, j, 8:16], left[:, j, :]))
                        two = topv.rearrange("p (h s) k -> p h s k", s=2)
                        st.step(dve.tensor_tensor(cand.rearrange("p (h a b) -> p h a b", h=PH, a=TOPK),
                                                  two[:, :, 0, :].unsqueeze(3).broadcast_to([P, PH, TOPK, TOPK]),
                                                  two[:, :, 1, :].unsqueeze(2).broadcast_to([P, PH, TOPK, TOPK]), ALU.add))
                        st.settle()
                        st.step(dve.tensor_copy(topif, topi))
                        cd = cand.rearrange("p (h n) -> p h n", h=PH)
                        cl = scratch.rearrange("p (h n) -> p h n", h=PH)
                        for h in range(PH):
                            st.step(dve.max(candv[:, h, 0:8], cd[:, h, :]))
                        st.settle()
                        for h in range(PH):
                            st.step(dve.max_index(candp[:, h, 0:8], candv[:, h, 0:8], cd[:, h, :]))
                            st.step(dve.match_replace(cl[:, h, :], candv[:, h, 0:8], cd[:, h, :], LOWEST))
                        st.settle()
                        for h in range(PH):
                            st.step(dve.max(candv[:, h, 8:16], cl[:, h, :]))
                        st.settle()
                        for h in range(PH):
                            st.step(dve.max_index(candp[:, h, 8:16], candv[:, h, 8:16], cl[:, h, :]))
                        if t:
                            dve.wait_ge(exp_ready, t)
                        dve.tensor_tensor(gate_e, candv, candv[:, :, 0:1].broadcast_to([P, PH, TOPK]),
                                          ALU.subtract).then_inc(shifted, 1)
                        st.settle()
                        flatp = candp.rearrange("p h k -> p (h k)")
                        st.step(dve.tensor_scalar(halfp[:, 0, :], flatp, 4, None, ALU.logical_shift_right))
                        st.step(dve.tensor_scalar(halfp[:, 1, :], flatp, 15, None, ALU.bitwise_and))
                        st.settle()
                        st.link(dve.tensor_copy(halff, halfp))
                        lists = topif.rearrange("p (h s) k -> p h s k", s=2)
                        for s in range(2):
                            st.link(dve.tensor_tensor(eq, halff[:, s, :].unsqueeze(2).broadcast_to([P, PICKS, TOPK]),
                                                      iota16[:].unsqueeze(1).broadcast_to([P, PICKS, TOPK]), ALU.is_equal))
                            st.link(dve.tensor_tensor(eq4, eq4, lists[:, :, s, :].unsqueeze(2).broadcast_to([P, PH, TOPK, TOPK]), ALU.mult))
                            st.link(dve.tensor_reduce(picked[:, s, :], eq, AX.X, ALU.add))
                        st.link(dve.scalar_tensor_tensor(expert_f, picked[:, 0, :], float(NKEYS), picked[:, 1, :], ALU.mult, ALU.add))
                        st.step(dve.tensor_scalar(expert[:, t, :], expert_f, layer_base[:, 0:1], None, ALU.add))
                        dve.wait_ge(exp_ready, t + 1)
                        st.link(dve.tensor_reduce(gate_s[:, 0:PH], gate_e, AX.X, ALU.add))
                        st.link(dve.reciprocal(gate_s[:, 8:8 + PH], gate_s[:, 0:PH]))
                        st.link(dve.tensor_tensor(gates[:, t, :].rearrange("p (h k) -> p h k", k=TOPK), gate_e,
                                                  gate_s[:, 8:8 + PH].unsqueeze(2).broadcast_to([P, PH, TOPK]), ALU.mult))
                        dve.sem_inc(picks_ready, 1)
                    st.link(dve.tensor_scalar(layer_base[:], layer_base[:], float(EXPERTS), None, ALU.add))
                    with dve.Fori(0, NT) as t:
                        dve.tensor_copy(h_now, h_tok.rearrange("p t d -> p (t d)")[:, bass.ds(t * D, D)]).then_inc(h_copied, 1)
                        dve.wait_ge(h_copied, t + 1)
                        dve.sem_inc(dve_turn, 1)
                        with dve.Fori(0, ROUNDS) as i:
                            rnd = t * (2 * ROUNDS) + i
                            for j in range(NB):
                                dve.wait_ge(land[j], (layer * (NT * 2 * ROUNDS) + rnd) * 16 + 16)
                                dve.tensor_tensor_reduce(rows[:, j, :], rows[:, j, :], h_now, 1.0, 0.0, ALU.mult, ALU.add,
                                                         act_stage[:, j:j + 1]).then_inc(freed[j], 1)
                            dve.wait_ge(freed[NB - 1], rnd + 2)
                            dve.tensor_copy(act_all[:, bass.ts(i, NB)], act_stage).then_inc(act_copied, 1)
                            dve.wait_ge(act_copied, t * ROUNDS + i + 1)
                        dve.sem_inc(acts_ready, 1)
                        dve.wait_ge(gelu_ready, t + 1)
                        dve.tensor_tensor(w_all, gelu_all, gates.rearrange("p t n -> p (t n)")[:, bass.ts(t, PICKS)],
                                          ALU.mult).then_inc(w_ready, 1)
                        dve.wait_ge(w_ready, t + 1)
                        dve.sem_inc(dve_turn, 1)
                        with dve.Fori(0, ROUNDS) as i:
                            rnd = t * (2 * ROUNDS) + ROUNDS + i
                            dve.tensor_copy(w_stage, w_all[:, bass.ts(i, NB)]).then_inc(w_staged, 1)
                            dve.wait_ge(w_staged, t * ROUNDS + i + 1)
                            for j in range(NB):
                                dve.wait_ge(freed[j], rnd + 1)
                                dve.tensor_scalar(diag[:, j, :], ident[:], w_stage[:, j:j + 1], None,
                                                  ALU.mult).then_inc(diag_ready, 1)
                            dve.wait_ge(diag_ready, t * PICKS + i * NB + NB)
                    for t in range(NT):
                        for half in range(2):
                            n = 2 * t + half
                            dve.wait_ge(back_done, n + 1)
                            dst = xT[:, 4 * half:4 * half + 4, t * P:(t + 1) * P]
                            dve.tensor_tensor(dst, dst, ps[:, n % 4, :].rearrange("p (k c) -> p k c", k=4),
                                              ALU.add).then_inc(back_taken, 1)

                @block.scalar
                def _(act):
                    for t in range(NT):
                        act.wait_ge(shifted, t + 1)
                        act.activation(gate_e, gate_e, ACT.Exp).then_inc(exp_ready, 1)
                    act.sem_inc(acc_free, 1)
                    with act.Fori(0, NT) as t:
                        act.wait_ge(acts_ready, t + 1)
                        act.activation(gelu_all, act_all, ACT.Gelu_apprx_tanh).then_inc(gelu_ready, 1)
                        act.wait_ge(acc_done, t + 1)
                        act.copy(out_tok.rearrange("p t d -> p (t d)")[:, bass.ds(t * D, D)],
                                 ps[:, 4:6, :].rearrange("p a t -> p (a t)")).then_inc(acc_free, 1)

                @block.tensor
                def _(pe):
                    pe.wait_ge(zeroed, 1)
                    with pe.Fori(0, NT) as t:
                        pe.wait_ge(acc_free, t + 1)
                        for half in range(2):
                            pe.matmul(ps[:, 4 + half, :], zeros, cosT[:], start=True, stop=False)
                        with pe.Fori(0, ROUNDS) as i:
                            rnd = t * (2 * ROUNDS) + ROUNDS + i
                            for j in range(NB):
                                pe.wait_ge(diag_ready, t * PICKS + i * NB + (j + 1))
                                pe.wait_ge(land[j], (layer * (NT * 2 * ROUNDS) + rnd) * 16 + 16)
                                for half in range(2):
                                    mm = pe.matmul(ps[:, 4 + half, :], diag[:, j, :], rows[:, j, half * L:(half + 1) * L],
                                                   start=False, stop=False)
                                mm.then_inc(freed[j], 1)
                        for half in range(2):
                            mm = pe.matmul(ps[:, 4 + half, :], zeros, cosT[:], start=False, stop=True)
                        mm.then_inc(acc_done, 1)
                    pe.wait_ge(acc_free, NT + 1)
                    for t in range(NT):
                        for half in range(2):
                            n = 2 * t + half
                            if n >= 4:
                                pe.wait_ge(back_taken, n - 3)
                            for k in range(4):
                                c = 4 * half + k
                                mm = pe.transpose(ps[:, n % 4, k * P:(k + 1) * P], out_tok[:, t, c * P:(c + 1) * P], ident[:])
                            mm.then_inc(back_done, 1)

        nc.all_engine_barrier(sems_to_clear=range(min(s.num for s in sems), max(s.num for s in sems) + 1))
        with nc.Fori(0, DEPTH) as layer:
            mixer(layer)
            peer(layer)
            nc.all_engine_barrier(sems_to_clear=range(min(s.num for s in sems), max(s.num for s in sems) + 1))

        with nc.Block() as block:
            @block.scalar
            def _(act):
                norm_squares(act, 0)
                norm_root(act, 0)

            @block.tensor
            def _(pe):
                norm_mean(pe, 0)

            @block.vector
            def _(dve):
                dve.wait_ge(small_landed, 16)
                norm_scale(dve, 0, fing, hT)

            @block.sync
            def _(sp):
                sp.dma_start(fing, final_g).then_inc(small_landed, 16)
                sp.wait_ge(normed, KD + 1)
                sp.dma_start(out_cm, hT[:].rearrange("p a t -> p (a t)")).then_inc(out_stored, 16)
                sp.wait_ge(out_stored, 16)


def pack_weights(w_in, pool_w, pool_proj, ssm_glu, ssm_proj, attn_proj, w_out, peer_wq):
    def blocks(w, cols):
        part = w[:, cols]
        return part.reshape(-1, P, part.shape[1]).transpose(1, 0, 2).reshape(P, -1)

    out = np.zeros((DEPTH, CHUNKS, P, CHUNK), w_in.dtype)
    for l in range(DEPTH):
        put = lambda c, a: out[l, c, :, :a.shape[1]].__setitem__(slice(None), a)
        for c in range(13):
            put(c, blocks(w_in[l], slice(256 * c, 256 * c + 256)))
        put(C_MIX, pool_w[l].transpose(1, 0, 2).reshape(P, -1))
        for i in range(2):
            cols = np.r_[256 * i:256 * i + 256, 512 + 256 * i:512 + 256 * i + 256]
            put(C_GLU + i, blocks(ssm_glu[l], cols))
        for m in range(KD):
            col = slice(P * m, P * m + P)
            parts = []
            for b, w in enumerate((pool_proj[l], ssm_proj[l], attn_proj[l])):
                at = W_IN_MAIN + D * b + P * m
                parts += [blocks(w, col), blocks(w_in[l], slice(at, at + P))]
            both = np.concatenate(parts, axis=1)
            put(C_MERGE + 2 * m, both[:, :CHUNK])
            put(C_MERGE + 2 * m + 1, both[:, CHUNK:])
        for c in range(4):
            put(C_OUT + c, blocks(w_out[l], slice(256 * c, 256 * c + 256)))
        for c in range(8):
            put(C_WQ + c, blocks(peer_wq[l], slice(256 * c, 256 * c + 256)))
    return out.reshape(DEPTH * CHUNKS * P, CHUNK)


def kernel(x, positions, norm1_g, w_in, pool_w, pool_scale, pool_proj, ssm_a_re, ssm_a_im, ssm_log_dt,
           ssm_b_re, ssm_b_im, ssm_c_re, ssm_c_im, ssm_d, ssm_glu, ssm_proj, attn_proj, w_out, norm2_g,
           peer_wq, peer_k1, peer_k2, peer_u, peer_v, final_g):
    import concourse.bacc as bacc
    from concourse.bass_utils import run_bass_kernel_spmd

    a = {k: np.asarray(v) for k, v in locals().items() if k not in ("bacc", "run_bass_kernel_spmd")}
    columns = lambda v: v.reshape(DEPTH, -1, P).transpose(0, 2, 1)
    states = lambda v: v.reshape(DEPTH, PAIRS, 2 * 64).transpose(0, 2, 1)
    b_lay = lambda v: v.reshape(DEPTH, PAIRS, 2 * 64, 16).transpose(0, 2, 1, 3).reshape(DEPTH, P, -1)
    c_lay = lambda v: v.reshape(DEPTH, PAIRS, 2, 16, 64).transpose(0, 2, 4, 1, 3).reshape(DEPTH, P, -1)
    arrays = {
        "x_cm": a["x"][0].reshape(L, KD, P).transpose(2, 1, 0).reshape(P, KD * L),
        "positions": a["positions"].astype(np.int32).reshape(1, L),
        "inv_freq": np.tile(np.power(np.float32(10000.0), -np.arange(32, dtype=np.float32) / np.float32(32)), 4)
                      .astype(np.float32).reshape(P, 1),
        "weights": pack_weights(*(a[n] for n in ("w_in", "pool_w", "pool_proj", "ssm_glu", "ssm_proj", "attn_proj",
                                                 "w_out", "peer_wq"))),
        "keys": np.concatenate([a["peer_k1"].transpose(0, 2, 1), a["peer_k2"].transpose(0, 2, 1)], axis=2)
                  .reshape(DEPTH * P, 2 * NKEYS),
        "vecs": np.concatenate([columns(a["norm1_g"]), columns(a["norm2_g"]), columns(a["pool_scale"]), columns(a["ssm_d"]),
                                states(a["ssm_a_re"]), states(a["ssm_a_im"])], axis=2).reshape(DEPTH * P, V_END),
        "log_dt": a["ssm_log_dt"].reshape(DEPTH, PAIRS, 2).transpose(0, 2, 1).reshape(DEPTH * 2, PAIRS),
        "ssm_bc": np.concatenate([b_lay(a["ssm_b_re"]), b_lay(a["ssm_b_im"]), c_lay(a["ssm_c_re"]), c_lay(a["ssm_c_im"])],
                                 axis=2).reshape(DEPTH * P, -1),
        "table_u": a["peer_u"].reshape(DEPTH * EXPERTS, D),
        "table_v": a["peer_v"].reshape(DEPTH * EXPERTS, D),
        "final_g": a["final_g"].reshape(KD, P).T,
    }
    arrays = {k: np.ascontiguousarray(v) for k, v in arrays.items()}
    nc = bacc.Bacc("TRN2", target_bir_lowering=False, num_devices=1)
    args = [nc.dram_tensor(k, v.shape, mybir.dt.from_np(v.dtype), kind="ExternalInput").ap() for k, v in arrays.items()]
    args.append(nc.dram_tensor("out_cm", (P, KD * L), F32, kind="ExternalOutput").ap())
    trunk(nc, *args)
    r = run_bass_kernel_spmd(nc, [arrays], core_ids=[0])
    out = r.results[0]["out_cm"].reshape(P, KD, L).transpose(2, 1, 0).reshape(1, L, D)
    return np.ascontiguousarray(out)
```

```python
import math
from contextlib import ExitStack

import numpy as np

import concourse.bass as bass
from concourse import mybir

F32 = mybir.dt.float32
I32 = mybir.dt.int32
U32 = mybir.dt.uint32
ALU = mybir.AluOpType
ACT = mybir.ActivationFunctionType
AX = mybir.AxisListType

P = 128
L = 512
D = 1024
DEPTH = 2
KD = D // P
NT = L // P
EPS = 1e-6

POOL_WINDOWS = (2, 4, 8, 16)
PAIRS = 16
PER_TILE = 4
HEAD = 64
SLOTS = 4
KEYS = L + 2 * P
SCALE = HEAD ** -0.5
NEG = -1e30
LOWEST = -3.0e38

W_IN_MAIN = 3328
CHUNK = 17 * P
RING = 4
C_POOL, C_SSM, C_Q, C_K, C_V, C_MIX, C_GLU, C_MERGE, C_OUT, C_WQ, CHUNKS = 0, 2, 4, 7, 10, 13, 14, 16, 32, 36, 44

PH = 8
TOPK = 16
NKEYS = 128
EXPERTS = NKEYS * NKEYS
PICKS = PH * TOPK
NB = 8
ROUNDS = PICKS // NB
PE_SLOTS, DVE_SLOTS = (0, 1, 3, 4, 6, 7), (2, 5)
LIST_STEPS, HEAD_STEPS, PICK_STEPS = 8, 13, 4

V_G1, V_G2, V_PSCALE, V_D, V_ARE, V_AIM, V_END = 0, 8, 16, 20, 24, 40, 56

TWO_PI_HI = 6.28125
TWO_PI_MID = 0.0019350051879882812
TWO_PI_LO = 2 * math.pi - TWO_PI_HI - TWO_PI_MID
ROUND = 1.5 * 2.0 ** 23
PI_SAFE = 3.1415925
LN2_HI = 0.693359375
LN2_LO = math.log(2.0) - LN2_HI


class Steps:

    def __init__(self, eng, sem):
        self.eng, self.sem, self.n = eng, sem, 0

    def step(self, ins):
        ins.then_inc(self.sem, 1)
        self.n += 1

    def settle(self):
        self.eng.wait_ge(self.sem, self.n)

    def link(self, ins):
        self.step(ins)
        self.settle()


def mixer_order():
    head = [("tile", "pool_u", m) for m in range(4)] + [("tile", "ssm_u", m) for m in range(4)]
    dense = []
    for which in ("q", "k"):
        for m in range(6):
            dense.append(("tile", which, m))
            if m:
                dense.append(("tile", which + "swap", m - 1))
        dense.append(("tile", which + "swap", 5))
    dense += [("tile", "v", c, b) for c in range(3) for b in range(NT)]
    dense += [("tile", "mix", g) for g in range(4)]
    out, pair = list(head), 0
    for n, item in enumerate(dense):
        out.append(item)
        if n >= 2 and pair < PAIRS and (n - 2) % 2 == 0:
            out.append(("pair", pair))
            pair += 1
    out += [("pair", p) for p in range(pair, PAIRS)]
    out.append(("pairs_end",))
    for i in range(2):
        for j in range(2):
            out += [("tile", "glu_gate", 2 * i + j), ("tile", "glu_val", 2 * i + j)]
    out.append(("attention",))
    for m in range(KD):
        for b in range(3):
            out += [("tile", "branch", m, b), ("tile", "gate", m, b)]
    out += [("tile", "out", m) for m in range(KD)]
    out.append(("norm2",))
    out += [("tile", "h_tok", t, half) for t in range(NT) for half in range(2)]
    for h in range(PH):
        out += [("tile", "wq", 2 * h), ("tile", "wq", 2 * h + 1)]
        if h:
            out += [("tile", "score", h - 1, 0), ("tile", "score", h - 1, 1)]
    out += [("tile", "score", PH - 1, 0), ("tile", "score", PH - 1, 1)]
    return out


ORDER = mixer_order()
TILES = [item for item in ORDER if item[0] == "tile"]
TILE_NUMBER = {item: n for n, item in enumerate(TILES)}
BRANCH_START = {(0, 0): 0, (0, 1): 4, (1, 0): 12, (1, 1): 16, (2, 0): 24, (2, 1): 26}
BRANCH_K = {0: 4, 1: 4, 2: 2}


def chunk_last_tile():
    last = {}
    for item in TILES:
        n, kind = TILE_NUMBER[item], item[1]
        first = {"pool_u": C_POOL, "ssm_u": C_SSM, "q": C_Q, "k": C_K, "out": C_OUT, "wq": C_WQ}.get(kind)
        if first is not None:
            last[first + item[2] // 2] = n
        elif kind == "v":
            last[C_V + item[2]] = n
        elif kind == "mix":
            last[C_MIX] = n
        elif kind in ("glu_gate", "glu_val"):
            last[C_GLU + item[2] // 2] = n
        elif kind in ("branch", "gate"):
            m, b = item[2], item[3]
            at = BRANCH_START[(b, kind == "gate")]
            end = at + (8 if kind == "gate" else BRANCH_K[b]) - 1
            for j in {at // 17, end // 17}:
                last[C_MERGE + 2 * m + j] = n
    return last


CHUNK_LAST_TILE = chunk_last_tile()


def trunk(nc, x_cm, positions, inv_freq, weights, keys, vecs, log_dt, ssm_bc, table_u, table_v, final_g, out_cm):
    with ExitStack() as ctx:
        def sb(name, shape, dt=F32):
            return ctx.enter_context(nc.sbuf_tensor(name, shape, dt))

        sems = []
        land = [ctx.enter_context(nc.semaphore(f"row_landed{j}")) for j in range(NB)]

        def sem(name):
            s = ctx.enter_context(nc.semaphore(name))
            sems.append(s)
            return s

        xT = sb("xT", [P, KD, L])
        hT = sb("hT", [P, KD, L])
        wring = sb("wring", [P, RING, CHUNK])
        cosT = sb("cosT", [P, L])
        sinT = sb("sinT", [P, L])
        mask = sb("mask", [P, NT, KEYS])
        ident = sb("ident", [P, P])
        mean_ones = sb("mean_ones", [P, P])
        swap = sb("swap", [P, P])
        vec = sb("vec", [P, V_END])
        keysT = sb("keysT", [P, 2 * NKEYS])
        eps = sb("eps", [P, 1])
        layer_base = sb("layer_base", [P, 1])
        iota16 = sb("iota16", [P, TOPK])

        ARENA = 31488
        arena = sb("arena", [P, ARENA])

        def carve(at, n):
            assert at + n <= ARENA, (at, n)
            return arena[:, at:at + n]

        qT = carve(0, 3072).rearrange("p (m t) -> p m t", t=L)
        kT = carve(3072, 3072).rearrange("p (m t) -> p m t", t=L)
        vtok = carve(6144, 3072).rearrange("p (b c) -> p b c", b=NT)
        merged = carve(0, 4096).rearrange("p (m t) -> p m t", t=L)
        pool_in = carve(9216, 2048).rearrange("p (g t) -> p g t", t=L)
        pool_sum = carve(11264, 2048).rearrange("p (g t) -> p g t", t=L)
        mixT = pool_sum
        gluT = pool_in
        ssmT = carve(13312, 2048).rearrange("p (m t) -> p m t", t=L)
        pool_scratch = carve(15360, 1024).rearrange("p (i t) -> p i t", t=L)
        attnT = carve(27392, 1024).rearrange("p (m t) -> p m t", t=L)
        bbarT = carve(16384, 1024).rearrange("p (s m n) -> p s m n", s=2, m=4)
        c_blocks = carve(17408, 1536).rearrange("p (s g c) -> p s g c", s=3, g=PAIRS)
        pow_b = carve(18944, 1024).rearrange("p (s g t) -> p s g t", s=2, g=PAIRS)
        pow_a = carve(19968, 512).rearrange("p (s g t) -> p s g t", s=2, g=PAIRS)
        small = carve(20480, 544).rearrange("p (i g) -> p i g", g=PAIRS)
        raw = carve(21248, 1024).rearrange("p (i t) -> p i t", t=L)
        rope_t = carve(22272, 1024).rearrange("p (i t) -> p i t", t=L)
        tabs = carve(23296, 2048).rearrange("p (i s t) -> p i s t", i=2, s=2)
        rotin = carve(25344, 2048).rearrange("p (s t) -> p s t", t=L)
        scanned = carve(27392, 2048).rearrange("p (i s t) -> p i s t", i=2, s=2)
        prods = [carve(29440 + i * L, L) for i in range(4)]
        pow_tmp = carve(25344, 1024).rearrange("p (s g t) -> p s g t", s=2, g=PAIRS)
        bc_in = carve(23296, 1024).rearrange("p (s g c) -> p s g c", s=4, g=PAIRS)
        b_blocks = carve(27392, 1024).rearrange("p (s g c) -> p s g c", s=2, g=PAIRS)
        bbar = carve(28416, 1024).rearrange("p (s g c) -> p s g c", s=2, g=PAIRS)
        bb_tmp = carve(24320, 1024).rearrange("p (s g c) -> p s g c", s=2, g=PAIRS)
        srow = carve(23296, 1536).rearrange("p (i k) -> p i k", i=2)
        pT = carve(24832, 1536).rearrange("p (i k) -> p i k", i=2)
        otok = carve(26368, 512).rearrange("p (i c) -> p i c", i=2)
        stats = carve(26880, 64)
        sig = carve(23296, 1024).rearrange("p (i t) -> p i t", t=L)
        gated = carve(24320, 1024).rearrange("p (i t) -> p i t", t=L)
        rms = carve(30000, L)
        rstd = carve(30512, L)
        scores_flat = carve(0, 8192)
        scores = carve(0, 8192).rearrange("p (t j k) -> p t j k", t=NT, j=16)
        out_tok = hT[:].rearrange("p a t -> p (a t)").rearrange("p (t d) -> p t d", t=NT)
        qpT = carve(8192, 8192).rearrange("p (j t) -> p j t", t=L)
        rows = carve(8192, NB * D).rearrange("p (j d) -> p j d", d=D)
        h_tok = carve(16384, 4096).rearrange("p (t d) -> p t d", t=NT)
        diag = carve(20480, NB * P).rearrange("p (j c) -> p j c", c=P)
        h_now = carve(21504, D)
        topv = carve(22528, 256)
        topif = carve(22784, 256)
        list_in = carve(23040, NKEYS)
        list_left = carve(23168, NKEYS)
        list_v = carve(23296, TOPK)
        list_i = carve(23312, TOPK).bitcast(U32)
        cand = carve(23328, TOPK * TOPK)
        cand_left = carve(23584, TOPK * TOPK)
        cand_v = carve(23840, TOPK)
        cand_p = carve(23856, TOPK).bitcast(U32)
        place_u = carve(23872, 2 * TOPK).bitcast(U32).rearrange("p (s k) -> p s k", s=2)
        place_f = carve(23904, 2 * TOPK)
        onehot = carve(23936, 2 * TOPK * TOPK)
        head_s = carve(24448, PICKS)
        head_k = carve(24576, 2 * PICKS)
        expert_f = carve(24832, PICKS)
        gate_e = carve(24960, PICKS)
        gate_s = carve(25088, 2 * PH)
        expert = carve(25600, NT * PICKS).bitcast(U32)
        gates = carve(26112, NT * PICKS)
        act_all = carve(26752, PICKS)
        gelu_all = carve(26880, PICKS)
        w_all = carve(27008, PICKS)
        act_stage = carve(27136, NB)
        w_stage = carve(27144, NB)
        idx_stage = carve(27152, 2 * NB).bitcast(U32).rearrange("p (i n) -> p i n", i=2)
        zeros = carve(27168, P)
        fing = carve(27296, KD)
        dve_sum = carve(27304, D)

        ps = ctx.enter_context(nc.psum_tensor("ps", [P, 8, L], F32))

        s_load = sem("s_load")
        s_const = sem("s_const")
        s_masks = sem("s_masks")
        s_modmask = sem("s_modmask")
        s_angle = sem("s_angle")
        s_dve = sem("s_dve")
        residue = carve(0, P)
        posi = carve(128, L).bitcast(I32)
        freq = carve(1700, 1)
        angle = carve(2048, L)
        turns = carve(2560, L)
        ang_c = carve(3072, L)
        wrap = carve(3584, L)

        def reduce_angle(dve, st, ang, k, cos_ang, tmp):
            st.link(dve.tensor_scalar(k, ang, 1 / (2 * math.pi), ROUND, ALU.mult, ALU.add))
            st.link(dve.tensor_scalar(k, k, -ROUND, None, ALU.add))
            for part in (TWO_PI_HI, TWO_PI_MID, TWO_PI_LO):
                st.link(dve.scalar_tensor_tensor(ang, k, -part, ang, ALU.mult, ALU.add))
            st.link(dve.tensor_scalar(cos_ang, ang, math.pi / 2, None, ALU.add))
            st.link(dve.tensor_scalar(tmp, cos_ang, math.pi, -2 * math.pi, ALU.is_gt, ALU.mult))
            st.link(dve.tensor_tensor(cos_ang, cos_ang, tmp, ALU.add))
            st.link(dve.tensor_scalar(cos_ang, cos_ang, PI_SAFE, -PI_SAFE, ALU.min, ALU.max))
            st.link(dve.tensor_scalar(ang, ang, PI_SAFE, -PI_SAFE, ALU.min, ALU.max))

        with nc.Block() as block:
            @block.sync
            def _(sp):
                sp.dma_start(xT[:].rearrange("p a t -> p (a t)"), x_cm).then_inc(s_load, 16)
                sp.dma_start(posi, positions.broadcast_to([P, L])).then_inc(s_load, 16)
                sp.dma_start(freq, inv_freq).then_inc(s_load, 16)

            @block.gpsimd
            def _(pool):
                st = Steps(pool, s_const)
                st.step(pool.memset(ident[:], 0.0))
                st.step(pool.memset(mean_ones[:], 1.0 / D))
                st.step(pool.memset(swap[:], 0.0))
                st.step(pool.memset(residue[0:4, :], 0.0))
                st.step(pool.memset(eps[:], EPS))
                st.step(pool.memset(layer_base[:], 0.0))
                st.step(pool.memset(mask[:], 0.0))
                st.settle()
                st.step(pool.iota(iota16[:], [[1, TOPK]], base=0, channel_multiplier=0,
                                  allow_small_or_imprecise_dtypes=True))
                st.step(pool.affine_select(out=ident[:], in_=ident[:], compare_op=ALU.not_equal, fill=1.0, base=0,
                                           pattern=[[-1, P]], channel_multiplier=1))
                st.step(pool.affine_select(out=residue[0:4, :].rearrange("p (m c) -> p m c", c=4),
                                           in_=residue[0:4, :].rearrange("p (m c) -> p m c", c=4),
                                           compare_op=ALU.not_equal, fill=1.0, base=0,
                                           pattern=[[0, P // 4], [-1, 4]], channel_multiplier=1))
                sw = swap[:].rearrange("p (h s j) -> p h s j", h=2, s=2)
                st.step(pool.affine_select(out=sw[:, :, 0, :], in_=sw[:, :, 0, :], compare_op=ALU.not_equal, fill=-1.0,
                                           base=-32, pattern=[[-64, 2], [-1, 32]], channel_multiplier=1))
                st.settle()
                st.step(pool.affine_select(out=sw[:, :, 1, :], in_=sw[:, :, 1, :], compare_op=ALU.not_equal, fill=1.0,
                                           base=0, pattern=[[-64, 2], [-1, 32]], channel_multiplier=1))
                for b in range(NT):
                    near = mask[:, b, 0:L].rearrange("p (b i) -> p b i", b=NT)
                    st.link(pool.affine_select(out=near, in_=near, compare_op=ALU.is_ge, fill=NEG, base=b,
                                               pattern=[[-1, NT], [-4, P]], channel_multiplier=4))
                    st.step(pool.affine_select(out=near, in_=near, compare_op=ALU.is_ge, fill=NEG, base=P - b,
                                               pattern=[[1, NT], [4, P]], channel_multiplier=-4))
                far = mask[:, :, L:KEYS].rearrange("p b (s i) -> p b s i", s=2)
                st.link(pool.affine_select(out=far, in_=far, compare_op=ALU.is_ge, fill=NEG, base=0,
                                           pattern=[[0, NT], [0, 2], [-1, P]], channel_multiplier=1))
                pool.sem_inc(s_masks, 1)

            @block.tensor
            def _(pe):
                pe.wait_ge(s_masks, 1)
                pe.matmul(ps[:, 0, 0:P], residue[0:4, :], residue[0:4, :], start=True, stop=True).then_inc(s_modmask, 1)

            @block.vector
            def _(dve):
                st = Steps(dve, s_dve)
                dve.wait_ge(s_load, 48)
                st.link(dve.tensor_copy(angle, posi))
                st.link(dve.tensor_scalar(angle, angle, freq, None, ALU.mult))
                reduce_angle(dve, st, angle, turns, ang_c, wrap)
                dve.sem_inc(s_angle, 1)
                dve.wait_ge(s_modmask, 1)
                st.link(dve.tensor_scalar(wrap[:, 0:P], ps[:, 0, 0:P], -1.0, -NEG, ALU.add, ALU.mult))
                for b in range(NT):
                    st.step(dve.tensor_tensor(mask[:, b, L + P:KEYS], mask[:, b, L + P:KEYS], wrap[:, 0:P], ALU.add))

            @block.scalar
            def _(act):
                act.wait_ge(s_angle, 1)
                act.activation(sinT[:], angle, ACT.Sin)
                act.activation(cosT[:], ang_c, ACT.Sin)

        layer_sems_from = len(sems)
        w_landed = [sem(f"w_landed{i}") for i in range(RING)]
        small_landed = sem("small_landed")
        tiles_done = sem("tiles_done")
        bank_free = [sem(f"bank_free{i}") for i in range(4)]
        squares = sem("squares")
        mean_done = sem("mean_done")
        root_done = sem("root_done")
        normed = sem("normed")
        act_steps = sem("act_steps")
        dve_steps = sem("dve_steps")
        pool_steps = sem("pool_steps")
        raw_ready = sem("raw_ready")
        roped = sem("roped")
        pool_in_ready = sem("pool_in_ready")
        pooled_ready = sem("pooled_ready")
        mixed = sem("mixed")
        ssm_in_ready = sem("ssm_in_ready")
        blocks_ready = sem("blocks_ready")
        poles_ready = sem("poles_ready")
        bbar_ready = sem("bbar_ready")
        bbarT_done = sem("bbarT_done")
        bbarT_ready = sem("bbarT_ready")
        tab_ready = sem("tab_ready")
        x_done = sem("x_done")
        x_free = sem("x_free")
        scan_done = sem("scan_done")
        prod_dve = sem("prod_dve")
        prod_pool = sem("prod_pool")
        y_done = sem("y_done")
        y_taken = sem("y_taken")
        y_gelu = sem("y_gelu")
        v_ready = sem("v_ready")
        glu_sig = sem("glu_sig")
        glu_ready = sem("glu_ready")
        sc_done = sem("sc_done")
        sc_max = sem("sc_max")
        exp_done = sem("exp_done")
        pt_done = sem("pt_done")
        pt_copied = sem("pt_copied")
        pv_done = sem("pv_done")
        o_done = sem("o_done")
        ot_done = sem("ot_done")
        ot_copied = sem("ot_copied")
        gate_sig = sem("gate_sig")
        gate_used = sem("gate_used")
        x_mixed = sem("x_mixed")
        wq_copied = sem("wq_copied")
        mix_evac = sem("mix_evac")
        out_stored = sem("out_stored")

        def norm_squares(act, base):
            for k in range(KD):
                act.activation(hT[:, k, :], xT[:, k, :], ACT.Square).then_inc(squares, 1)

        def norm_mean(pe, which):
            for k in range(KD):
                pe.wait_ge(squares, KD * which + k + 1)
                mm = pe.matmul(ps[:, 0, :], mean_ones[:], hT[:, k, :], start=(k == 0), stop=(k == KD - 1))
            mm.then_inc(mean_done, 1)

        def norm_root(act, which):
            act.wait_ge(mean_done, which + 1)
            act.activation(rms, ps[:, 0, :], ACT.Sqrt, bias=eps[:, 0:1]).then_inc(root_done, 1)

        def norm_scale(dve, which, gain, dst):
            dve.wait_ge(root_done, which + 1)
            dve.reciprocal(rstd, rms).then_inc(normed, 1)
            dve.wait_ge(normed, which * (KD + 1) + 1)
            for k in range(KD):
                dve.scalar_tensor_tensor(dst[:, k, :], xT[:, k, :], gain[:, k:k + 1], rstd, ALU.mult,
                                         ALU.mult).then_inc(normed, 1)

        def chunk_weight(c, at, n=P):
            return wring[:, c % RING, at:at + n]

        def pick_list(dve, n, j):
            base = (n * 16 + j) * LIST_STEPS + 1
            dve.wait_ge(list_steps, base)
            dve.tensor_copy(list_in, scores_flat[:, bass.ds(n * (16 * NKEYS) + j * NKEYS, NKEYS)]).then_inc(list_steps, 1)
            yield
            dve.wait_ge(list_steps, base + 1)
            dve.sem_inc(dve_turn, 1)
            dve.max(list_v[:, 0:8], list_in).then_inc(list_steps, 1)
            yield
            dve.wait_ge(list_steps, base + 2)
            dve.sem_inc(dve_turn, 1)
            dve.match_replace(list_left, list_v[:, 0:8], list_in, LOWEST).then_inc(list_steps, 1)
            yield
            dve.max_index(list_i[:, 0:8], list_v[:, 0:8], list_in).then_inc(list_steps, 1)
            yield
            dve.wait_ge(list_steps, base + 3)
            dve.sem_inc(dve_turn, 1)
            dve.max(list_v[:, 8:16], list_left).then_inc(list_steps, 1)
            yield
            dve.wait_ge(list_steps, base + 5)
            dve.sem_inc(dve_turn, 1)
            dve.max_index(list_i[:, 8:16], list_v[:, 8:16], list_left).then_inc(list_steps, 1)
            yield
            dve.tensor_copy(topv[:, bass.ds(j * TOPK, TOPK)], list_v).then_inc(list_steps, 1)
            yield
            dve.wait_ge(list_steps, base + 6)
            dve.tensor_copy(topif[:, bass.ds(j * TOPK, TOPK)], list_i).then_inc(list_steps, 1)
            yield

        def pick_head(dve, n, h):
            base = (n * PH + h) * HEAD_STEPS + 1
            dve.wait_ge(list_steps, (n * 16 + 2 * h + 2) * LIST_STEPS + 1)
            dve.sem_inc(dve_turn, 1)
            dve.wait_ge(head_steps, base)
            dve.tensor_tensor(cand.rearrange("p (a b) -> p a b", a=TOPK),
                              topv[:, bass.ds(h * (2 * TOPK), TOPK)].unsqueeze(2).broadcast_to([P, TOPK, TOPK]),
                              topv[:, bass.ds(h * (2 * TOPK) + TOPK, TOPK)].unsqueeze(1).broadcast_to([P, TOPK, TOPK]),
                              ALU.add).then_inc(head_steps, 1)
            yield
            dve.wait_ge(head_steps, base + 1)
            dve.sem_inc(dve_turn, 1)
            dve.max(cand_v[:, 0:8], cand).then_inc(head_steps, 1)
            yield
            dve.wait_ge(head_steps, base + 2)
            dve.sem_inc(dve_turn, 1)
            dve.match_replace(cand_left, cand_v[:, 0:8], cand, LOWEST).then_inc(head_steps, 1)
            yield
            dve.max_index(cand_p[:, 0:8], cand_v[:, 0:8], cand).then_inc(head_steps, 1)
            yield
            dve.wait_ge(head_steps, base + 3)
            dve.sem_inc(dve_turn, 1)
            dve.max(cand_v[:, 8:16], cand_left).then_inc(head_steps, 1)
            yield
            dve.wait_ge(head_steps, base + 5)
            dve.sem_inc(dve_turn, 1)
            dve.max_index(cand_p[:, 8:16], cand_v[:, 8:16], cand_left).then_inc(head_steps, 1)
            yield
            dve.tensor_copy(head_s[:, bass.ds(h * TOPK, TOPK)], cand_v).then_inc(head_steps, 1)
            yield
            dve.wait_ge(head_steps, base + 6)
            dve.tensor_scalar(place_u[:, 0, :], cand_p, 4, None, ALU.logical_shift_right).then_inc(head_steps, 1)
            yield
            dve.tensor_scalar(place_u[:, 1, :], cand_p, 15, None, ALU.bitwise_and).then_inc(head_steps, 1)
            yield
            dve.wait_ge(head_steps, base + 9)
            dve.tensor_copy(place_f, place_u.rearrange("p s k -> p (s k)")).then_inc(head_steps, 1)
            yield
            dve.wait_ge(head_steps, base + 10)
            dve.tensor_tensor(onehot.rearrange("p (n j) -> p n j", j=TOPK),
                              place_f.unsqueeze(2).broadcast_to([P, 2 * TOPK, TOPK]),
                              iota16[:].unsqueeze(1).broadcast_to([P, 2 * TOPK, TOPK]), ALU.is_equal).then_inc(head_steps, 1)
            yield
            dve.wait_ge(head_steps, base + 11)
            four = onehot.rearrange("p (s k j) -> p s k j", s=2, k=TOPK)
            keys_of = topif[:, bass.ds(h * (2 * TOPK), 2 * TOPK)].rearrange("p (s j) -> p s j", s=2)
            dve.tensor_tensor(four, four, keys_of.unsqueeze(2).broadcast_to([P, 2, TOPK, TOPK]),
                              ALU.mult).then_inc(head_steps, 1)
            yield
            dve.wait_ge(head_steps, base + 12)
            dve.tensor_reduce(head_k[:, bass.ds(h * (2 * TOPK), 2 * TOPK)],
                              onehot.rearrange("p (n j) -> p n j", j=TOPK), AX.X, ALU.add).then_inc(head_steps, 1)
            yield

        def settle_picks(dve, n):
            base = n * PICK_STEPS + 1
            dve.wait_ge(head_steps, (n + 1) * (PH * HEAD_STEPS) + 1)
            hs = head_s.rearrange("p (h k) -> p h k", k=TOPK)
            hk = head_k.rearrange("p (h s k) -> p h s k", s=2, k=TOPK)
            ge = gate_e.rearrange("p (h k) -> p h k", k=TOPK)
            dve.tensor_tensor(ge, hs, hs[:, :, 0:1].broadcast_to([P, PH, TOPK]), ALU.subtract).then_inc(shifted, 1)
            dve.scalar_tensor_tensor(expert_f.rearrange("p (h k) -> p h k", k=TOPK), hk[:, :, 0, :], float(NKEYS),
                                     hk[:, :, 1, :], ALU.mult, ALU.add).then_inc(pick_steps, 1)
            dve.wait_ge(pick_steps, base + 1)
            dve.tensor_scalar(expert[:, bass.ds(n * PICKS, PICKS)], expert_f, layer_base[:, 0:1], None,
                              ALU.add).then_inc(picks_ready, 1)
            dve.wait_ge(exp_ready, n + 1)
            dve.tensor_reduce(gate_s[:, 0:PH], ge, AX.X, ALU.add).then_inc(pick_steps, 1)
            dve.wait_ge(pick_steps, base + 2)
            dve.reciprocal(gate_s[:, PH:2 * PH], gate_s[:, 0:PH]).then_inc(pick_steps, 1)
            dve.wait_ge(pick_steps, base + 3)
            dve.tensor_tensor(gates[:, bass.ds(n * PICKS, PICKS)].rearrange("p (h k) -> p h k", k=TOPK), ge,
                              gate_s[:, PH:2 * PH].unsqueeze(2).broadcast_to([P, PH, TOPK]), ALU.mult).then_inc(pick_steps, 1)
            dve.wait_ge(pick_steps, base + 4)
            dve.sem_inc(dve_turn, 1)

        def mixer(layer):
            def attend_out(dve, st, i):
                b, h = i // SLOTS, i % SLOTS
                dve.wait_ge(pv_done, i + 1)
                st.link(dve.reciprocal(stats[:, 48 + i % 2:49 + i % 2], stats[:, 32 + i:33 + i]))
                dve.tensor_scalar(otok[:, b % 2, h * HEAD:(h + 1) * HEAD], ps[:, 2 + i % 2, 0:HEAD],
                                  stats[:, 48 + i % 2:49 + i % 2], None, ALU.mult).then_inc(o_done, 1)
                if h == 0 and b:
                    move_home(dve, b - 1)
                if i == 15:
                    move_home(dve, b)

            def move_home(dve, b):
                dve.wait_ge(ot_done, b + 1)
                dve.tensor_copy(attnT[:, :, :].rearrange("p m (i b) -> p m b i", b=NT)[:, :, b, :],
                                ps[:, 1, 0:256].rearrange("p (m i) -> p m i", m=2)).then_inc(ot_copied, 1)

            with nc.Block() as block:
                @block.sync
                def _(sp):
                    sp.dma_start(vec[:], vecs[bass.ts(layer, P), :]).then_inc(small_landed, 16)
                    for half in range(2):
                        sp.dma_start(small[64 * half:64 * half + 64, 0, :],
                                     log_dt[bass.ds(layer * 2 + half, 1), :].broadcast_to([64, PAIRS])).then_inc(small_landed, 16)
                    sp.dma_start(bc_in.rearrange("p s g c -> p (s g c)"), ssm_bc[bass.ts(layer, P), :]).then_inc(small_landed, 16)
                    sp.dma_start(keysT[:], keys[bass.ts(layer, P), :]).then_inc(small_landed, 16)
                    for c in range(CHUNKS):
                        if c >= RING:
                            sp.wait_ge(tiles_done, CHUNK_LAST_TILE[c - RING] + 1)
                        sp.dma_start(wring[:, c % RING, :],
                                     weights[bass.ts(layer * CHUNKS + c, P), :]).then_inc(w_landed[c % RING], 16)

                @block.gpsimd
                def _(pool):
                    st = Steps(pool, pool_steps)
                    st.step(pool.memset(b_blocks, 0.0))
                    st.step(pool.memset(c_blocks, 0.0))
                    pool.wait_ge(small_landed, 80)
                    st.settle()
                    for g in range(2):
                        rows_g, cols_g = slice(64 * g, 64 * g + 64), slice(16 * g, 16 * g + 16)
                        st.step(pool.tensor_copy(b_blocks[rows_g, :, :, cols_g], bc_in[rows_g, 0:2, :, :]))
                        st.step(pool.tensor_copy(c_blocks[rows_g, 0, :, cols_g], bc_in[rows_g, 2, :, :]))
                        st.step(pool.tensor_scalar(c_blocks[rows_g, 1, :, cols_g], bc_in[rows_g, 2, :, :], -1.0, None, ALU.mult))
                        st.step(pool.tensor_scalar(c_blocks[rows_g, 2, :, cols_g], bc_in[rows_g, 3, :, :], -1.0, None, ALU.mult))
                    st.settle()
                    pool.sem_inc(blocks_ready, 1)

                    pool.wait_ge(poles_ready, 1)
                    pool.wait_ge(bbar_ready, 1)
                    st.step(pool.memset(pow_b[:, 0, :, 0:1], 1.0))
                    st.step(pool.memset(pow_b[:, 1, :, 0:1], 0.0))
                    st.step(pool.memset(pow_a[:, 0, :, 0:1], 1.0))
                    st.step(pool.memset(pow_a[:, 1, :, 0:1], 0.0))
                    st.settle()
                    w_re, w_im, t0, t1 = small[:, 30, :], small[:, 31, :], small[:, 32, :], small[:, 33, :]
                    for table, count in ((pow_b, 5), (pow_a, 4)):
                        for e in range(count):
                            d = 1 << e
                            lo = lambda s: table[:, s, :, 0:d]
                            hi = lambda s: table[:, s, :, d:2 * d]
                            bc = lambda w: w.unsqueeze(2).broadcast_to([P, PAIRS, d])
                            ta, tb = pow_tmp[:, 0, :, 0:d], pow_tmp[:, 1, :, 0:d]
                            st.step(pool.tensor_tensor(hi(0), lo(0), bc(w_re), ALU.mult))
                            st.step(pool.tensor_tensor(hi(1), lo(1), bc(w_re), ALU.mult))
                            st.step(pool.tensor_tensor(ta, lo(1), bc(w_im), ALU.mult))
                            st.step(pool.tensor_tensor(tb, lo(0), bc(w_im), ALU.mult))
                            st.settle()
                            st.step(pool.tensor_tensor(hi(0), hi(0), ta, ALU.subtract))
                            st.step(pool.tensor_tensor(hi(1), hi(1), tb, ALU.add))
                            st.step(pool.tensor_tensor(t0, w_im, w_im, ALU.mult))
                            st.step(pool.tensor_tensor(t1, w_re, w_im, ALU.mult))
                            st.settle()
                            st.link(pool.tensor_tensor(w_re, w_re, w_re, ALU.mult))
                            st.step(pool.tensor_tensor(w_re, w_re, t0, ALU.subtract))
                            st.step(pool.tensor_tensor(w_im, t1, t1, ALU.add))
                            st.settle()

                    def table_of(p):
                        a = lambda s: pow_a[:, s, p, :].unsqueeze(2).broadcast_to([P, 16, 32])
                        b = lambda s: pow_b[:, s, p, :].unsqueeze(1).broadcast_to([P, 16, 32])
                        o = lambda s: tabs[:, p % 2, s, :].rearrange("p (a b) -> p a b", b=32)
                        ta = pool_scratch[:, 0, :].rearrange("p (a b) -> p a b", b=32)
                        tb = pool_scratch[:, 1, :].rearrange("p (a b) -> p a b", b=32)
                        st.step(pool.tensor_tensor(o(0), a(0), b(0), ALU.mult))
                        st.step(pool.tensor_tensor(ta, a(1), b(1), ALU.mult))
                        st.step(pool.tensor_tensor(o(1), a(1), b(0), ALU.mult))
                        st.step(pool.tensor_tensor(tb, a(0), b(1), ALU.mult))
                        st.settle()
                        st.step(pool.tensor_tensor(o(0), o(0), ta, ALU.subtract))
                        st.link(pool.tensor_tensor(o(1), o(1), tb, ALU.add))
                        pool.sem_inc(tab_ready, 1)

                    table_of(0)
                    table_of(1)

                    def windows():
                        pool.wait_ge(pool_in_ready, 4)
                        for g, win in enumerate(POOL_WINDOWS):
                            src = pool_in[:, g, :]
                            bufs = [pool_sum[:, g, :], pool_scratch[:, 0, :]]
                            cur, shift, n = src, 1, 0
                            while shift < win:
                                left = int(math.log2(win // shift)) - 1
                                dst = bufs[left % 2]
                                st.step(pool.tensor_copy(dst[:, 0:shift], cur[:, 0:shift]))
                                st.step(pool.tensor_tensor(dst[:, shift:L], cur[:, shift:L], cur[:, 0:L - shift], ALU.add))
                                st.settle()
                                cur, shift = dst, shift * 2
                            st.step(pool.tensor_scalar(cur[:, win - 1:L], cur[:, win - 1:L], 1.0 / win, None, ALU.mult))
                            for t in range(1, win - 1):
                                st.step(pool.tensor_scalar(cur[:, t:t + 1], cur[:, t:t + 1], 1.0 / (t + 1), None, ALU.mult))
                            st.settle()
                            st.link(pool.tensor_tensor(src, cur, src, ALU.subtract))
                            pool.sem_inc(pooled_ready, 1)

                    windows()
                    for p in range(PAIRS):
                        pool.wait_ge(scan_done, 2 * (p + 1))
                        if p:
                            pool.wait_ge(y_done, p)
                        st.step(pool.tensor_tensor(prods[2], scanned[:, p % 2, 1, :], tabs[:, p % 2, 0, :], ALU.mult))
                        st.link(pool.tensor_tensor(prods[3], scanned[:, p % 2, 0, :], tabs[:, p % 2, 1, :], ALU.mult))
                        pool.sem_inc(prod_pool, 1)
                        if p + 2 < PAIRS:
                            pool.wait_ge(prod_dve, 2 * (p + 1))
                            table_of(p + 2)

                @block.tensor
                def _(pe):
                    norm_mean(pe, 0)
                    pe.wait_ge(normed, KD + 1)

                    def need_chunk(c):
                        pe.wait_ge(w_landed[c % RING], 16 * (c // RING + 1))

                    def product(n, lhs, rhs, width=L, chunk_at=None):
                        for k in range(len(lhs)):
                            if chunk_at and k in chunk_at:
                                need_chunk(chunk_at[k])
                            mm = pe.matmul(ps[:, n % 4, 0:width], lhs[k], rhs[k], start=(k == 0), stop=(k == len(lhs) - 1))
                        return mm

                    def tile(item):
                        n, kind = TILE_NUMBER[item], item[1]
                        if n >= 4:
                            pe.wait_ge(bank_free[n % 4], n // 4)
                        first = {"pool_u": C_POOL, "ssm_u": C_SSM, "q": C_Q, "k": C_K, "out": C_OUT, "wq": C_WQ}.get(kind)
                        if first is not None:
                            m = item[2]
                            c = first + m // 2
                            src = merged if kind == "out" else hT
                            if kind == "out" and m == 0:
                                pe.wait_ge(gate_used, 3 * KD)
                            mm = product(n, [chunk_weight(c, k * 256 + (m % 2) * P) for k in range(KD)],
                                         [src[:, k, :] for k in range(KD)], chunk_at={0: c})
                        elif kind in ("qswap", "kswap"):
                            pe.wait_ge(raw_ready, item[2] + 1 + (6 if kind == "kswap" else 0))
                            mm = product(n, [swap[:]], [raw[:, item[2] % 2, :]])
                        elif kind == "v":
                            c, b = C_V + item[2], item[3]
                            mm = product(n, [hT[:, k, :].rearrange("p (i b) -> p b i", b=NT)[:, b, :] for k in range(KD)],
                                         [chunk_weight(c, k * 256, 256) for k in range(KD)], width=256, chunk_at={0: c})
                        elif kind == "mix":
                            g = item[2]
                            pe.wait_ge(pooled_ready, g + 1)
                            mm = product(n, [chunk_weight(C_MIX, g * P)], [pool_in[:, g, :]], chunk_at={0: C_MIX})
                        elif kind in ("glu_gate", "glu_val"):
                            m = item[2]
                            c = C_GLU + m // 2
                            pe.wait_ge(y_gelu, 4)
                            at = (m % 2) * P + (256 if kind == "glu_gate" else 0)
                            mm = product(n, [chunk_weight(c, k * 512 + at) for k in range(4)],
                                         [ssmT[:, k, :] for k in range(4)], chunk_at={0: c})
                        elif kind in ("branch", "gate"):
                            m, b = item[2], item[3]
                            at = BRANCH_START[(b, kind == "gate")]
                            rows_n = 8 if kind == "gate" else BRANCH_K[b]
                            src = hT if kind == "gate" else (mixT, gluT, attnT)[b]
                            if kind == "branch" and m == 0:
                                pe.wait_ge((mixed, glu_ready, ot_copied)[b], 4)
                            where = [(C_MERGE + 2 * m + (at + k) // 17, (at + k) % 17) for k in range(rows_n)]
                            mm = product(n, [chunk_weight(c, j * P) for c, j in where],
                                         [src[:, k, :] for k in range(rows_n)],
                                         chunk_at={k: c for k, (c, j) in enumerate(where) if k == 0 or c != where[k - 1][0]})
                        elif kind == "h_tok":
                            t, half = item[2], item[3]
                            if (t, half) == (0, 0):
                                pe.wait_ge(normed, 2 * (KD + 1))
                            for k in range(4):
                                mm = pe.transpose(ps[:, n % 4, k * P:(k + 1) * P], hT[:, 4 * half + k, t * P:(t + 1) * P], ident[:])
                        elif kind == "score":
                            j = 2 * item[2] + item[3]
                            pe.wait_ge(wq_copied, j + 1)
                            for k in range(NT):
                                mm = pe.matmul(ps[:, n % 4, k * P:(k + 1) * P], qpT[:, j, k * P:(k + 1) * P],
                                               keysT[:, (j % 2) * NKEYS:(j % 2 + 1) * NKEYS], start=True, stop=True)
                        mm.then_inc(tiles_done, 1)

                    def pair_in(p):
                        m, a = p // PER_TILE, p % PER_TILE
                        part = slice(32 * a, 32 * a + 32)
                        if p == 0:
                            pe.wait_ge(bbar_ready, 1)
                            for s in range(2):
                                for mm_ in range(4):
                                    blk = bbar[:, s, 4 * mm_:4 * mm_ + 4, :].rearrange("p g c -> p (g c)")
                                    last = pe.transpose(ps[:, 4 + s, mm_ * P:(mm_ + 1) * P], blk, ident[:])
                            last.then_inc(bbarT_done, 1)
                            pe.wait_ge(ssm_in_ready, 4)
                            pe.wait_ge(bbarT_ready, 2)
                        else:
                            pe.wait_ge(x_free, p)
                        for s in range(2):
                            mm = pe.matmul(ps[:, 4 + s, :], bbarT[part, s, m, :], ssmT[part, m, :], start=True, stop=True)
                        mm.then_inc(x_done, 1)

                    def pair_out(p):
                        m, a = p // PER_TILE, p % PER_TILE
                        if p == 0:
                            pe.wait_ge(blocks_ready, 1)
                        if a == 0 and m >= 2:
                            pe.wait_ge(y_taken, m - 1)
                        pe.wait_ge(prod_dve, 2 * (p + 1))
                        pe.wait_ge(prod_pool, p + 1)
                        for i, c in enumerate((0, 1, 2, 2)):
                            mm = pe.matmul(ps[32 * a:32 * a + 32, 6 + m % 2, :], c_blocks[:, c, p, :], prods[i],
                                           start=(i == 0), stop=(i == 3))
                        mm.then_inc(y_done, 1)

                    def attention():
                        for b in range(4):
                            done = len([i for i in range(TILE_NUMBER[("tile", "branch", 0, 0)]) if i % 4 == b])
                            pe.wait_ge(bank_free[b], done)
                        pe.wait_ge(y_taken, 4)
                        pe.wait_ge(roped, 12)
                        pe.wait_ge(v_ready, 12)
                        its = [(b, h) for b in range(NT) for h in range(SLOTS)]

                        def rows_of(t, h, g):
                            m = 2 * g + h // 2
                            return t[HEAD * (h % 2):HEAD * (h % 2) + HEAD, m, :].rearrange("p (i b) -> p b i", b=NT)

                        def score(i):
                            b, h = its[i]
                            bank = 4 + 2 * (i % 2)
                            if i >= 2:
                                pe.wait_ge(sc_max, i - 1)
                            pe.matmul(ps[:, bank, :], rows_of(qT, h, 0)[:, b, :], rows_of(kT, h, 0), start=True, stop=True)
                            for g in (1, 2):
                                mm = pe.matmul(ps[:, bank + 1, (g - 1) * P:g * P], rows_of(qT, h, g)[:, b, :],
                                               rows_of(kT, h, g)[:, b, :], start=True, stop=True)
                            mm.then_inc(sc_done, 1)

                        def turn(i):
                            pe.wait_ge(exp_done, i + 1)
                            if i:
                                pe.wait_ge(pt_copied, i)
                            if i > 1 and (i - 1) % SLOTS == 0:
                                pe.wait_ge(ot_copied, (i - 1) // SLOTS)
                            for j in range(6):
                                mm = pe.transpose(ps[:, j // 4, (j % 4) * P:(j % 4 + 1) * P],
                                                  srow[:, i % 2, j * P:(j + 1) * P], ident[:])
                            mm.then_inc(pt_done, 1)

                        def weigh(i):
                            b, h = its[i]
                            pe.wait_ge(pt_copied, i + 1)
                            if i >= 2:
                                pe.wait_ge(o_done, i - 1)
                            for j in range(6):
                                g, kb = (0, j) if j < 4 else (j - 3, b)
                                mm = pe.matmul(ps[:, 2 + i % 2, 0:HEAD], pT[:, i % 2, j * P:(j + 1) * P],
                                               vtok[:, kb, (4 * g + h) * HEAD:(4 * g + h + 1) * HEAD],
                                               start=(j == 0), stop=(j == 5))
                            mm.then_inc(pv_done, 1)
                            if h == SLOTS - 1:
                                return b
                            return None

                        def turn_out(b):
                            pe.wait_ge(o_done, 4 * (b + 1))
                            for j in range(2):
                                mm = pe.transpose(ps[:, 1, j * P:(j + 1) * P], otok[:, b % 2, j * P:(j + 1) * P], ident[:])
                            mm.then_inc(ot_done, 1)

                        score(0)
                        pending = None
                        for i in range(len(its)):
                            if i + 1 < len(its):
                                score(i + 1)
                            turn(i)
                            last_b = weigh(i)
                            if pending is not None:
                                turn_out(pending)
                            pending = last_b
                        turn_out(pending)
                        pe.wait_ge(ot_copied, 4)

                    for item in ORDER:
                        if item[0] == "tile":
                            tile(item)
                        elif item[0] == "pair":
                            pair_in(item[1])
                            if item[1]:
                                pair_out(item[1] - 1)
                        elif item[0] == "pairs_end":
                            pair_out(PAIRS - 1)
                        elif item[0] == "attention":
                            attention()
                        elif item[0] == "norm2":
                            for b in range(4):
                                done = len([i for i in range(TILE_NUMBER[("tile", "h_tok", 0, 0)]) if i % 4 == b])
                                pe.wait_ge(bank_free[b], done)
                            norm_mean(pe, 1)
                            pe.wait_ge(root_done, 2)

                @block.scalar
                def _(act):
                    norm_squares(act, 0)
                    norm_root(act, 0)
                    st = Steps(act, act_steps)
                    act.wait_ge(poles_angle, 1)
                    act.activation(small[:, 12, :], small[:, 4, :], ACT.Sin).then_inc(poles_sincos, 1)
                    act.activation(small[:, 13, :], small[:, 6, :], ACT.Sin).then_inc(poles_sincos, 1)
                    glu_n = gate_n = raw_n = 0
                    for item in ORDER:
                        kind = item[1] if item[0] == "tile" else item[0]
                        if item[0] == "tile":
                            n = TILE_NUMBER[item]
                            src = ps[:, n % 4, :]
                            free = bank_free[n % 4]
                        if kind in ("pool_u", "ssm_u"):
                            act.wait_ge(tiles_done, n + 1)
                            dst, ready = (pool_in, pool_in_ready) if kind == "pool_u" else (ssmT, ssm_in_ready)
                            st.step(act.copy(dst[:, item[2], :], src))
                            st.settle()
                            act.sem_inc(ready, 1)
                            act.sem_inc(free, 1)
                        elif kind in ("q", "k"):
                            act.wait_ge(tiles_done, n + 1)
                            if raw_n >= 2:
                                act.wait_ge(roped, raw_n - 1)
                            st.link(act.copy(raw[:, item[2] % 2, :], src))
                            act.sem_inc(raw_ready, 1)
                            act.sem_inc(free, 1)
                            raw_n += 1
                        elif kind == "v":
                            act.wait_ge(tiles_done, n + 1)
                            st.link(act.copy(vtok[:, item[3], 256 * item[2]:256 * item[2] + 256], src[:, 0:256]))
                            act.sem_inc(v_ready, 1)
                            act.sem_inc(free, 1)
                        elif kind == "pair" and item[1] == 0:
                            act.wait_ge(bbarT_done, 1)
                            for s in range(2):
                                act.copy(bbarT[:, s, :, :], ps[:, 4 + s, :].rearrange("p (m n) -> p m n", m=4)).then_inc(bbarT_ready, 1)
                        elif kind == "mix":
                            act.wait_ge(tiles_done, n + 1)
                            g = item[2]
                            st.link(act.activation(mixT[:, g, :], src, ACT.Copy, scale=vec[:, V_PSCALE + g:V_PSCALE + g + 1]))
                            act.sem_inc(mixed, 1)
                            act.sem_inc(free, 1)
                        elif kind == "pairs_end":
                            for m in range(4):
                                act.wait_ge(y_taken, m + 1)
                                act.activation(ssmT[:, m, :], ssmT[:, m, :], ACT.Gelu_apprx_tanh).then_inc(y_gelu, 1)
                        elif kind == "glu_gate":
                            act.wait_ge(tiles_done, n + 1)
                            if glu_n >= 2:
                                act.wait_ge(glu_ready, glu_n - 1)
                            st.link(act.activation(rope_t[:, glu_n % 2, :], src, ACT.Sigmoid))
                            act.sem_inc(glu_sig, 1)
                            act.sem_inc(free, 1)
                            glu_n += 1
                        elif kind == "gate":
                            act.wait_ge(tiles_done, n + 1)
                            if gate_n >= 2:
                                act.wait_ge(gate_used, gate_n - 1)
                            st.link(act.activation(sig[:, gate_n % 2, :], src, ACT.Sigmoid))
                            act.sem_inc(gate_sig, 1)
                            act.sem_inc(free, 1)
                            gate_n += 1
                        elif kind == "attention":
                            for i in range(16):
                                act.wait_ge(sc_max, i + 1)
                                act.activation(srow[:, i % 2, :], srow[:, i % 2, :], ACT.Exp, bias=stats[:, 16 + i:17 + i],
                                               scale=SCALE, accum_out=stats[:, 32 + i:33 + i]).then_inc(exp_done, 1)
                                act.wait_ge(pt_done, i + 1)
                                if i >= 2:
                                    act.wait_ge(pv_done, i - 1)
                                act.copy(pT[:, i % 2, :], ps[:, 0:2, :].rearrange("p a t -> p (a t)")[:, 0:KEYS]).then_inc(pt_copied, 1)
                        elif kind == "norm2":
                            act.wait_ge(x_mixed, KD)
                            norm_squares(act, 1)
                            norm_root(act, 1)
                        elif kind == "wq":
                            act.wait_ge(tiles_done, n + 1)
                            st.link(act.copy(qpT[:, item[2], :], src))
                            act.sem_inc(wq_copied, 1)
                            act.sem_inc(free, 1)
                        elif kind == "h_tok":
                            act.wait_ge(tiles_done, n + 1)
                            st.step(act.copy(h_tok[:, item[2], 512 * item[3]:512 * item[3] + 512], src))
                            st.settle()
                            act.sem_inc(free, 1)
                        elif kind == "score":
                            act.wait_ge(tiles_done, n + 1)
                            st.link(act.copy(scores[:, :, 2 * item[2] + item[3], :], src.rearrange("p (t k) -> p t k", t=NT)))
                            act.sem_inc(scores_ready, 1)
                            act.sem_inc(free, 1)
                    act.wait_ge(shifted, 1)
                    act.activation(gate_e, gate_e, ACT.Exp).then_inc(exp_ready, 1)

                @block.vector
                def _(dve):
                    st = Steps(dve, dve_steps)

                    def own_exp(x, out, k, r, q):
                        st.link(dve.tensor_scalar(k, x, 1 / math.log(2.0), ROUND, ALU.mult, ALU.add))
                        st.link(dve.tensor_scalar(k, k, -ROUND, -126.0, ALU.add, ALU.max))
                        st.link(dve.scalar_tensor_tensor(r, k, -LN2_HI, x, ALU.mult, ALU.add))
                        st.link(dve.scalar_tensor_tensor(r, k, -LN2_LO, r, ALU.mult, ALU.add))
                        st.link(dve.tensor_scalar(q, r, 1 / 5040.0, None, ALU.mult))
                        for c in (1 / 720.0, 1 / 120.0, 1 / 24.0, 1 / 6.0, 0.5, 1.0):
                            st.link(dve.scalar_tensor_tensor(q, q, c, r, ALU.add, ALU.mult))
                        st.link(dve.tensor_scalar(k.bitcast(I32), k, 127.0, 2.0 ** 23, ALU.add, ALU.mult))
                        st.link(dve.scalar_tensor_tensor(out, q, 1.0, k, ALU.add, ALU.mult))

                    def tt(out, a, b, op):
                        st.link(dve.tensor_tensor(out, a, b, op))

                    S = lambda i: small[:, i, :]
                    log_dt_, dt, x, decay, theta, kk, theta_c, tmp = (S(i) for i in range(8))
                    r_, q_ = S(8), S(9)
                    sin_, cos_ = S(12), S(13)
                    a_re, a_im = vec[:, V_ARE:V_ARE + PAIRS], vec[:, V_AIM:V_AIM + PAIRS]
                    ab_re, ab_im, den, k_re, k_im, nr = S(14), S(15), S(16), S(17), S(18), S(19)
                    dve.wait_ge(small_landed, 80)
                    own_exp(log_dt_, dt, kk, r_, q_)
                    tt(x, a_re, dt, ALU.mult)
                    own_exp(x, decay, kk, r_, q_)
                    tt(theta, a_im, dt, ALU.mult)
                    reduce_angle(dve, st, theta, kk, theta_c, tmp)
                    dve.sem_inc(poles_angle, 1)
                    norm_scale(dve, 0, vec[:, V_G1:V_G1 + KD], hT)
                    dve.wait_ge(poles_sincos, 2)
                    tt(ab_re, decay, cos_, ALU.mult)
                    tt(ab_im, decay, sin_, ALU.mult)
                    tt(den, a_re, a_re, ALU.mult)
                    tt(tmp, a_im, a_im, ALU.mult)
                    tt(den, den, tmp, ALU.add)
                    st.link(dve.reciprocal(den, den))
                    st.link(dve.tensor_scalar(nr, ab_re, -1.0, None, ALU.add))
                    tt(k_re, nr, a_re, ALU.mult)
                    tt(tmp, ab_im, a_im, ALU.mult)
                    tt(k_re, k_re, tmp, ALU.add)
                    tt(k_re, k_re, den, ALU.mult)
                    tt(k_im, ab_im, a_re, ALU.mult)
                    tt(tmp, nr, a_im, ALU.mult)
                    tt(k_im, k_im, tmp, ALU.subtract)
                    tt(k_im, k_im, den, ALU.mult)
                    st.step(dve.tensor_copy(S(30), cos_))
                    st.link(dve.tensor_copy(S(31), sin_))
                    dve.sem_inc(poles_ready, 1)
                    dve.wait_ge(blocks_ready, 1)
                    wide = lambda v: v.unsqueeze(2).broadcast_to([P, PAIRS, 32])
                    tt(bbar[:, 0, :, :], b_blocks[:, 0, :, :], wide(k_re), ALU.mult)
                    tt(bb_tmp[:, 0, :, :], b_blocks[:, 1, :, :], wide(k_im), ALU.mult)
                    tt(bbar[:, 0, :, :], bbar[:, 0, :, :], bb_tmp[:, 0, :, :], ALU.subtract)
                    tt(bbar[:, 1, :, :], b_blocks[:, 1, :, :], wide(k_re), ALU.mult)
                    tt(bb_tmp[:, 0, :, :], b_blocks[:, 0, :, :], wide(k_im), ALU.mult)
                    tt(bbar[:, 1, :, :], bbar[:, 1, :, :], bb_tmp[:, 0, :, :], ALU.add)
                    dve.sem_inc(bbar_ready, 1)

                    def pair(p):
                        cs, sn = tabs[:, p % 2, 0, :], tabs[:, p % 2, 1, :]
                        xr, xi = ps[:, 4, :], ps[:, 5, :]
                        m1, m2, m3, m4 = (rotin[:, i, :] for i in range(4))
                        dve.wait_ge(tab_ready, p + 1)
                        dve.wait_ge(x_done, p + 1)
                        dve.tensor_tensor(m1, xr, cs, ALU.mult)
                        dve.tensor_tensor(m2, xi, sn, ALU.mult)
                        dve.tensor_tensor(m3, xi, cs, ALU.mult)
                        dve.tensor_tensor(m4, xr, sn, ALU.mult).then_inc(x_free, 1)
                        dve.wait_ge(x_free, p + 1)
                        st.step(dve.tensor_tensor(m1, m1, m2, ALU.add))
                        st.step(dve.tensor_tensor(m3, m3, m4, ALU.subtract))
                        if p >= 2:
                            dve.wait_ge(prod_pool, p - 1)
                        st.settle()
                        rate = decay[:, p:p + 1].broadcast_to([P, L])
                        for s, v in enumerate((m1, m3)):
                            dve.tensor_tensor_scan(scanned[:, p % 2, s, :], rate, v, 0.0, ALU.mult, ALU.add).then_inc(scan_done, 1)
                        dve.wait_ge(scan_done, 2 * (p + 1))
                        if p:
                            dve.wait_ge(y_done, p)
                        dve.tensor_tensor(prods[0], scanned[:, p % 2, 0, :], cs, ALU.mult).then_inc(prod_dve, 1)
                        dve.tensor_tensor(prods[1], scanned[:, p % 2, 1, :], sn, ALU.mult).then_inc(prod_dve, 1)

                    def take_y(m):
                        dve.wait_ge(y_done, PER_TILE * (m + 1))
                        dve.scalar_tensor_tensor(ssmT[:, m, :], ssmT[:, m, :], vec[:, V_D + m:V_D + m + 1], ps[:, 6 + m % 2, :],
                                                 ALU.mult, ALU.add).then_inc(y_taken, 1)

                    rope_n = glu_n = gate_n = 0
                    for item in ORDER:
                        kind = item[1] if item[0] == "tile" else item[0]
                        if item[0] == "tile":
                            n = TILE_NUMBER[item]
                            src = ps[:, n % 4, :]
                            free = bank_free[n % 4]
                        if kind in ("qswap", "kswap"):
                            dst = (qT if kind == "qswap" else kT)[:, item[2], :]
                            dve.wait_ge(raw_ready, rope_n + 1)
                            st.step(dve.tensor_tensor(rope_t[:, 0, :], raw[:, item[2] % 2, :], cosT[:], ALU.mult))
                            dve.wait_ge(tiles_done, n + 1)
                            st.link(dve.tensor_tensor(rope_t[:, 1, :], src, sinT[:], ALU.mult))
                            dve.sem_inc(free, 1)
                            dve.tensor_tensor(dst, rope_t[:, 0, :], rope_t[:, 1, :], ALU.add).then_inc(roped, 1)
                            rope_n += 1
                            dve.wait_ge(roped, rope_n)
                        elif kind == "pair":
                            pair(item[1])
                            if item[1] and item[1] % PER_TILE == 0:
                                take_y(item[1] // PER_TILE - 1)
                        elif kind == "pairs_end":
                            take_y(3)
                        elif kind == "glu_val":
                            dve.wait_ge(tiles_done, n + 1)
                            dve.wait_ge(glu_sig, glu_n + 1)
                            dve.tensor_tensor(gluT[:, item[2], :], src, rope_t[:, glu_n % 2, :], ALU.mult).then_inc(glu_ready, 1)
                            glu_n += 1
                            dve.wait_ge(glu_ready, glu_n)
                            dve.sem_inc(free, 1)
                        elif kind == "attention":
                            for i in range(16):
                                b, h = i // SLOTS, i % SLOTS
                                bank = 4 + 2 * (i % 2)
                                dve.wait_ge(sc_done, i + 1)
                                if i >= 2:
                                    dve.wait_ge(pt_done, i - 1)
                                st.link(dve.tensor_tensor_reduce(
                                    srow[:, i % 2, :], ps[:, bank:bank + 2, :].rearrange("p a t -> p (a t)")[:, 0:KEYS],
                                    mask[:, b, :], 1.0, LOWEST, ALU.add, ALU.max, stats[:, i:i + 1]))
                                dve.tensor_scalar(stats[:, 16 + i:17 + i], stats[:, i:i + 1], -SCALE, None, ALU.mult).then_inc(sc_max, 1)
                                if i:
                                    attend_out(dve, st, i - 1)
                            attend_out(dve, st, 15)
                        elif kind == "gate":
                            m, b = item[2], item[3]
                            ny = TILE_NUMBER[("tile", "branch", m, b)]
                            y = ps[:, ny % 4, :]
                            dve.wait_ge(tiles_done, ny + 1)
                            dve.wait_ge(gate_sig, gate_n + 1)
                            if b == 0:
                                dve.tensor_tensor(merged[:, m, :], y, sig[:, gate_n % 2, :], ALU.mult).then_inc(gate_used, 1)
                            else:
                                st.link(dve.tensor_tensor(gated[:, 0, :], y, sig[:, gate_n % 2, :], ALU.mult))
                                dve.wait_ge(gate_used, gate_n)
                                dve.tensor_tensor(merged[:, m, :], merged[:, m, :], gated[:, 0, :], ALU.add).then_inc(gate_used, 1)
                            gate_n += 1
                            dve.wait_ge(gate_used, gate_n)
                            dve.sem_inc(bank_free[ny % 4], 1)
                        elif kind == "out":
                            dve.wait_ge(tiles_done, n + 1)
                            dve.tensor_tensor(xT[:, item[2], :], xT[:, item[2], :], src, ALU.add).then_inc(x_mixed, 1)
                            dve.wait_ge(x_mixed, item[2] + 1)
                            dve.sem_inc(free, 1)
                        elif kind == "norm2":
                            norm_scale(dve, 1, vec[:, V_G2:V_G2 + KD], hT)
                            dve.sem_inc(list_steps, 1)
                            dve.sem_inc(head_steps, 1)
                            dve.sem_inc(pick_steps, 1)
                        elif kind == "score":
                            j = 2 * item[2] + item[3]
                            dve.wait_ge(scores_ready, j + 1)
                            for _ in pick_list(dve, 0, j):
                                pass
                            if item[3]:
                                for _ in pick_head(dve, 0, item[2]):
                                    pass
                    settle_picks(dve, 0)

        poles_angle = sem("poles_angle")
        poles_sincos = sem("poles_sincos")
        freed = [sem(f"row_free{j}") for j in range(NB)]
        picks_ready = sem("picks_ready")
        exp_ready = sem("exp_ready")
        shifted = sem("shifted")
        peer_dve = sem("peer_dve")
        idx_staged = sem("idx_staged")
        act_copied = sem("act_copied")
        acts_ready = sem("acts_ready")
        gelu_ready = sem("gelu_ready")
        w_ready = sem("w_ready")
        w_staged = sem("w_staged")
        diag_ready = sem("diag_ready")
        acc_open = sem("acc_open")
        acc_done = sem("acc_done")
        acc_free = sem("acc_free")
        back_done = sem("back_done")
        back_taken = sem("back_taken")
        h_copied = sem("h_copied")
        zeroed = sem("zeroed")
        list_steps = sem("list_steps")
        head_steps = sem("head_steps")
        pick_steps = sem("pick_steps")
        scores_ready = sem("scores_ready")
        sum_cleared = sem("sum_cleared")
        sum_ready = sem("sum_ready")
        sum_read = sem("sum_read")
        pool_turn = sem("pool_turn")
        dve_turn = sem("dve_turn")

        def peer(layer):
            with nc.Block() as block:
                @block.gpsimd
                def _(pool):
                    for j in range(NB):
                        pool.sem_inc(freed[j], 1)
                    with pool.Fori(0, NT) as t:
                        pool.wait_ge(picks_ready, t + 1)
                        pool.sem_inc(pool_turn, 1)
                        for half, table in enumerate((table_u, table_v)):
                            with pool.Fori(0, ROUNDS // 2) as i2:
                                for par in range(2):
                                    rnd = t * (2 * ROUNDS) + half * ROUNDS + i2 * 2 + par
                                    stage = idx_stage[:, par, :]
                                    for j in range(NB):
                                        pool.wait_ge(freed[j], rnd + 1)
                                        if j == 0:
                                            pool.tensor_copy(stage, expert[
                                                :, bass.ds(t * PICKS + (i2 * 2 + par) * NB, NB)]).then_inc(idx_staged, 1)
                                            pool.wait_ge(idx_staged, rnd + 1)
                                        pool.sem_inc(pool_turn, 1)
                                        pool.indirect_dma_start(rows[:, j, :], None, table,
                                                                bass.IndirectOffsetOnAxis(stage[:, j:j + 1], 0)).then_inc(land[j], 16)

                @block.vector
                def _(dve):
                    dve.memset(zeros, 0.0).then_inc(zeroed, 1)
                    def work(t, nxt):
                        dve.tensor_copy(h_now, h_tok.rearrange("p t d -> p (t d)")[:, bass.ds(t * D, D)]).then_inc(h_copied, 1)
                        dve.wait_ge(h_copied, t + 1)
                        dve.sem_inc(dve_turn, 1)
                        with dve.Fori(0, ROUNDS) as i:
                            rnd = t * (2 * ROUNDS) + i
                            picks = pick_list(dve, nxt, i) if nxt is not None else iter(())
                            for j in range(NB):
                                dve.wait_ge(land[j], (layer * (NT * 2 * ROUNDS) + rnd) * 16 + 16)
                                dve.tensor_tensor_reduce(rows[:, j, :], rows[:, j, :], h_now, 1.0, 0.0, ALU.mult, ALU.add,
                                                         act_stage[:, j:j + 1]).then_inc(freed[j], 1)
                                next(picks, None)
                            assert next(picks, None) is None
                            dve.wait_ge(freed[NB - 1], rnd + 2)
                            dve.tensor_copy(act_all[:, bass.ts(i, NB)], act_stage).then_inc(act_copied, 1)
                            dve.wait_ge(act_copied, t * ROUNDS + i + 1)
                        dve.sem_inc(acts_ready, 1)
                        dve.wait_ge(gelu_ready, t + 1)
                        dve.tensor_tensor(w_all, gelu_all, gates[:, bass.ds(t * PICKS, PICKS)], ALU.mult).then_inc(w_ready, 1)
                        dve.wait_ge(w_ready, t + 1)
                        dve.sem_inc(dve_turn, 1)
                        dve.wait_ge(sum_read, t + 1)
                        dve.sem_inc(dve_turn, 1)
                        dve.memset(dve_sum, 0.0).then_inc(sum_cleared, 1)
                        dve.wait_ge(sum_cleared, t + 1)
                        dve.sem_inc(dve_turn, 1)
                        with dve.Fori(0, PH) as h:
                            picks = pick_head(dve, nxt, h) if nxt is not None else iter(())
                            for part in range(ROUNDS // PH):
                                i = h * (ROUNDS // PH) + part
                                rnd = t * (2 * ROUNDS) + ROUNDS + i
                                dve.tensor_copy(w_stage, w_all[:, bass.ds(i * NB, NB)]).then_inc(w_staged, 1)
                                dve.wait_ge(w_staged, t * ROUNDS + i + 1)
                                for j in PE_SLOTS:
                                    dve.wait_ge(freed[j], rnd + 1)
                                    dve.tensor_scalar(diag[:, j, :], ident[:], w_stage[:, j:j + 1], None,
                                                      ALU.mult).then_inc(diag_ready, 1)
                                for n, j in enumerate(DVE_SLOTS):
                                    for _ in range(4):
                                        next(picks, None)
                                    dve.wait_ge(freed[DVE_SLOTS[n - 1]], rnd + (2 if n else 1))
                                    dve.wait_ge(land[j], (layer * (NT * 2 * ROUNDS) + rnd) * 16 + 16)
                                    dve.scalar_tensor_tensor(dve_sum, rows[:, j, :], w_stage[:, j:j + 1], dve_sum,
                                                             ALU.mult, ALU.add).then_inc(freed[j], 1)
                                dve.wait_ge(freed[DVE_SLOTS[-1]], rnd + 2)
                                dve.wait_ge(diag_ready, (t * ROUNDS + i) * len(PE_SLOTS) + len(PE_SLOTS))
                            assert next(picks, None) is None
                        dve.sem_inc(sum_ready, 1)
                        if nxt is not None:
                            settle_picks(dve, nxt)

                    with dve.Fori(0, NT - 1) as t:
                        work(t, t + 1)
                    work(NT - 1, None)
                    dve.tensor_scalar(layer_base[:], layer_base[:], float(EXPERTS), None, ALU.add)
                    for t in range(NT):
                        for half in range(2):
                            n = 2 * t + half
                            dve.wait_ge(back_done, n + 1)
                            dst = xT[:, 4 * half:4 * half + 4, t * P:(t + 1) * P]
                            dve.tensor_tensor(dst, dst, ps[:, n % 4, :].rearrange("p (k c) -> p k c", k=4),
                                              ALU.add).then_inc(back_taken, 1)

                @block.scalar
                def _(act):
                    act.sem_inc(acc_free, 1)

                    def work(t, nxt):
                        act.wait_ge(acts_ready, t + 1)
                        act.activation(gelu_all, act_all, ACT.Gelu_apprx_tanh).then_inc(gelu_ready, 1)
                        if nxt is not None:
                            act.wait_ge(shifted, nxt + 1)
                            act.activation(gate_e, gate_e, ACT.Exp).then_inc(exp_ready, 1)
                        act.wait_ge(acc_done, t + 1)
                        act.copy(out_tok.rearrange("p t d -> p (t d)")[:, bass.ds(t * D, D)],
                                 ps[:, 4:6, :].rearrange("p a t -> p (a t)")).then_inc(acc_free, 1)

                    with act.Fori(0, NT - 1) as t:
                        work(t, t + 1)
                    work(NT - 1, None)

                @block.tensor
                def _(pe):
                    pe.wait_ge(zeroed, 1)
                    pe.sem_inc(sum_read, 1)
                    with pe.Fori(0, NT) as t:
                        pe.wait_ge(acc_free, t + 1)
                        for half in range(2):
                            pe.matmul(ps[:, 4 + half, :], zeros, cosT[:], start=True, stop=False)
                        with pe.Fori(0, ROUNDS) as i:
                            rnd = t * (2 * ROUNDS) + ROUNDS + i
                            for n, j in enumerate(PE_SLOTS):
                                pe.wait_ge(diag_ready, (t * ROUNDS + i) * len(PE_SLOTS) + n + 1)
                                pe.wait_ge(land[j], (layer * (NT * 2 * ROUNDS) + rnd) * 16 + 16)
                                for half in range(2):
                                    mm = pe.matmul(ps[:, 4 + half, :], diag[:, j, :], rows[:, j, half * L:(half + 1) * L],
                                                   start=False, stop=False)
                                mm.then_inc(freed[j], 1)
                        pe.wait_ge(sum_ready, t + 1)
                        for half in range(2):
                            mm = pe.matmul(ps[:, 4 + half, :], ident[:], dve_sum[:, half * L:(half + 1) * L], start=False, stop=True)
                        mm.then_inc(sum_read, 1)
                        pe.wait_ge(sum_read, t + 2)
                        pe.sem_inc(acc_done, 1)
                    pe.wait_ge(acc_free, NT + 1)
                    for t in range(NT):
                        for half in range(2):
                            n = 2 * t + half
                            if n >= 4:
                                pe.wait_ge(back_taken, n - 3)
                            for k in range(4):
                                c = 4 * half + k
                                mm = pe.transpose(ps[:, n % 4, k * P:(k + 1) * P], out_tok[:, t, c * P:(c + 1) * P], ident[:])
                            mm.then_inc(back_done, 1)

        nc.all_engine_barrier(sems_to_clear=range(min(s.num for s in sems), max(s.num for s in sems) + 1))
        with nc.Fori(0, DEPTH) as layer:
            mixer(layer)
            peer(layer)
            nc.all_engine_barrier(sems_to_clear=range(min(s.num for s in sems), max(s.num for s in sems) + 1))

        with nc.Block() as block:
            @block.scalar
            def _(act):
                norm_squares(act, 0)
                norm_root(act, 0)

            @block.tensor
            def _(pe):
                norm_mean(pe, 0)

            @block.vector
            def _(dve):
                dve.wait_ge(small_landed, 16)
                norm_scale(dve, 0, fing, hT)

            @block.sync
            def _(sp):
                sp.dma_start(fing, final_g).then_inc(small_landed, 16)
                sp.wait_ge(normed, KD + 1)
                sp.dma_start(out_cm, hT[:].rearrange("p a t -> p (a t)")).then_inc(out_stored, 16)
                sp.wait_ge(out_stored, 16)


def pack_weights(w_in, pool_w, pool_proj, ssm_glu, ssm_proj, attn_proj, w_out, peer_wq):
    def blocks(w, cols):
        part = w[:, cols]
        return part.reshape(-1, P, part.shape[1]).transpose(1, 0, 2).reshape(P, -1)

    out = np.zeros((DEPTH, CHUNKS, P, CHUNK), w_in.dtype)
    for l in range(DEPTH):
        put = lambda c, a: out[l, c, :, :a.shape[1]].__setitem__(slice(None), a)
        for c in range(13):
            put(c, blocks(w_in[l], slice(256 * c, 256 * c + 256)))
        put(C_MIX, pool_w[l].transpose(1, 0, 2).reshape(P, -1))
        for i in range(2):
            cols = np.r_[256 * i:256 * i + 256, 512 + 256 * i:512 + 256 * i + 256]
            put(C_GLU + i, blocks(ssm_glu[l], cols))
        for m in range(KD):
            col = slice(P * m, P * m + P)
            parts = []
            for b, w in enumerate((pool_proj[l], ssm_proj[l], attn_proj[l])):
                at = W_IN_MAIN + D * b + P * m
                parts += [blocks(w, col), blocks(w_in[l], slice(at, at + P))]
            both = np.concatenate(parts, axis=1)
            put(C_MERGE + 2 * m, both[:, :CHUNK])
            put(C_MERGE + 2 * m + 1, both[:, CHUNK:])
        for c in range(4):
            put(C_OUT + c, blocks(w_out[l], slice(256 * c, 256 * c + 256)))
        for c in range(8):
            put(C_WQ + c, blocks(peer_wq[l], slice(256 * c, 256 * c + 256)))
    return out.reshape(DEPTH * CHUNKS * P, CHUNK)


def kernel(x, positions, norm1_g, w_in, pool_w, pool_scale, pool_proj, ssm_a_re, ssm_a_im, ssm_log_dt,
           ssm_b_re, ssm_b_im, ssm_c_re, ssm_c_im, ssm_d, ssm_glu, ssm_proj, attn_proj, w_out, norm2_g,
           peer_wq, peer_k1, peer_k2, peer_u, peer_v, final_g):
    import concourse.bacc as bacc
    from concourse.bass_utils import run_bass_kernel_spmd

    a = {k: np.asarray(v) for k, v in locals().items() if k not in ("bacc", "run_bass_kernel_spmd")}
    columns = lambda v: v.reshape(DEPTH, -1, P).transpose(0, 2, 1)
    states = lambda v: v.reshape(DEPTH, PAIRS, 2 * 64).transpose(0, 2, 1)
    b_lay = lambda v: v.reshape(DEPTH, PAIRS, 2 * 64, 16).transpose(0, 2, 1, 3).reshape(DEPTH, P, -1)
    c_lay = lambda v: v.reshape(DEPTH, PAIRS, 2, 16, 64).transpose(0, 2, 4, 1, 3).reshape(DEPTH, P, -1)
    arrays = {
        "x_cm": a["x"][0].reshape(L, KD, P).transpose(2, 1, 0).reshape(P, KD * L),
        "positions": a["positions"].astype(np.int32).reshape(1, L),
        "inv_freq": np.tile(np.power(np.float32(10000.0), -np.arange(32, dtype=np.float32) / np.float32(32)), 4)
                      .astype(np.float32).reshape(P, 1),
        "weights": pack_weights(*(a[n] for n in ("w_in", "pool_w", "pool_proj", "ssm_glu", "ssm_proj", "attn_proj",
                                                 "w_out", "peer_wq"))),
        "keys": np.concatenate([a["peer_k1"].transpose(0, 2, 1), a["peer_k2"].transpose(0, 2, 1)], axis=2)
                  .reshape(DEPTH * P, 2 * NKEYS),
        "vecs": np.concatenate([columns(a["norm1_g"]), columns(a["norm2_g"]), columns(a["pool_scale"]), columns(a["ssm_d"]),
                                states(a["ssm_a_re"]), states(a["ssm_a_im"])], axis=2).reshape(DEPTH * P, V_END),
        "log_dt": a["ssm_log_dt"].reshape(DEPTH, PAIRS, 2).transpose(0, 2, 1).reshape(DEPTH * 2, PAIRS),
        "ssm_bc": np.concatenate([b_lay(a["ssm_b_re"]), b_lay(a["ssm_b_im"]), c_lay(a["ssm_c_re"]), c_lay(a["ssm_c_im"])],
                                 axis=2).reshape(DEPTH * P, -1),
        "table_u": a["peer_u"].reshape(DEPTH * EXPERTS, D),
        "table_v": a["peer_v"].reshape(DEPTH * EXPERTS, D),
        "final_g": a["final_g"].reshape(KD, P).T,
    }
    arrays = {k: np.ascontiguousarray(v) for k, v in arrays.items()}
    nc = bacc.Bacc("TRN2", target_bir_lowering=False, num_devices=1)
    args = [nc.dram_tensor(k, v.shape, mybir.dt.from_np(v.dtype), kind="ExternalInput").ap() for k, v in arrays.items()]
    args.append(nc.dram_tensor("out_cm", (P, KD * L), F32, kind="ExternalOutput").ap())
    trunk(nc, *args)
    r = run_bass_kernel_spmd(nc, [arrays], core_ids=[0])
    out = r.results[0]["out_cm"].reshape(P, KD, L).transpose(2, 1, 0).reshape(1, L, D)
    return np.ascontiguousarray(out)
```

```python
import math
from contextlib import ExitStack

import numpy as np

import concourse.bass as bass
from concourse import mybir

F32 = mybir.dt.float32
I32 = mybir.dt.int32
U32 = mybir.dt.uint32
ALU = mybir.AluOpType
ACT = mybir.ActivationFunctionType
AX = mybir.AxisListType

P = 128
L = 512
D = 1024
DEPTH = 2
KD = D // P
NT = L // P
EPS = 1e-6

POOL_WINDOWS = (2, 4, 8, 16)
PAIRS = 16
PER_TILE = 4
HEAD = 64
SLOTS = 4
KEYS = L + 2 * P
SCALE = HEAD ** -0.5
NEG = -1e30
LOWEST = -3.0e38

W_IN_MAIN = 3328
CHUNK = 17 * P
RING = 4
C_POOL, C_SSM, C_Q, C_K, C_V, C_MIX, C_GLU, C_MERGE, C_OUT, C_WQ, CHUNKS = 0, 2, 4, 7, 10, 13, 14, 16, 32, 36, 44
SIDE_HEADS = 4
C_SIDE = CHUNKS - SIDE_HEADS
LATER_WQ = 2 * SIDE_HEADS - 2

PH = 8
TOPK = 16
NKEYS = 128
EXPERTS = NKEYS * NKEYS
PICKS = PH * TOPK
NB = 8
ROUNDS = PICKS // NB
LATE_ROWS = (NB - 2, NB - 1)
PE_SLOTS, DVE_SLOTS = (0, 1, 3, 4, 6, 7), (2, 5)
FIRST_STEPS, LIST_STEPS, HEAD_STEPS, PICK_STEPS = 11, 8, 13, 4

V_G1, V_G2, V_PSCALE, V_D, V_ARE, V_AIM, V_END = 0, 8, 16, 20, 24, 40, 56

TWO_PI_HI = 6.28125
TWO_PI_MID = 0.0019350051879882812
TWO_PI_LO = 2 * math.pi - TWO_PI_HI - TWO_PI_MID
ROUND = 1.5 * 2.0 ** 23
PI_SAFE = 3.1415925
LN2_HI = 0.693359375
MEAN_BANK = 7
LN2_LO = math.log(2.0) - LN2_HI


class Steps:

    def __init__(self, eng, sem):
        self.eng, self.sem, self.n = eng, sem, 0

    def step(self, ins):
        ins.then_inc(self.sem, 1)
        self.n += 1

    def settle(self):
        self.eng.wait_ge(self.sem, self.n)

    def link(self, ins):
        self.step(ins)
        self.settle()


def mixer_order():
    head = [("tile", "pool_u", m) for m in range(4)] + [("tile", "ssm_u", m) for m in range(4)]
    dense = []
    for which in ("q", "k"):
        for m in range(6):
            dense.append(("tile", which, m))
            if m:
                dense.append(("rope", which, m - 1))
        dense.append(("rope", which, 5))
    dense += [("tile", "v", c, b) for c in range(3) for b in range(NT)]
    dense += [("tile", "mix", g) for g in range(4)]
    out, pair = list(head), 0
    for n, item in enumerate(dense):
        out.append(item)
        if out[-2] == ("pair", pair - 1) and pair > 1:
            out.append(("pair_out", pair - 2))
        if pair < PAIRS and n % 2 == 0:
            out.append(("pair", pair))
            pair += 1
    out += [("pair", p) for p in range(pair, PAIRS)]
    out += [("pair_out", PAIRS - 1), ("pairs_end",), ("attention_start",)]
    for i in range(2):
        for j in range(2):
            out += [("tile", "glu_gate", 2 * i + j), ("tile", "glu_val", 2 * i + j)]
    out.append(("attention",))
    for m in range(KD):
        for b in range(3):
            out += [("tile", "branch", m, b), ("tile", "gate", m, b)]
    for m in range(KD):
        out += [("tile", "out", m)] + ([("mean", m - 1)] if m else [])
    out += [("mean", KD - 1), ("norm2",)]
    rest = 0
    for h in range(PH + 1):
        out += [("tile", "first_wq", h)] if h < PH else []
        out += [("tile", "h_tok", 0, half) for half in range(2)] if h == 1 else []
        out += [("tile", "first_score", h - 1)] if h else []
        if h in (2, 5, 7, 8):
            out += [("tile", "wq", rest)] + ([("tile", "score", rest - 1)] if rest else [])
            rest += 1
    while rest < LATER_WQ:
        out += [("tile", "wq", rest), ("tile", "score", rest - 1)]
        rest += 1
    out.append(("tile", "score", rest - 1))
    return out


def rest_order():
    out = []
    for j in range(LATER_WQ, 2 * PH):
        out.append(("tile", "wq", j))
        if j > LATER_WQ:
            out.append(("tile", "score", j - 1))
        if j == 2 * SIDE_HEADS - 1:
            out.append(("side_read",))
            out += [("tile", "h_tok", t, half) for t in range(1, NT) for half in range(2)]
    return out + [("tile", "score", 2 * PH - 1)]


ORDER = mixer_order()
REST_ORDER = rest_order()
TILES = [item for item in ORDER + REST_ORDER if item[0] == "tile"]
TILE_NUMBER = {item: n for n, item in enumerate(TILES)}
BRANCH_START = {(0, 0): 0, (0, 1): 4, (1, 0): 12, (1, 1): 16, (2, 0): 24, (2, 1): 26}
BRANCH_K = {0: 4, 1: 4, 2: 2}
QUERY_KINDS = ("h_tok", "first_wq", "first_score", "wq", "score")


def chunk_last_tile():
    last = {}
    for item in TILES:
        n, kind = TILE_NUMBER[item], item[1]
        first = {"pool_u": C_POOL, "ssm_u": C_SSM, "q": C_Q, "k": C_K, "out": C_OUT}.get(kind)
        if first is not None:
            last[first + item[2] // 2] = n
        elif kind == "v":
            last[C_V + item[2]] = n
        elif kind == "mix":
            last[C_MIX] = n
        elif kind in ("glu_gate", "glu_val"):
            last[C_GLU + item[2] // 2] = n
        elif kind in ("branch", "gate"):
            m, b = item[2], item[3]
            at = BRANCH_START[(b, kind == "gate")]
            end = at + (8 if kind == "gate" else BRANCH_K[b]) - 1
            for j in {at // 17, end // 17}:
                last[C_MERGE + 2 * m + j] = n
    return last


CHUNK_LAST_TILE = chunk_last_tile()


def trunk(nc, x_cm, positions, inv_freq, weights, keys, vecs, log_dt, ssm_bc, table_u, table_v, final_g, out_cm):
    with ExitStack() as ctx:
        def sb(name, shape, dt=F32):
            return ctx.enter_context(nc.sbuf_tensor(name, shape, dt))

        sems = []
        land = [ctx.enter_context(nc.semaphore(f"row_landed{j}")) for j in range(NB)]

        def sem(name):
            s = ctx.enter_context(nc.semaphore(name))
            sems.append(s)
            return s

        xT = sb("xT", [P, KD, L])
        hT = sb("hT", [P, KD, L])
        wring = sb("wring", [P, RING, CHUNK])
        cosT = sb("cosT", [P, L])
        sinT = sb("sinT", [P, L])
        mask = sb("mask", [P, NT, KEYS])
        ident = sb("ident", [P, P])
        mean_ones = sb("mean_ones", [P, P])
        vec = sb("vec", [P, V_END])
        keysT = sb("keysT", [P, 2 * NKEYS])
        eps = sb("eps", [P, 1])
        layer_base = sb("layer_base", [P, 1])
        iota16 = sb("iota16", [P, TOPK])

        ARENA = 31488
        arena = sb("arena", [P, ARENA])

        def carve(at, n):
            assert at + n <= ARENA, (at, n)
            return arena[:, at:at + n]

        qT = carve(0, 3072).rearrange("p (m t) -> p m t", t=L)
        kT = carve(3072, 3072).rearrange("p (m t) -> p m t", t=L)
        vtok = carve(6144, 3072).rearrange("p (b c) -> p b c", b=NT)
        merged = carve(0, 4096).rearrange("p (m t) -> p m t", t=L)
        pool_in = carve(9216, 2048).rearrange("p (g t) -> p g t", t=L)
        pool_sum = carve(11264, 2048).rearrange("p (g t) -> p g t", t=L)
        mixT = pool_sum
        gluT = pool_in
        ssmT = carve(13312, 2048).rearrange("p (m t) -> p m t", t=L)
        pool_scratch = carve(15360, 1024).rearrange("p (i t) -> p i t", t=L)
        attnT = carve(27392, 1024).rearrange("p (m t) -> p m t", t=L)
        bbarT = carve(16384, 1024).rearrange("p (s m n) -> p s m n", s=2, m=4)
        c_blocks = carve(17408, 1024).rearrange("p (s g c) -> p s g c", s=2, g=PAIRS)
        pow_b = carve(18944, 1024).rearrange("p (s g t) -> p s g t", s=2, g=PAIRS)
        pow_a = carve(19968, 512).rearrange("p (s g t) -> p s g t", s=2, g=PAIRS)
        small = carve(20480, 544).rearrange("p (i g) -> p i g", g=PAIRS)
        raw = carve(21248, 1024).rearrange("p (i t) -> p i t", t=L)
        swapped = carve(22272, 1024).rearrange("p (i t) -> p i t", t=L)
        glu_sigmoid = swapped
        tabs = carve(23296, 2048).rearrange("p (i s t) -> p i s t", i=2, s=2)
        rotin = carve(25344, 2048).rearrange("p (s t) -> p s t", t=L)
        scanned = carve(27392, 2048).rearrange("p (i s t) -> p i s t", i=2, s=2)
        prods = [carve(29440 + i * L, L) for i in range(4)]
        pow_tmp = carve(25344, 1024).rearrange("p (s g t) -> p s g t", s=2, g=PAIRS)
        pow_tmp_a = carve(26368, 256).rearrange("p (s g t) -> p s g t", s=2, g=PAIRS)
        bc_in = carve(23296, 1024).rearrange("p (s g c) -> p s g c", s=4, g=PAIRS)
        b_blocks = carve(27392, 1024).rearrange("p (s g c) -> p s g c", s=2, g=PAIRS)
        bbar = carve(28416, 1024).rearrange("p (s g c) -> p s g c", s=2, g=PAIRS)
        bb_tmp = carve(24320, 1024).rearrange("p (s g c) -> p s g c", s=2, g=PAIRS)
        srow = carve(23296, 1536).rearrange("p (i k) -> p i k", i=2)
        pT = carve(24832, 1536).rearrange("p (i k) -> p i k", i=2)
        otok = carve(26368, 512).rearrange("p (i c) -> p i c", i=2)
        stats = carve(26880, 64)
        sig = carve(23296, 1024).rearrange("p (i t) -> p i t", t=L)
        gated = carve(24320, 1024).rearrange("p (i t) -> p i t", t=L)
        rms = carve(30000, L)
        rstd = carve(30512, L)
        scores_flat = carve(0, 8192)
        scores = carve(0, 8192).rearrange("p (t j k) -> p t j k", t=NT, j=16)
        out_tok = hT[:].rearrange("p a t -> p (a t)").rearrange("p (t d) -> p t d", t=NT)
        side_w = carve(8192, SIDE_HEADS * 2 * KD * P).rearrange("p (h w) -> p h w", h=SIDE_HEADS)
        rows = carve(8192, NB * D).rearrange("p (j d) -> p j d", d=D)
        first_q = carve(20480, 2048).rearrange("p (h s t) -> p h s t", h=PH, s=2)
        h_tok = carve(16384, 4096).rearrange("p (t d) -> p t d", t=NT)
        diag = carve(20480, NB * P).rearrange("p (j c) -> p j c", c=P)
        h_now = carve(21504, D)
        topv = carve(22528, 256)
        topif = carve(22784, 256)
        first_left = carve(23040, 2 * NKEYS).rearrange("p (s k) -> p s k", s=2)
        first_i = carve(23296, 2 * TOPK).bitcast(U32)
        list_in = carve(23040, NKEYS)
        list_left = carve(23168, NKEYS)
        list_v = carve(23296, TOPK)
        list_i = carve(23312, TOPK).bitcast(U32)
        cand = carve(23328, TOPK * TOPK)
        cand_left = carve(23584, TOPK * TOPK)
        cand_v = carve(23840, TOPK)
        cand_p = carve(23856, TOPK).bitcast(U32)
        place_u = carve(23872, 2 * TOPK).bitcast(U32).rearrange("p (s k) -> p s k", s=2)
        place_f = carve(23904, 2 * TOPK)
        onehot = carve(23936, 2 * TOPK * TOPK)
        head_s = carve(24448, PICKS)
        head_k = carve(24576, 2 * PICKS)
        expert_f = carve(24832, PICKS)
        gate_e = carve(24960, PICKS)
        gate_s = carve(25088, 2 * PH)
        expert = carve(25600, NT * PICKS).bitcast(U32)
        gates = carve(26112, NT * PICKS)
        act_all = carve(26752, PICKS)
        gelu_all = carve(26880, PICKS)
        w_all = carve(27008, PICKS)
        act_stage = carve(27136, NB)
        w_stage = carve(27144, NB)
        idx_stage = carve(27152, 2 * NB).bitcast(U32).rearrange("p (i n) -> p i n", i=2)
        zeros = carve(27168, P)
        fing = carve(27296, KD)
        dve_sum = carve(27304, D)
        rest_q = carve(28328, 4 * (L - P)).rearrange("p (j t) -> p j t", j=4)

        ps = ctx.enter_context(nc.psum_tensor("ps", [P, 8, L], F32))

        s_load = sem("s_load")
        s_const = sem("s_const")
        s_masks = sem("s_masks")
        s_modmask = sem("s_modmask")
        s_angle = sem("s_angle")
        s_dve = sem("s_dve")
        residue = carve(0, P)
        posi = carve(128, L).bitcast(I32)
        freq = carve(1700, 1)
        angle = carve(2048, L)
        turns = carve(2560, L)
        ang_c = carve(3072, L)
        wrap = carve(3584, L)

        def reduce_angle(dve, st, ang, k, cos_ang, tmp):
            st.link(dve.tensor_scalar(k, ang, 1 / (2 * math.pi), ROUND, ALU.mult, ALU.add))
            st.link(dve.tensor_scalar(k, k, -ROUND, None, ALU.add))
            for part in (TWO_PI_HI, TWO_PI_MID, TWO_PI_LO):
                st.link(dve.scalar_tensor_tensor(ang, k, -part, ang, ALU.mult, ALU.add))
            st.link(dve.tensor_scalar(cos_ang, ang, math.pi / 2, None, ALU.add))
            st.link(dve.tensor_scalar(tmp, cos_ang, math.pi, -2 * math.pi, ALU.is_gt, ALU.mult))
            st.link(dve.tensor_tensor(cos_ang, cos_ang, tmp, ALU.add))
            st.link(dve.tensor_scalar(cos_ang, cos_ang, PI_SAFE, -PI_SAFE, ALU.min, ALU.max))
            st.link(dve.tensor_scalar(ang, ang, PI_SAFE, -PI_SAFE, ALU.min, ALU.max))

        with nc.Block() as block:
            @block.sync
            def _(sp):
                sp.dma_start(xT[:].rearrange("p a t -> p (a t)"), x_cm).then_inc(s_load, 16)
                sp.dma_start(posi, positions.broadcast_to([P, L])).then_inc(s_load, 16)
                sp.dma_start(freq, inv_freq).then_inc(s_load, 16)

            @block.gpsimd
            def _(pool):
                st = Steps(pool, s_const)
                st.step(pool.memset(ident[:], 0.0))
                st.step(pool.memset(mean_ones[:], 1.0 / D))
                st.step(pool.memset(residue[0:4, :], 0.0))
                st.step(pool.memset(eps[:], EPS))
                st.step(pool.memset(layer_base[:], 0.0))
                st.step(pool.memset(mask[:], 0.0))
                st.settle()
                st.step(pool.iota(iota16[:], [[1, TOPK]], base=0, channel_multiplier=0,
                                  allow_small_or_imprecise_dtypes=True))
                st.step(pool.affine_select(out=ident[:], in_=ident[:], compare_op=ALU.not_equal, fill=1.0, base=0,
                                           pattern=[[-1, P]], channel_multiplier=1))
                st.step(pool.affine_select(out=residue[0:4, :].rearrange("p (m c) -> p m c", c=4),
                                           in_=residue[0:4, :].rearrange("p (m c) -> p m c", c=4),
                                           compare_op=ALU.not_equal, fill=1.0, base=0,
                                           pattern=[[0, P // 4], [-1, 4]], channel_multiplier=1))
                st.settle()
                for b in range(NT):
                    near = mask[:, b, 0:L].rearrange("p (b i) -> p b i", b=NT)
                    st.link(pool.affine_select(out=near, in_=near, compare_op=ALU.is_ge, fill=NEG, base=b,
                                               pattern=[[-1, NT], [-4, P]], channel_multiplier=4))
                    st.step(pool.affine_select(out=near, in_=near, compare_op=ALU.is_ge, fill=NEG, base=P - b,
                                               pattern=[[1, NT], [4, P]], channel_multiplier=-4))
                far = mask[:, :, L:KEYS].rearrange("p b (s i) -> p b s i", s=2)
                st.link(pool.affine_select(out=far, in_=far, compare_op=ALU.is_ge, fill=NEG, base=0,
                                           pattern=[[0, NT], [0, 2], [-1, P]], channel_multiplier=1))
                pool.sem_inc(s_masks, 1)

            @block.tensor
            def _(pe):
                pe.wait_ge(s_masks, 1)
                pe.matmul(ps[:, 0, 0:P], residue[0:4, :], residue[0:4, :], start=True, stop=True).then_inc(s_modmask, 1)

            @block.vector
            def _(dve):
                st = Steps(dve, s_dve)
                dve.wait_ge(s_load, 48)
                st.link(dve.tensor_copy(angle, posi))
                st.link(dve.tensor_scalar(angle, angle, freq, None, ALU.mult))
                reduce_angle(dve, st, angle, turns, ang_c, wrap)
                dve.sem_inc(s_angle, 1)
                dve.wait_ge(s_modmask, 1)
                st.link(dve.tensor_scalar(wrap[:, 0:P], ps[:, 0, 0:P], -1.0, -NEG, ALU.add, ALU.mult))
                for b in range(NT):
                    st.step(dve.tensor_tensor(mask[:, b, L + P:KEYS], mask[:, b, L + P:KEYS], wrap[:, 0:P], ALU.add))

            @block.scalar
            def _(act):
                act.wait_ge(s_angle, 1)
                act.activation(sinT[:], angle, ACT.Sin)
                act.activation(cosT[:], ang_c, ACT.Sin)

        w_landed = [sem(f"w_landed{i}") for i in range(RING)]
        small_landed = sem("small_landed")
        side_landed = sem("side_landed")
        tiles_done = sem("tiles_done")
        bank_free = [sem(f"bank_free{i}") for i in range(4)]
        squares = sem("squares")
        mean_done = sem("mean_done")
        root_done = sem("root_done")
        normed = sem("normed")
        act_steps = sem("act_steps")
        dve_steps = sem("dve_steps")
        pool_steps = sem("pool_steps")
        raw_ready = sem("raw_ready")
        roped = sem("roped")
        pool_in_ready = sem("pool_in_ready")
        pooled_ready = sem("pooled_ready")
        mixed = sem("mixed")
        ssm_in_ready = sem("ssm_in_ready")
        blocks_ready = sem("blocks_ready")
        poles_ready = sem("poles_ready")
        pow_a_ready = sem("pow_a_ready")
        bbar_ready = sem("bbar_ready")
        bbarT_done = sem("bbarT_done")
        bbarT_ready = sem("bbarT_ready")
        tab_ready = sem("tab_ready")
        x_done = sem("x_done")
        x_free = sem("x_free")
        scan_done = sem("scan_done")
        prod_dve = sem("prod_dve")
        prod_pool = sem("prod_pool")
        turned_back = sem("turned_back")
        y_done = sem("y_done")
        y_taken = sem("y_taken")
        y_gelu = sem("y_gelu")
        v_ready = sem("v_ready")
        glu_sig = sem("glu_sig")
        glu_ready = sem("glu_ready")
        sc_done = sem("sc_done")
        sc_max = sem("sc_max")
        exp_done = sem("exp_done")
        pt_done = sem("pt_done")
        pt_copied = sem("pt_copied")
        pv_done = sem("pv_done")
        o_done = sem("o_done")
        ot_done = sem("ot_done")
        ot_copied = sem("ot_copied")
        gate_sig = sem("gate_sig")
        gate_used = sem("gate_used")
        x_mixed = sem("x_mixed")
        first_q_copied = sem("first_q_copied")
        first_scores_ready = sem("first_scores_ready")
        rest_q_copied = sem("rest_q_copied")
        h_tok_copied = sem("h_tok_copied")
        out_stored = sem("out_stored")

        def norm_squares(act):
            for k in range(KD):
                act.activation(hT[:, k, :], xT[:, k, :], ACT.Square).then_inc(squares, 1)

        def norm_mean(pe, which, blocks=range(KD)):
            for k in blocks:
                pe.wait_ge(squares, KD * which + k + 1)
                mm = pe.matmul(ps[:, MEAN_BANK, :], mean_ones[:], hT[:, k, :], start=(k == 0), stop=(k == KD - 1))
                if k == KD - 1:
                    mm.then_inc(mean_done, 1)

        def norm_root(act, which):
            act.wait_ge(mean_done, which + 1)
            act.activation(rms, ps[:, MEAN_BANK, :], ACT.Sqrt, bias=eps[:, 0:1]).then_inc(root_done, 1)

        def norm_scale(dve, which, gain, dst):
            dve.wait_ge(root_done, which + 1)
            dve.reciprocal(rstd, rms).then_inc(normed, 1)
            dve.wait_ge(normed, which * (KD + 1) + 1)
            for k in range(KD):
                dve.scalar_tensor_tensor(dst[:, k, :], xT[:, k, :], gain[:, k:k + 1], rstd, ALU.mult,
                                         ALU.mult).then_inc(normed, 1)

        def chunk_weight(c, at, n=P):
            return wring[:, c % RING, at:at + n]

        def need_chunk(pe, c):
            pe.wait_ge(w_landed[c % RING], 16 * (c // RING + 1))

        def need_head(pe, h):
            if h < SIDE_HEADS:
                pe.wait_ge(side_landed, 16 * SIDE_HEADS)
            else:
                need_chunk(pe, C_WQ + h - SIDE_HEADS)

        def head_weight(h, at):
            return side_w[:, h, at:at + P] if h < SIDE_HEADS else chunk_weight(C_WQ + h - SIDE_HEADS, at)

        def query_tile(pe, item):
            n, kind, i = TILE_NUMBER[item], item[1], item[2]
            pe.wait_ge(bank_free[n % 4], n // 4)
            if kind == "h_tok":
                for k in range(4):
                    mm = pe.transpose(ps[:, n % 4, k * P:(k + 1) * P], hT[:, 4 * item[3] + k, i * P:(i + 1) * P], ident[:])
            elif kind == "first_wq":
                need_head(pe, i)
                for s in range(2):
                    for k in range(KD):
                        if i == 0 and s == 0:
                            pe.wait_ge(normed, KD + 1 + k + 2)
                        mm = pe.matmul(ps[:, n % 4, s * P:(s + 1) * P], head_weight(i, k * 256 + s * P), hT[:, k, 0:P],
                                       start=(k == 0), stop=(k == KD - 1))
            elif kind == "wq":
                need_head(pe, i // 2)
                for k in range(KD):
                    mm = pe.matmul(ps[:, n % 4, 0:L - P], head_weight(i // 2, k * 256 + (i % 2) * P), hT[:, k, P:L],
                                   start=(k == 0), stop=(k == KD - 1))
            elif kind == "first_score":
                pe.wait_ge(first_q_copied, i + 1)
                for s in range(2):
                    mm = pe.matmul(ps[:, n % 4, s * NKEYS:(s + 1) * NKEYS], first_q[:, i, s, :],
                                   keysT[:, s * NKEYS:(s + 1) * NKEYS], start=True, stop=True)
            else:
                pe.wait_ge(rest_q_copied, i + 1)
                for k in range(NT - 1):
                    mm = pe.matmul(ps[:, n % 4, k * NKEYS:(k + 1) * NKEYS], rest_q[:, i % 4, k * P:(k + 1) * P],
                                   keysT[:, (i % 2) * NKEYS:(i % 2 + 1) * NKEYS], start=True, stop=True)
            mm.then_inc(tiles_done, 1)

        def query_evacuate(act, item):
            n, kind, i = TILE_NUMBER[item], item[1], item[2]
            act.wait_ge(tiles_done, n + 1)
            src = ps[:, n % 4, :]
            if kind == "h_tok":
                act.copy(h_tok[:, i, L * item[3]:L * item[3] + L], src).then_inc(h_tok_copied, 1)
                act.wait_ge(h_tok_copied, 2 * i + item[3] + 1)
            elif kind == "first_wq":
                act.copy(first_q[:, i, :, :].rearrange("p s t -> p (s t)"), src[:, 0:2 * P]).then_inc(first_q_copied, 1)
                act.wait_ge(first_q_copied, i + 1)
            elif kind == "wq":
                act.copy(rest_q[:, i % 4, :], src[:, 0:L - P]).then_inc(rest_q_copied, 1)
                act.wait_ge(rest_q_copied, i + 1)
            elif kind == "first_score":
                act.copy(scores[:, 0, 2 * i:2 * i + 2, :].rearrange("p j k -> p (j k)"),
                         src[:, 0:2 * NKEYS]).then_inc(first_scores_ready, 1)
                act.wait_ge(first_scores_ready, i + 1)
            else:
                act.copy(scores[:, 1:NT, i, :], src[:, 0:(NT - 1) * NKEYS].rearrange("p (t k) -> p t k", k=NKEYS)
                         ).then_inc(scores_ready, 1)
                act.wait_ge(scores_ready, i + 1)
            act.sem_inc(bank_free[n % 4], 1)

        def pick_first_lists(dve, h):
            base = h * FIRST_STEPS
            at = 2 * h * TOPK
            top = lambda s, half: topv[:, at + s * TOPK + 8 * half:at + s * TOPK + 8 * half + 8]
            index = lambda s, half: first_i[:, s * TOPK + 8 * half:s * TOPK + 8 * half + 8]
            full = lambda s: scores[:, 0, 2 * h + s, :]
            for s in range(2):
                dve.max(top(s, 0), full(s)).then_inc(first_steps, 1)
            for s in range(2):
                dve.wait_ge(first_steps, base + s + 1)
                dve.match_replace(first_left[:, s, :], top(s, 0), full(s), LOWEST).then_inc(first_steps, 1)
            for s in range(2):
                dve.max_index(index(s, 0), top(s, 0), full(s)).then_inc(first_steps, 1)
            for s in range(2):
                dve.wait_ge(first_steps, base + s + 3)
                dve.max(top(s, 1), first_left[:, s, :]).then_inc(first_steps, 1)
            for s in range(2):
                dve.wait_ge(first_steps, base + s + 7)
                dve.max_index(index(s, 1), top(s, 1), first_left[:, s, :]).then_inc(first_steps, 1)
            dve.wait_ge(first_steps, base + 10)
            dve.tensor_copy(topif[:, at:at + 2 * TOPK], first_i).then_inc(first_steps, 1)
            dve.wait_ge(first_steps, base + FIRST_STEPS)

        def pick_list(dve, n, j):
            base = (n * 16 + j) * LIST_STEPS + 1
            dve.wait_ge(list_steps, base)
            dve.tensor_copy(list_in, scores_flat[:, bass.ds((n + 1) * (16 * NKEYS) + j * NKEYS, NKEYS)]).then_inc(list_steps, 1)
            yield
            dve.wait_ge(list_steps, base + 1)
            dve.sem_inc(dve_turn, 1)
            dve.max(list_v[:, 0:8], list_in).then_inc(list_steps, 1)
            yield
            dve.wait_ge(list_steps, base + 2)
            dve.sem_inc(dve_turn, 1)
            dve.match_replace(list_left, list_v[:, 0:8], list_in, LOWEST).then_inc(list_steps, 1)
            yield
            dve.max_index(list_i[:, 0:8], list_v[:, 0:8], list_in).then_inc(list_steps, 1)
            yield
            dve.wait_ge(list_steps, base + 3)
            dve.sem_inc(dve_turn, 1)
            dve.max(list_v[:, 8:16], list_left).then_inc(list_steps, 1)
            yield
            dve.wait_ge(list_steps, base + 5)
            dve.sem_inc(dve_turn, 1)
            dve.max_index(list_i[:, 8:16], list_v[:, 8:16], list_left).then_inc(list_steps, 1)
            yield
            dve.tensor_copy(topv[:, bass.ds(j * TOPK, TOPK)], list_v).then_inc(list_steps, 1)
            yield
            dve.wait_ge(list_steps, base + 6)
            dve.tensor_copy(topif[:, bass.ds(j * TOPK, TOPK)], list_i).then_inc(list_steps, 1)
            yield

        def pick_head(dve, n, h):
            base = (n * PH + h) * HEAD_STEPS + 1
            dve.wait_ge(head_steps, base)
            dve.tensor_tensor(cand.rearrange("p (a b) -> p a b", a=TOPK),
                              topv[:, bass.ds(h * (2 * TOPK), TOPK)].unsqueeze(2).broadcast_to([P, TOPK, TOPK]),
                              topv[:, bass.ds(h * (2 * TOPK) + TOPK, TOPK)].unsqueeze(1).broadcast_to([P, TOPK, TOPK]),
                              ALU.add).then_inc(head_steps, 1)
            yield
            dve.wait_ge(head_steps, base + 1)
            dve.sem_inc(dve_turn, 1)
            dve.max(cand_v[:, 0:8], cand).then_inc(head_steps, 1)
            yield
            dve.wait_ge(head_steps, base + 2)
            dve.sem_inc(dve_turn, 1)
            dve.match_replace(cand_left, cand_v[:, 0:8], cand, LOWEST).then_inc(head_steps, 1)
            yield
            dve.max_index(cand_p[:, 0:8], cand_v[:, 0:8], cand).then_inc(head_steps, 1)
            yield
            dve.wait_ge(head_steps, base + 3)
            dve.sem_inc(dve_turn, 1)
            dve.max(cand_v[:, 8:16], cand_left).then_inc(head_steps, 1)
            yield
            dve.wait_ge(head_steps, base + 5)
            dve.sem_inc(dve_turn, 1)
            dve.max_index(cand_p[:, 8:16], cand_v[:, 8:16], cand_left).then_inc(head_steps, 1)
            yield
            dve.tensor_copy(head_s[:, bass.ds(h * TOPK, TOPK)], cand_v).then_inc(head_steps, 1)
            yield
            dve.wait_ge(head_steps, base + 6)
            dve.tensor_scalar(place_u[:, 0, :], cand_p, 4, None, ALU.logical_shift_right).then_inc(head_steps, 1)
            yield
            dve.tensor_scalar(place_u[:, 1, :], cand_p, 15, None, ALU.bitwise_and).then_inc(head_steps, 1)
            yield
            dve.wait_ge(head_steps, base + 9)
            dve.tensor_copy(place_f, place_u.rearrange("p s k -> p (s k)")).then_inc(head_steps, 1)
            yield
            dve.wait_ge(head_steps, base + 10)
            dve.tensor_tensor(onehot.rearrange("p (n j) -> p n j", j=TOPK),
                              place_f.unsqueeze(2).broadcast_to([P, 2 * TOPK, TOPK]),
                              iota16[:].unsqueeze(1).broadcast_to([P, 2 * TOPK, TOPK]), ALU.is_equal).then_inc(head_steps, 1)
            yield
            dve.wait_ge(head_steps, base + 11)
            four = onehot.rearrange("p (s k j) -> p s k j", s=2, k=TOPK)
            keys_of = topif[:, bass.ds(h * (2 * TOPK), 2 * TOPK)].rearrange("p (s j) -> p s j", s=2)
            dve.tensor_tensor(four, four, keys_of.unsqueeze(2).broadcast_to([P, 2, TOPK, TOPK]),
                              ALU.mult).then_inc(head_steps, 1)
            yield
            dve.wait_ge(head_steps, base + 12)
            dve.tensor_reduce(head_k[:, bass.ds(h * (2 * TOPK), 2 * TOPK)],
                              onehot.rearrange("p (n j) -> p n j", j=TOPK), AX.X, ALU.add).then_inc(head_steps, 1)
            yield

        def settle_picks(dve, n):
            base = n * PICK_STEPS + 1
            dve.wait_ge(head_steps, (n + 1) * (PH * HEAD_STEPS) + 1)
            hs = head_s.rearrange("p (h k) -> p h k", k=TOPK)
            hk = head_k.rearrange("p (h s k) -> p h s k", s=2, k=TOPK)
            ge = gate_e.rearrange("p (h k) -> p h k", k=TOPK)
            dve.tensor_tensor(ge, hs, hs[:, :, 0:1].broadcast_to([P, PH, TOPK]), ALU.subtract).then_inc(shifted, 1)
            dve.scalar_tensor_tensor(expert_f.rearrange("p (h k) -> p h k", k=TOPK), hk[:, :, 0, :], float(NKEYS),
                                     hk[:, :, 1, :], ALU.mult, ALU.add).then_inc(pick_steps, 1)
            dve.wait_ge(pick_steps, base + 1)
            dve.tensor_scalar(expert[:, bass.ds(n * PICKS, PICKS)], expert_f, layer_base[:, 0:1], None,
                              ALU.add).then_inc(picks_ready, 1)
            dve.wait_ge(exp_ready, n + 1)
            dve.tensor_reduce(gate_s[:, 0:PH], ge, AX.X, ALU.add).then_inc(pick_steps, 1)
            dve.wait_ge(pick_steps, base + 2)
            dve.reciprocal(gate_s[:, PH:2 * PH], gate_s[:, 0:PH]).then_inc(pick_steps, 1)
            dve.wait_ge(pick_steps, base + 3)
            dve.tensor_tensor(gates[:, bass.ds(n * PICKS, PICKS)].rearrange("p (h k) -> p h k", k=TOPK), ge,
                              gate_s[:, PH:2 * PH].unsqueeze(2).broadcast_to([P, PH, TOPK]), ALU.mult).then_inc(pick_steps, 1)
            dve.wait_ge(pick_steps, base + 4)
            dve.sem_inc(dve_turn, 1)

        def powers(eng, st, table, count, scratch, wide, skip=0):
            w_re, w_im, t0, t1 = scratch
            for e in range(-skip, count):
                if e >= 0:
                    d = 1 << e
                    lo = lambda s: table[:, s, :, 0:d]
                    hi = lambda s: table[:, s, :, d:2 * d]
                    bc = lambda w: w.unsqueeze(2).broadcast_to([P, PAIRS, d])
                    ta, tb = wide[:, 0, :, 0:d], wide[:, 1, :, 0:d]
                    st.step(eng.tensor_tensor(hi(0), lo(0), bc(w_re), ALU.mult))
                    st.step(eng.tensor_tensor(hi(1), lo(1), bc(w_re), ALU.mult))
                    st.step(eng.tensor_tensor(ta, lo(1), bc(w_im), ALU.mult))
                    st.step(eng.tensor_tensor(tb, lo(0), bc(w_im), ALU.mult))
                if e < count - 1:
                    st.step(eng.tensor_tensor(t0, w_im, w_im, ALU.mult))
                    st.step(eng.tensor_tensor(t1, w_re, w_im, ALU.mult))
                st.settle()
                if e >= 0:
                    st.step(eng.tensor_tensor(hi(0), hi(0), ta, ALU.subtract))
                    st.step(eng.tensor_tensor(hi(1), hi(1), tb, ALU.add))
                if e < count - 1:
                    st.link(eng.tensor_tensor(w_re, w_re, w_re, ALU.mult))
                    st.step(eng.tensor_tensor(w_re, w_re, t0, ALU.subtract))
                    st.step(eng.tensor_tensor(w_im, t1, t1, ALU.add))
                st.settle()

        def mixer(layer):
            def attend_max(dve, st, i):
                b = i // SLOTS
                bank = 4 + 2 * (i % 2)
                dve.wait_ge(sc_done, i + 1)
                if i >= 2:
                    dve.wait_ge(pt_done, i - 1)
                st.link(dve.tensor_tensor_reduce(
                    srow[:, i % 2, :], ps[:, bank:bank + 2, :].rearrange("p a t -> p (a t)")[:, 0:KEYS],
                    mask[:, b, :], 1.0, LOWEST, ALU.add, ALU.max, stats[:, i:i + 1]))
                dve.tensor_scalar(stats[:, 16 + i:17 + i], stats[:, i:i + 1], -SCALE, None, ALU.mult).then_inc(sc_max, 1)

            def attend_out(dve, st, i):
                b, h = i // SLOTS, i % SLOTS
                dve.wait_ge(pv_done, i + 1)
                st.link(dve.reciprocal(stats[:, 48 + i % 2:49 + i % 2], stats[:, 32 + i:33 + i]))
                dve.tensor_scalar(otok[:, b % 2, h * HEAD:(h + 1) * HEAD], ps[:, 2 + i % 2, 0:HEAD],
                                  stats[:, 48 + i % 2:49 + i % 2], None, ALU.mult).then_inc(o_done, 1)
                if h == 0 and b:
                    move_home(dve, b - 1)
                if i == 15:
                    move_home(dve, b)

            def move_home(dve, b):
                dve.wait_ge(ot_done, b + 1)
                dve.tensor_copy(attnT[:, :, :].rearrange("p m (i b) -> p m b i", b=NT)[:, :, b, :],
                                ps[:, 1, 0:256].rearrange("p (m i) -> p m i", m=2)).then_inc(ot_copied, 1)

            with nc.Block() as block:
                @block.sync
                def _(sp):
                    sp.dma_start(vec[:], vecs[bass.ts(layer, P), :]).then_inc(small_landed, 16)
                    for half in range(2):
                        sp.dma_start(small[64 * half:64 * half + 64, 0, :],
                                     log_dt[bass.ds(layer * 2 + half, 1), :].broadcast_to([64, PAIRS])).then_inc(small_landed, 16)
                    sp.dma_start(bc_in.rearrange("p s g c -> p (s g c)"), ssm_bc[bass.ts(layer, P), :]).then_inc(small_landed, 16)
                    sp.dma_start(keysT[:], keys[bass.ts(layer, P), :]).then_inc(small_landed, 16)
                    for c in range(C_SIDE):
                        if c == C_WQ:
                            sp.wait_ge(tiles_done, TILE_NUMBER[("tile", "gate", KD - 1, 2)] + 1)
                            for h in range(SIDE_HEADS):
                                sp.dma_start(side_w[:, h, :], weights[bass.ts(layer * CHUNKS + C_SIDE + h, P), 0:2 * KD * P]
                                             ).then_inc(side_landed, 16)
                        if c >= RING:
                            sp.wait_ge(tiles_done, CHUNK_LAST_TILE[c - RING] + 1)
                        sp.dma_start(wring[:, c % RING, :],
                                     weights[bass.ts(layer * CHUNKS + c, P), :]).then_inc(w_landed[c % RING], 16)

                @block.gpsimd
                def _(pool):
                    st = Steps(pool, pool_steps)
                    st.step(pool.memset(b_blocks, 0.0))
                    st.step(pool.memset(c_blocks, 0.0))
                    pool.wait_ge(small_landed, 80)
                    st.settle()
                    for g in range(2):
                        rows_g, cols_g = slice(64 * g, 64 * g + 64), slice(16 * g, 16 * g + 16)
                        st.step(pool.tensor_copy(b_blocks[rows_g, :, :, cols_g], bc_in[rows_g, 0:2, :, :]))
                        st.step(pool.tensor_copy(c_blocks[rows_g, 0, :, cols_g], bc_in[rows_g, 2, :, :]))
                        st.step(pool.tensor_scalar(c_blocks[rows_g, 1, :, cols_g], bc_in[rows_g, 3, :, :], -1.0, None, ALU.mult))
                    st.settle()
                    pool.sem_inc(blocks_ready, 1)

                    pool.wait_ge(poles_ready, 1)
                    st.step(pool.memset(pow_b[:, 0, :, 0:1], 1.0))
                    st.step(pool.memset(pow_b[:, 1, :, 0:1], 0.0))
                    st.settle()
                    powers(pool, st, pow_b, 5, [small[:, i, :] for i in range(30, 34)], pow_tmp)

                    def table_of(p):
                        a = lambda s: pow_a[:, s, p, :].unsqueeze(2).broadcast_to([P, 16, 32])
                        b = lambda s: pow_b[:, s, p, :].unsqueeze(1).broadcast_to([P, 16, 32])
                        o = lambda s: tabs[:, p % 2, s, :].rearrange("p (a b) -> p a b", b=32)
                        ta = pool_scratch[:, 0, :].rearrange("p (a b) -> p a b", b=32)
                        tb = pool_scratch[:, 1, :].rearrange("p (a b) -> p a b", b=32)
                        st.step(pool.tensor_tensor(o(0), a(0), b(0), ALU.mult))
                        st.step(pool.tensor_tensor(ta, a(1), b(1), ALU.mult))
                        st.step(pool.tensor_tensor(o(1), a(1), b(0), ALU.mult))
                        st.step(pool.tensor_tensor(tb, a(0), b(1), ALU.mult))
                        st.settle()
                        st.step(pool.tensor_tensor(o(0), o(0), ta, ALU.subtract))
                        st.link(pool.tensor_tensor(o(1), o(1), tb, ALU.add))
                        pool.sem_inc(tab_ready, 1)

                    pool.wait_ge(bbar_ready, 1)
                    pool.wait_ge(pow_a_ready, 1)
                    table_of(0)
                    table_of(1)

                    def windows():
                        pool.wait_ge(pool_in_ready, 4)
                        for g, win in enumerate(POOL_WINDOWS):
                            src = pool_in[:, g, :]
                            bufs = [pool_sum[:, g, :], pool_scratch[:, 0, :]]
                            cur, shift, n = src, 1, 0
                            while shift < win:
                                left = int(math.log2(win // shift)) - 1
                                dst = bufs[left % 2]
                                st.step(pool.tensor_copy(dst[:, 0:shift], cur[:, 0:shift]))
                                st.step(pool.tensor_tensor(dst[:, shift:L], cur[:, shift:L], cur[:, 0:L - shift], ALU.add))
                                st.settle()
                                cur, shift = dst, shift * 2
                            st.step(pool.tensor_scalar(cur[:, win - 1:L], cur[:, win - 1:L], 1.0 / win, None, ALU.mult))
                            for t in range(1, win - 1):
                                st.step(pool.tensor_scalar(cur[:, t:t + 1], cur[:, t:t + 1], 1.0 / (t + 1), None, ALU.mult))
                            st.settle()
                            st.link(pool.tensor_tensor(src, cur, src, ALU.subtract))
                            pool.sem_inc(pooled_ready, 1)

                    windows()
                    for p in range(PAIRS):
                        pool.wait_ge(scan_done, 2 * (p + 1))
                        if p:
                            pool.wait_ge(y_done, p)
                        st.step(pool.tensor_tensor(prods[2], scanned[:, p % 2, 1, :], tabs[:, p % 2, 0, :], ALU.mult))
                        st.link(pool.tensor_tensor(prods[3], scanned[:, p % 2, 0, :], tabs[:, p % 2, 1, :], ALU.mult))
                        pool.sem_inc(prod_pool, 1)
                        if p + 2 < PAIRS:
                            pool.wait_ge(prod_dve, 2 * (p + 1))
                            table_of(p + 2)

                @block.tensor
                def _(pe):
                    norm_mean(pe, 0)

                    def product(n, lhs, rhs, width=L, chunk_at=None):
                        for k in range(len(lhs)):
                            if n == 0:
                                pe.wait_ge(normed, k + 2)
                            if chunk_at and k in chunk_at:
                                need_chunk(pe, chunk_at[k])
                            mm = pe.matmul(ps[:, n % 4, 0:width], lhs[k], rhs[k], start=(k == 0), stop=(k == len(lhs) - 1))
                        return mm

                    def tile(item):
                        n, kind = TILE_NUMBER[item], item[1]
                        if n >= 4:
                            pe.wait_ge(bank_free[n % 4], n // 4)
                        first = {"pool_u": C_POOL, "ssm_u": C_SSM, "q": C_Q, "k": C_K, "out": C_OUT}.get(kind)
                        if kind in QUERY_KINDS:
                            query_tile(pe, item)
                            return
                        if first is not None:
                            m = item[2]
                            c = first + m // 2
                            src = merged if kind == "out" else hT
                            if kind == "out" and m == 0:
                                pe.wait_ge(gate_used, 3 * KD)
                            mm = product(n, [chunk_weight(c, k * 256 + (m % 2) * P) for k in range(KD)],
                                         [src[:, k, :] for k in range(KD)], chunk_at={0: c})
                        elif kind == "v":
                            c, b = C_V + item[2], item[3]
                            mm = product(n, [hT[:, k, :].rearrange("p (i b) -> p b i", b=NT)[:, b, :] for k in range(KD)],
                                         [chunk_weight(c, k * 256, 256) for k in range(KD)], width=256, chunk_at={0: c})
                        elif kind == "mix":
                            g = item[2]
                            pe.wait_ge(pooled_ready, g + 1)
                            mm = product(n, [chunk_weight(C_MIX, g * P)], [pool_in[:, g, :]], chunk_at={0: C_MIX})
                        elif kind in ("glu_gate", "glu_val"):
                            m = item[2]
                            c = C_GLU + m // 2
                            pe.wait_ge(y_gelu, 4)
                            at = (m % 2) * P + (256 if kind == "glu_gate" else 0)
                            mm = product(n, [chunk_weight(c, k * 512 + at) for k in range(4)],
                                         [ssmT[:, k, :] for k in range(4)], chunk_at={0: c})
                        elif kind in ("branch", "gate"):
                            m, b = item[2], item[3]
                            at = BRANCH_START[(b, kind == "gate")]
                            rows_n = 8 if kind == "gate" else BRANCH_K[b]
                            src = hT if kind == "gate" else (mixT, gluT, attnT)[b]
                            if kind == "branch" and m == 0:
                                pe.wait_ge((mixed, glu_ready, ot_copied)[b], 4)
                            where = [(C_MERGE + 2 * m + (at + k) // 17, (at + k) % 17) for k in range(rows_n)]
                            mm = product(n, [chunk_weight(c, j * P) for c, j in where],
                                         [src[:, k, :] for k in range(rows_n)],
                                         chunk_at={k: c for k, (c, j) in enumerate(where) if k == 0 or c != where[k - 1][0]})
                        mm.then_inc(tiles_done, 1)

                    def pair_in(p):
                        m, a = p // PER_TILE, p % PER_TILE
                        part = slice(32 * a, 32 * a + 32)
                        if p == 0:
                            pe.wait_ge(bbar_ready, 1)
                            for s in range(2):
                                for mm_ in range(4):
                                    blk = bbar[:, s, 4 * mm_:4 * mm_ + 4, :].rearrange("p g c -> p (g c)")
                                    last = pe.transpose(ps[:, 4 + s, mm_ * P:(mm_ + 1) * P], blk, ident[:])
                            last.then_inc(bbarT_done, 1)
                            pe.wait_ge(ssm_in_ready, 4)
                            pe.wait_ge(bbarT_ready, 2)
                        else:
                            pe.wait_ge(x_free, p)
                        for s in range(2):
                            mm = pe.matmul(ps[:, 4 + s, :], bbarT[part, s, m, :], ssmT[part, m, :], start=True, stop=True)
                        mm.then_inc(x_done, 1)

                    def pair_out(p):
                        m, a = p // PER_TILE, p % PER_TILE
                        if p == 0:
                            pe.wait_ge(blocks_ready, 1)
                        if a == 0 and m >= 2:
                            pe.wait_ge(y_taken, m - 1)
                        pe.wait_ge(turned_back, 2 * (p + 1))
                        for i in range(2):
                            mm = pe.matmul(ps[32 * a:32 * a + 32, 6 + m % 2, :], c_blocks[:, i, p, :], prods[2 * i],
                                           start=(i == 0), stop=(i == 1))
                        mm.then_inc(y_done, 1)

                    its = [(b, h) for b in range(NT) for h in range(SLOTS)]

                    def attend_score(i):
                        b, h = its[i]
                        bank = 4 + 2 * (i % 2)
                        if i >= 2:
                            pe.wait_ge(sc_max, i - 1)

                        def rows_of(t, g):
                            m = 2 * g + h // 2
                            return t[HEAD * (h % 2):HEAD * (h % 2) + HEAD, m, :].rearrange("p (i b) -> p b i", b=NT)

                        pe.matmul(ps[:, bank, :], rows_of(qT, 0)[:, b, :], rows_of(kT, 0), start=True, stop=True)
                        for g in (1, 2):
                            mm = pe.matmul(ps[:, bank + 1, (g - 1) * P:g * P], rows_of(qT, g)[:, b, :],
                                           rows_of(kT, g)[:, b, :], start=True, stop=True)
                        mm.then_inc(sc_done, 1)

                    def attention():
                        for b in range(4):
                            done = len([i for i in range(TILE_NUMBER[("tile", "branch", 0, 0)]) if i % 4 == b])
                            pe.wait_ge(bank_free[b], done)
                        pe.wait_ge(v_ready, 12)

                        def turn(i):
                            pe.wait_ge(exp_done, i + 1)
                            if i:
                                pe.wait_ge(pt_copied, i)
                            if i > 1 and (i - 1) % SLOTS == 0:
                                pe.wait_ge(ot_copied, (i - 1) // SLOTS)
                            for j in range(6):
                                mm = pe.transpose(ps[:, j // 4, (j % 4) * P:(j % 4 + 1) * P],
                                                  srow[:, i % 2, j * P:(j + 1) * P], ident[:])
                            mm.then_inc(pt_done, 1)

                        def weigh(i):
                            b, h = its[i]
                            pe.wait_ge(pt_copied, i + 1)
                            if i >= 2:
                                pe.wait_ge(o_done, i - 1)
                            for j in range(6):
                                g, kb = (0, j) if j < 4 else (j - 3, b)
                                mm = pe.matmul(ps[:, 2 + i % 2, 0:HEAD], pT[:, i % 2, j * P:(j + 1) * P],
                                               vtok[:, kb, (4 * g + h) * HEAD:(4 * g + h + 1) * HEAD],
                                               start=(j == 0), stop=(j == 5))
                            mm.then_inc(pv_done, 1)
                            if h == SLOTS - 1:
                                return b
                            return None

                        def turn_out(b):
                            pe.wait_ge(o_done, 4 * (b + 1))
                            for j in range(2):
                                mm = pe.transpose(ps[:, 1, j * P:(j + 1) * P], otok[:, b % 2, j * P:(j + 1) * P], ident[:])
                            mm.then_inc(ot_done, 1)

                        pending = None
                        for i in range(len(its)):
                            turn(i)
                            if i + 2 < len(its):
                                attend_score(i + 2)
                            last_b = weigh(i)
                            if pending is not None:
                                turn_out(pending)
                            pending = last_b
                        turn_out(pending)
                        pe.wait_ge(ot_copied, 4)

                    for item in ORDER:
                        if item[0] == "tile":
                            tile(item)
                        elif item[0] == "pair":
                            pair_in(item[1])
                        elif item[0] == "pair_out":
                            pair_out(item[1])
                        elif item[0] == "attention_start":
                            pe.wait_ge(roped, 12)
                            pe.wait_ge(x_free, PAIRS)
                            attend_score(0)
                            pe.wait_ge(y_taken, 4)
                            attend_score(1)
                        elif item[0] == "attention":
                            attention()
                        elif item[0] == "mean":
                            norm_mean(pe, 1, [item[1]])

                @block.scalar
                def _(act):
                    norm_squares(act)
                    st = Steps(act, act_steps)
                    act.wait_ge(poles_angle, 1)
                    act.activation(small[:, 12, :], small[:, 4, :], ACT.Sin).then_inc(poles_sincos, 1)
                    act.activation(small[:, 13, :], small[:, 6, :], ACT.Sin).then_inc(poles_sincos, 1)
                    norm_root(act, 0)

                    def attend_exp(i):
                        act.wait_ge(sc_max, i + 1)
                        act.activation(srow[:, i % 2, :], srow[:, i % 2, :], ACT.Exp, bias=stats[:, 16 + i:17 + i],
                                       scale=SCALE, accum_out=stats[:, 32 + i:33 + i]).then_inc(exp_done, 1)

                    glu_n = gate_n = raw_n = 0
                    for item in ORDER:
                        kind = item[1] if item[0] == "tile" else item[0]
                        if item[0] == "tile":
                            n = TILE_NUMBER[item]
                            src = ps[:, n % 4, :]
                            free = bank_free[n % 4]
                        if kind in ("pool_u", "ssm_u"):
                            act.wait_ge(tiles_done, n + 1)
                            dst, ready = (pool_in, pool_in_ready) if kind == "pool_u" else (ssmT, ssm_in_ready)
                            st.step(act.copy(dst[:, item[2], :], src))
                            st.settle()
                            act.sem_inc(ready, 1)
                            act.sem_inc(free, 1)
                        elif kind in ("q", "k"):
                            act.wait_ge(tiles_done, n + 1)
                            if raw_n >= 2:
                                act.wait_ge(roped, raw_n - 1)
                            act.copy(raw[:, item[2] % 2, :], src).then_inc(raw_ready, 1)
                            for q in range(4):
                                to, at = slice(32 * q, 32 * q + 32), 32 * (q ^ 1)
                                act.activation(swapped[to, item[2] % 2, :], ps[at:at + 32, n % 4, :], ACT.Copy,
                                               scale=1.0 if q % 2 else -1.0).then_inc(raw_ready, 1)
                            act.wait_ge(raw_ready, 5 * (raw_n + 1))
                            act.sem_inc(free, 1)
                            raw_n += 1
                        elif kind == "v":
                            act.wait_ge(tiles_done, n + 1)
                            st.link(act.copy(vtok[:, item[3], 256 * item[2]:256 * item[2] + 256], src[:, 0:256]))
                            act.sem_inc(v_ready, 1)
                            act.sem_inc(free, 1)
                        elif kind == "pair" and item[1] == 0:
                            act.wait_ge(bbarT_done, 1)
                            for s in range(2):
                                act.copy(bbarT[:, s, :, :], ps[:, 4 + s, :].rearrange("p (m n) -> p m n", m=4)).then_inc(bbarT_ready, 1)
                        elif kind == "mix":
                            act.wait_ge(tiles_done, n + 1)
                            g = item[2]
                            st.link(act.activation(mixT[:, g, :], src, ACT.Copy, scale=vec[:, V_PSCALE + g:V_PSCALE + g + 1]))
                            act.sem_inc(mixed, 1)
                            act.sem_inc(free, 1)
                        elif kind == "pairs_end":
                            for m in range(4):
                                act.wait_ge(y_taken, m + 1)
                                act.activation(ssmT[:, m, :], ssmT[:, m, :], ACT.Gelu_apprx_tanh).then_inc(y_gelu, 1)
                        elif kind == "glu_gate":
                            act.wait_ge(tiles_done, n + 1)
                            if glu_n >= 2:
                                act.wait_ge(glu_ready, glu_n - 1)
                            st.link(act.activation(glu_sigmoid[:, glu_n % 2, :], src, ACT.Sigmoid))
                            act.sem_inc(glu_sig, 1)
                            act.sem_inc(free, 1)
                            glu_n += 1
                        elif kind == "gate":
                            act.wait_ge(tiles_done, n + 1)
                            if gate_n >= 2:
                                act.wait_ge(gate_used, gate_n - 1)
                            st.link(act.activation(sig[:, gate_n % 2, :], src, ACT.Sigmoid))
                            act.sem_inc(gate_sig, 1)
                            act.sem_inc(free, 1)
                            gate_n += 1
                        elif kind == "attention_start":
                            attend_exp(0)
                            attend_exp(1)
                        elif kind == "attention":
                            for i in range(16):
                                act.wait_ge(pt_done, i + 1)
                                if i >= 2:
                                    act.wait_ge(pv_done, i - 1)
                                act.copy(pT[:, i % 2, :], ps[:, 0:2, :].rearrange("p a t -> p (a t)")[:, 0:KEYS]).then_inc(pt_copied, 1)
                                if i + 2 < 16:
                                    attend_exp(i + 2)
                        elif kind == "out":
                            act.wait_ge(x_mixed, item[2] + 1)
                            act.activation(hT[:, item[2], :], xT[:, item[2], :], ACT.Square).then_inc(squares, 1)
                        elif kind == "norm2":
                            norm_root(act, 1)
                        elif kind in QUERY_KINDS:
                            query_evacuate(act, item)
                    act.wait_ge(shifted, 1)
                    act.activation(gate_e, gate_e, ACT.Exp).then_inc(exp_ready, 1)

                @block.vector
                def _(dve):
                    st = Steps(dve, dve_steps)

                    def own_exp(x, out, k, r, q):
                        st.link(dve.tensor_scalar(k, x, 1 / math.log(2.0), ROUND, ALU.mult, ALU.add))
                        st.link(dve.tensor_scalar(k, k, -ROUND, -126.0, ALU.add, ALU.max))
                        st.link(dve.scalar_tensor_tensor(r, k, -LN2_HI, x, ALU.mult, ALU.add))
                        st.link(dve.scalar_tensor_tensor(r, k, -LN2_LO, r, ALU.mult, ALU.add))
                        st.link(dve.tensor_scalar(q, r, 1 / 5040.0, None, ALU.mult))
                        for c in (1 / 720.0, 1 / 120.0, 1 / 24.0, 1 / 6.0, 0.5, 1.0):
                            st.link(dve.scalar_tensor_tensor(q, q, c, r, ALU.add, ALU.mult))
                        st.link(dve.tensor_scalar(k.bitcast(I32), k, 127.0, 2.0 ** 23, ALU.add, ALU.mult))
                        st.link(dve.scalar_tensor_tensor(out, q, 1.0, k, ALU.add, ALU.mult))

                    def tt(out, a, b, op):
                        st.link(dve.tensor_tensor(out, a, b, op))

                    S = lambda i: small[:, i, :]
                    log_dt_, dt, x, decay, theta, kk, theta_c, tmp = (S(i) for i in range(8))
                    r_, q_ = S(8), S(9)
                    sin_, cos_ = S(12), S(13)
                    a_re, a_im = vec[:, V_ARE:V_ARE + PAIRS], vec[:, V_AIM:V_AIM + PAIRS]
                    ab_re, ab_im, den, k_re, k_im, nr = S(14), S(15), S(16), S(17), S(18), S(19)
                    dve.wait_ge(small_landed, 80)
                    own_exp(log_dt_, dt, kk, r_, q_)
                    tt(x, a_re, dt, ALU.mult)
                    own_exp(x, decay, kk, r_, q_)
                    tt(theta, a_im, dt, ALU.mult)
                    reduce_angle(dve, st, theta, kk, theta_c, tmp)
                    dve.sem_inc(poles_angle, 1)
                    norm_scale(dve, 0, vec[:, V_G1:V_G1 + KD], hT)
                    dve.wait_ge(poles_sincos, 2)
                    tt(ab_re, decay, cos_, ALU.mult)
                    tt(ab_im, decay, sin_, ALU.mult)
                    tt(den, a_re, a_re, ALU.mult)
                    tt(tmp, a_im, a_im, ALU.mult)
                    tt(den, den, tmp, ALU.add)
                    st.link(dve.reciprocal(den, den))
                    st.link(dve.tensor_scalar(nr, ab_re, -1.0, None, ALU.add))
                    tt(k_re, nr, a_re, ALU.mult)
                    tt(tmp, ab_im, a_im, ALU.mult)
                    tt(k_re, k_re, tmp, ALU.add)
                    tt(k_re, k_re, den, ALU.mult)
                    tt(k_im, ab_im, a_re, ALU.mult)
                    tt(tmp, nr, a_im, ALU.mult)
                    tt(k_im, k_im, tmp, ALU.subtract)
                    tt(k_im, k_im, den, ALU.mult)
                    st.step(dve.tensor_copy(S(20), cos_))
                    st.step(dve.tensor_copy(S(21), sin_))
                    st.step(dve.tensor_copy(S(30), cos_))
                    st.link(dve.tensor_copy(S(31), sin_))
                    dve.sem_inc(poles_ready, 1)
                    dve.wait_ge(blocks_ready, 1)
                    wide = lambda v: v.unsqueeze(2).broadcast_to([P, PAIRS, 32])
                    tt(bbar[:, 0, :, :], b_blocks[:, 0, :, :], wide(k_re), ALU.mult)
                    tt(bb_tmp[:, 0, :, :], b_blocks[:, 1, :, :], wide(k_im), ALU.mult)
                    tt(bbar[:, 0, :, :], bbar[:, 0, :, :], bb_tmp[:, 0, :, :], ALU.subtract)
                    tt(bbar[:, 1, :, :], b_blocks[:, 1, :, :], wide(k_re), ALU.mult)
                    tt(bb_tmp[:, 0, :, :], b_blocks[:, 0, :, :], wide(k_im), ALU.mult)
                    tt(bbar[:, 1, :, :], bbar[:, 1, :, :], bb_tmp[:, 0, :, :], ALU.add)
                    dve.sem_inc(bbar_ready, 1)
                    st.step(dve.memset(pow_a[:, 0, :, 0:1], 1.0))
                    st.link(dve.memset(pow_a[:, 1, :, 0:1], 0.0))
                    powers(dve, st, pow_a, 4, [S(20), S(21), S(22), S(23)], pow_tmp_a, skip=5)
                    dve.sem_inc(pow_a_ready, 1)

                    def turn_back(p):
                        dve.wait_ge(prod_dve, 2 * (p + 1))
                        dve.tensor_tensor(prods[0], prods[0], prods[1], ALU.subtract).then_inc(turned_back, 1)
                        dve.wait_ge(prod_pool, p + 1)
                        dve.tensor_tensor(prods[2], prods[2], prods[3], ALU.add).then_inc(turned_back, 1)

                    def pair(p):
                        if p:
                            turn_back(p - 1)
                        cs, sn = tabs[:, p % 2, 0, :], tabs[:, p % 2, 1, :]
                        xr, xi = ps[:, 4, :], ps[:, 5, :]
                        m1, m2, m3, m4 = (rotin[:, i, :] for i in range(4))
                        dve.wait_ge(tab_ready, p + 1)
                        dve.wait_ge(x_done, p + 1)
                        dve.tensor_tensor(m1, xr, cs, ALU.mult)
                        dve.tensor_tensor(m2, xi, sn, ALU.mult)
                        dve.tensor_tensor(m3, xi, cs, ALU.mult)
                        dve.tensor_tensor(m4, xr, sn, ALU.mult).then_inc(x_free, 1)
                        dve.wait_ge(x_free, p + 1)
                        st.step(dve.tensor_tensor(m1, m1, m2, ALU.add))
                        st.step(dve.tensor_tensor(m3, m3, m4, ALU.subtract))
                        if p >= 2:
                            dve.wait_ge(prod_pool, p - 1)
                        st.settle()
                        rate = decay[:, p:p + 1].broadcast_to([P, L])
                        for s, v in enumerate((m1, m3)):
                            dve.tensor_tensor_scan(scanned[:, p % 2, s, :], rate, v, 0.0, ALU.mult, ALU.add).then_inc(scan_done, 1)
                        dve.wait_ge(scan_done, 2 * (p + 1))
                        if p:
                            dve.wait_ge(y_done, p)
                        dve.tensor_tensor(prods[0], scanned[:, p % 2, 0, :], cs, ALU.mult).then_inc(prod_dve, 1)
                        dve.tensor_tensor(prods[1], scanned[:, p % 2, 1, :], sn, ALU.mult).then_inc(prod_dve, 1)

                    def take_y(m):
                        dve.wait_ge(y_done, PER_TILE * (m + 1))
                        dve.scalar_tensor_tensor(ssmT[:, m, :], ssmT[:, m, :], vec[:, V_D + m:V_D + m + 1], ps[:, 6 + m % 2, :],
                                                 ALU.mult, ALU.add).then_inc(y_taken, 1)

                    rope_n = glu_n = gate_n = 0
                    for item in ORDER:
                        kind = item[1] if item[0] == "tile" else item[0]
                        if item[0] == "tile":
                            n = TILE_NUMBER[item]
                            src = ps[:, n % 4, :]
                            free = bank_free[n % 4]
                        if kind == "rope":
                            dst = (qT if item[1] == "q" else kT)[:, item[2], :]
                            dve.wait_ge(raw_ready, 5 * (rope_n + 1))
                            turn_c, turn_s = raw[:, item[2] % 2, :], swapped[:, item[2] % 2, :]
                            st.step(dve.tensor_tensor(turn_c, turn_c, cosT[:], ALU.mult))
                            st.link(dve.tensor_tensor(turn_s, turn_s, sinT[:], ALU.mult))
                            dve.tensor_tensor(dst, turn_c, turn_s, ALU.add).then_inc(roped, 1)
                            rope_n += 1
                            dve.wait_ge(roped, rope_n)
                        elif kind == "pair":
                            pair(item[1])
                            if item[1] > 1 and item[1] % PER_TILE == 1:
                                take_y(item[1] // PER_TILE - 1)
                        elif kind == "pairs_end":
                            turn_back(PAIRS - 1)
                            take_y(3)
                        elif kind == "glu_val":
                            dve.wait_ge(tiles_done, n + 1)
                            dve.wait_ge(glu_sig, glu_n + 1)
                            dve.tensor_tensor(gluT[:, item[2], :], src, glu_sigmoid[:, glu_n % 2, :], ALU.mult).then_inc(glu_ready, 1)
                            glu_n += 1
                            dve.wait_ge(glu_ready, glu_n)
                            dve.sem_inc(free, 1)
                        elif kind == "attention_start":
                            attend_max(dve, st, 0)
                            attend_max(dve, st, 1)
                        elif kind == "attention":
                            for i in range(16):
                                if i + 2 < 16:
                                    attend_max(dve, st, i + 2)
                                attend_out(dve, st, i)
                        elif kind == "gate":
                            m, b = item[2], item[3]
                            ny = TILE_NUMBER[("tile", "branch", m, b)]
                            y = ps[:, ny % 4, :]
                            dve.wait_ge(tiles_done, ny + 1)
                            dve.wait_ge(gate_sig, gate_n + 1)
                            if b == 0:
                                dve.tensor_tensor(merged[:, m, :], y, sig[:, gate_n % 2, :], ALU.mult).then_inc(gate_used, 1)
                            else:
                                st.link(dve.tensor_tensor(gated[:, 0, :], y, sig[:, gate_n % 2, :], ALU.mult))
                                dve.wait_ge(gate_used, gate_n)
                                dve.tensor_tensor(merged[:, m, :], merged[:, m, :], gated[:, 0, :], ALU.add).then_inc(gate_used, 1)
                            gate_n += 1
                            dve.wait_ge(gate_used, gate_n)
                            dve.sem_inc(bank_free[ny % 4], 1)
                        elif kind == "out":
                            dve.wait_ge(tiles_done, n + 1)
                            dve.tensor_tensor(xT[:, item[2], :], xT[:, item[2], :], src, ALU.add).then_inc(x_mixed, 1)
                            dve.wait_ge(x_mixed, item[2] + 1)
                            dve.sem_inc(free, 1)
                        elif kind == "norm2":
                            norm_scale(dve, 1, vec[:, V_G2:V_G2 + KD], hT)
                            dve.sem_inc(list_steps, 1)
                            dve.sem_inc(head_steps, 1)
                            dve.sem_inc(pick_steps, 1)
                        elif kind == "first_score":
                            h = item[2]
                            dve.wait_ge(first_scores_ready, h + 1)
                            pick_first_lists(dve, h)
                            for _ in pick_head(dve, 0, h):
                                pass
                    settle_picks(dve, 0)

        poles_angle = sem("poles_angle")
        poles_sincos = sem("poles_sincos")
        freed = [sem(f"row_free{j}") for j in range(NB)]
        picks_ready = sem("picks_ready")
        exp_ready = sem("exp_ready")
        shifted = sem("shifted")
        idx_staged = sem("idx_staged")
        act_copied = sem("act_copied")
        acts_ready = sem("acts_ready")
        gelu_ready = sem("gelu_ready")
        w_ready = sem("w_ready")
        w_staged = sem("w_staged")
        diag_ready = sem("diag_ready")
        acc_done = sem("acc_done")
        acc_free = sem("acc_free")
        back_done = sem("back_done")
        back_taken = sem("back_taken")
        h_copied = sem("h_copied")
        zeroed = sem("zeroed")
        first_steps = sem("first_steps")
        list_steps = sem("list_steps")
        head_steps = sem("head_steps")
        pick_steps = sem("pick_steps")
        scores_ready = sem("scores_ready")
        sum_cleared = sem("sum_cleared")
        sum_ready = sem("sum_ready")
        sum_read = sem("sum_read")
        pool_turn = sem("pool_turn")
        dve_turn = sem("dve_turn")

        def peer(layer):
            with nc.Block() as block:
                @block.gpsimd
                def _(pool):
                    for j in range(NB):
                        if j not in LATE_ROWS:
                            pool.sem_inc(freed[j], 1)
                    with pool.Fori(0, NT) as t:
                        pool.wait_ge(picks_ready, t + 1)
                        pool.sem_inc(pool_turn, 1)
                        for half, table in enumerate((table_u, table_v)):
                            with pool.Fori(0, ROUNDS // 2) as i2:
                                for par in range(2):
                                    rnd = t * (2 * ROUNDS) + half * ROUNDS + i2 * 2 + par
                                    stage = idx_stage[:, par, :]
                                    for j in range(NB):
                                        pool.wait_ge(freed[j], rnd + 1)
                                        if j == 0:
                                            pool.tensor_copy(stage, expert[
                                                :, bass.ds(t * PICKS + (i2 * 2 + par) * NB, NB)]).then_inc(idx_staged, 1)
                                            pool.wait_ge(idx_staged, rnd + 1)
                                        pool.sem_inc(pool_turn, 1)
                                        pool.indirect_dma_start(rows[:, j, :], None, table,
                                                                bass.IndirectOffsetOnAxis(stage[:, j:j + 1], 0)).then_inc(land[j], 16)

                @block.vector
                def _(dve):
                    dve.memset(zeros, 0.0).then_inc(zeroed, 1)
                    def work(t, nxt):
                        dve.tensor_copy(h_now, h_tok.rearrange("p t d -> p (t d)")[:, bass.ds(t * D, D)]).then_inc(h_copied, 1)
                        dve.wait_ge(h_copied, t + 1)
                        dve.sem_inc(dve_turn, 1)
                        with dve.Fori(0, ROUNDS) as i:
                            rnd = t * (2 * ROUNDS) + i
                            if nxt is not None:
                                dve.wait_ge(scores_ready, i + 1)
                                dve.sem_inc(dve_turn, 1)
                            picks = pick_list(dve, t, i) if nxt is not None else iter(())
                            for j in range(NB):
                                dve.wait_ge(land[j], (layer * (NT * 2 * ROUNDS) + rnd) * 16 + 16)
                                dve.tensor_tensor_reduce(rows[:, j, :], rows[:, j, :], h_now, 1.0, 0.0, ALU.mult, ALU.add,
                                                         act_stage[:, j:j + 1]).then_inc(freed[j], 1)
                                next(picks, None)
                            assert next(picks, None) is None
                            dve.wait_ge(freed[NB - 1], rnd + 2)
                            dve.tensor_copy(act_all[:, bass.ts(i, NB)], act_stage).then_inc(act_copied, 1)
                            dve.wait_ge(act_copied, t * ROUNDS + i + 1)
                        dve.sem_inc(acts_ready, 1)
                        dve.wait_ge(gelu_ready, t + 1)
                        dve.tensor_tensor(w_all, gelu_all, gates[:, bass.ds(t * PICKS, PICKS)], ALU.mult).then_inc(w_ready, 1)
                        dve.wait_ge(w_ready, t + 1)
                        dve.sem_inc(dve_turn, 1)
                        dve.wait_ge(sum_read, t + 1)
                        dve.sem_inc(dve_turn, 1)
                        dve.memset(dve_sum, 0.0).then_inc(sum_cleared, 1)
                        dve.wait_ge(sum_cleared, t + 1)
                        dve.sem_inc(dve_turn, 1)
                        if nxt is not None:
                            dve.wait_ge(list_steps, (t + 1) * (16 * LIST_STEPS) + 1)
                            dve.sem_inc(dve_turn, 1)
                        with dve.Fori(0, PH) as h:
                            picks = pick_head(dve, nxt, h) if nxt is not None else iter(())
                            for part in range(ROUNDS // PH):
                                i = h * (ROUNDS // PH) + part
                                rnd = t * (2 * ROUNDS) + ROUNDS + i
                                dve.tensor_copy(w_stage, w_all[:, bass.ds(i * NB, NB)]).then_inc(w_staged, 1)
                                dve.wait_ge(w_staged, t * ROUNDS + i + 1)
                                for j in PE_SLOTS:
                                    dve.wait_ge(freed[j], rnd + 1)
                                    dve.tensor_scalar(diag[:, j, :], ident[:], w_stage[:, j:j + 1], None,
                                                      ALU.mult).then_inc(diag_ready, 1)
                                for n, j in enumerate(DVE_SLOTS):
                                    for _ in range(4):
                                        next(picks, None)
                                    dve.wait_ge(freed[DVE_SLOTS[n - 1]], rnd + (2 if n else 1))
                                    dve.wait_ge(land[j], (layer * (NT * 2 * ROUNDS) + rnd) * 16 + 16)
                                    dve.scalar_tensor_tensor(dve_sum, rows[:, j, :], w_stage[:, j:j + 1], dve_sum,
                                                             ALU.mult, ALU.add).then_inc(freed[j], 1)
                                dve.wait_ge(freed[DVE_SLOTS[-1]], rnd + 2)
                                dve.wait_ge(diag_ready, (t * ROUNDS + i) * len(PE_SLOTS) + len(PE_SLOTS))
                            assert next(picks, None) is None
                        dve.sem_inc(sum_ready, 1)
                        if nxt is not None:
                            settle_picks(dve, nxt)

                    with dve.Fori(0, NT - 1) as t:
                        work(t, t + 1)
                    work(NT - 1, None)
                    dve.tensor_scalar(layer_base[:], layer_base[:], float(EXPERTS), None, ALU.add)
                    for t in range(NT):
                        for half in range(2):
                            n = 2 * t + half
                            dve.wait_ge(back_done, n + 1)
                            dst = xT[:, 4 * half:4 * half + 4, t * P:(t + 1) * P]
                            dve.tensor_tensor(dst, dst, ps[:, n % 4, :].rearrange("p (k c) -> p k c", k=4),
                                              ALU.add).then_inc(back_taken, 1)

                @block.scalar
                def _(act):
                    act.sem_inc(acc_free, 1)
                    for item in REST_ORDER:
                        if item[0] == "tile":
                            query_evacuate(act, item)

                    def work(t, nxt):
                        act.wait_ge(acts_ready, t + 1)
                        act.activation(gelu_all, act_all, ACT.Gelu_apprx_tanh).then_inc(gelu_ready, 1)
                        if nxt is not None:
                            act.wait_ge(shifted, nxt + 1)
                            act.activation(gate_e, gate_e, ACT.Exp).then_inc(exp_ready, 1)
                        act.wait_ge(acc_done, t + 1)
                        act.copy(out_tok.rearrange("p t d -> p (t d)")[:, bass.ds(t * D, D)],
                                 ps[:, 4:6, :].rearrange("p a t -> p (a t)")).then_inc(acc_free, 1)

                    with act.Fori(0, NT - 1) as t:
                        work(t, t + 1)
                    work(NT - 1, None)

                @block.tensor
                def _(pe):
                    pe.wait_ge(zeroed, 1)
                    pe.sem_inc(sum_read, 1)
                    for item in REST_ORDER:
                        if item[0] == "tile":
                            query_tile(pe, item)
                        else:
                            pe.wait_ge(tiles_done, TILE_NUMBER[("tile", "wq", 2 * SIDE_HEADS - 1)] + 1)
                            for j in LATE_ROWS:
                                pe.sem_inc(freed[j], 1)
                    with pe.Fori(0, NT) as t:
                        pe.wait_ge(acc_free, t + 1)
                        for half in range(2):
                            pe.matmul(ps[:, 4 + half, :], zeros, cosT[:], start=True, stop=False)
                        with pe.Fori(0, ROUNDS) as i:
                            rnd = t * (2 * ROUNDS) + ROUNDS + i
                            for n, j in enumerate(PE_SLOTS):
                                pe.wait_ge(diag_ready, (t * ROUNDS + i) * len(PE_SLOTS) + n + 1)
                                pe.wait_ge(land[j], (layer * (NT * 2 * ROUNDS) + rnd) * 16 + 16)
                                for half in range(2):
                                    mm = pe.matmul(ps[:, 4 + half, :], diag[:, j, :], rows[:, j, half * L:(half + 1) * L],
                                                   start=False, stop=False)
                                mm.then_inc(freed[j], 1)
                        pe.wait_ge(sum_ready, t + 1)
                        for half in range(2):
                            mm = pe.matmul(ps[:, 4 + half, :], ident[:], dve_sum[:, half * L:(half + 1) * L], start=False, stop=True)
                        mm.then_inc(sum_read, 1)
                        pe.wait_ge(sum_read, t + 2)
                        pe.sem_inc(acc_done, 1)
                    pe.wait_ge(acc_free, NT + 1)
                    for t in range(NT):
                        for half in range(2):
                            n = 2 * t + half
                            if n >= 4:
                                pe.wait_ge(back_taken, n - 3)
                            for k in range(4):
                                c = 4 * half + k
                                mm = pe.transpose(ps[:, n % 4, k * P:(k + 1) * P], out_tok[:, t, c * P:(c + 1) * P], ident[:])
                            mm.then_inc(back_done, 1)

        nc.all_engine_barrier(sems_to_clear=range(min(s.num for s in sems), max(s.num for s in sems) + 1))
        with nc.Fori(0, DEPTH) as layer:
            mixer(layer)
            peer(layer)
            nc.all_engine_barrier(sems_to_clear=range(min(s.num for s in sems), max(s.num for s in sems) + 1))

        with nc.Block() as block:
            @block.scalar
            def _(act):
                norm_squares(act)
                norm_root(act, 0)

            @block.tensor
            def _(pe):
                norm_mean(pe, 0)

            @block.vector
            def _(dve):
                dve.wait_ge(small_landed, 16)
                norm_scale(dve, 0, fing, hT)

            @block.sync
            def _(sp):
                sp.dma_start(fing, final_g).then_inc(small_landed, 16)
                sp.wait_ge(normed, KD + 1)
                sp.dma_start(out_cm, hT[:].rearrange("p a t -> p (a t)")).then_inc(out_stored, 16)
                sp.wait_ge(out_stored, 16)


def pack_weights(w_in, pool_w, pool_proj, ssm_glu, ssm_proj, attn_proj, w_out, peer_wq):
    def blocks(w, cols):
        part = w[:, cols]
        return part.reshape(-1, P, part.shape[1]).transpose(1, 0, 2).reshape(P, -1)

    out = np.zeros((DEPTH, CHUNKS, P, CHUNK), w_in.dtype)
    for l in range(DEPTH):
        put = lambda c, a: out[l, c, :, :a.shape[1]].__setitem__(slice(None), a)
        for c in range(13):
            put(c, blocks(w_in[l], slice(256 * c, 256 * c + 256)))
        put(C_MIX, pool_w[l].transpose(1, 0, 2).reshape(P, -1))
        for i in range(2):
            cols = np.r_[256 * i:256 * i + 256, 512 + 256 * i:512 + 256 * i + 256]
            put(C_GLU + i, blocks(ssm_glu[l], cols))
        for m in range(KD):
            col = slice(P * m, P * m + P)
            parts = []
            for b, w in enumerate((pool_proj[l], ssm_proj[l], attn_proj[l])):
                at = W_IN_MAIN + D * b + P * m
                parts += [blocks(w, col), blocks(w_in[l], slice(at, at + P))]
            both = np.concatenate(parts, axis=1)
            put(C_MERGE + 2 * m, both[:, :CHUNK])
            put(C_MERGE + 2 * m + 1, both[:, CHUNK:])
        for c in range(4):
            put(C_OUT + c, blocks(w_out[l], slice(256 * c, 256 * c + 256)))
        for h in range(PH):
            put(C_SIDE + h if h < SIDE_HEADS else C_WQ + h - SIDE_HEADS, blocks(peer_wq[l], slice(256 * h, 256 * h + 256)))
    return out.reshape(DEPTH * CHUNKS * P, CHUNK)


def kernel(x, positions, norm1_g, w_in, pool_w, pool_scale, pool_proj, ssm_a_re, ssm_a_im, ssm_log_dt,
           ssm_b_re, ssm_b_im, ssm_c_re, ssm_c_im, ssm_d, ssm_glu, ssm_proj, attn_proj, w_out, norm2_g,
           peer_wq, peer_k1, peer_k2, peer_u, peer_v, final_g):
    import concourse.bacc as bacc
    from concourse.bass_utils import run_bass_kernel_spmd

    a = {k: np.asarray(v) for k, v in locals().items() if k not in ("bacc", "run_bass_kernel_spmd")}
    columns = lambda v: v.reshape(DEPTH, -1, P).transpose(0, 2, 1)
    states = lambda v: v.reshape(DEPTH, PAIRS, 2 * 64).transpose(0, 2, 1)
    b_lay = lambda v: v.reshape(DEPTH, PAIRS, 2 * 64, 16).transpose(0, 2, 1, 3).reshape(DEPTH, P, -1)
    c_lay = lambda v: v.reshape(DEPTH, PAIRS, 2, 16, 64).transpose(0, 2, 4, 1, 3).reshape(DEPTH, P, -1)
    arrays = {
        "x_cm": a["x"][0].reshape(L, KD, P).transpose(2, 1, 0).reshape(P, KD * L),
        "positions": a["positions"].astype(np.int32).reshape(1, L),
        "inv_freq": np.tile(np.power(np.float32(10000.0), -np.arange(32, dtype=np.float32) / np.float32(32)), 4)
                      .astype(np.float32).reshape(P, 1),
        "weights": pack_weights(*(a[n] for n in ("w_in", "pool_w", "pool_proj", "ssm_glu", "ssm_proj", "attn_proj",
                                                 "w_out", "peer_wq"))),
        "keys": np.concatenate([a["peer_k1"].transpose(0, 2, 1), a["peer_k2"].transpose(0, 2, 1)], axis=2)
                  .reshape(DEPTH * P, 2 * NKEYS),
        "vecs": np.concatenate([columns(a["norm1_g"]), columns(a["norm2_g"]), columns(a["pool_scale"]), columns(a["ssm_d"]),
                                states(a["ssm_a_re"]), states(a["ssm_a_im"])], axis=2).reshape(DEPTH * P, V_END),
        "log_dt": a["ssm_log_dt"].reshape(DEPTH, PAIRS, 2).transpose(0, 2, 1).reshape(DEPTH * 2, PAIRS),
        "ssm_bc": np.concatenate([b_lay(a["ssm_b_re"]), b_lay(a["ssm_b_im"]), c_lay(a["ssm_c_re"]), c_lay(a["ssm_c_im"])],
                                 axis=2).reshape(DEPTH * P, -1),
        "table_u": a["peer_u"].reshape(DEPTH * EXPERTS, D),
        "table_v": a["peer_v"].reshape(DEPTH * EXPERTS, D),
        "final_g": a["final_g"].reshape(KD, P).T,
    }
    arrays = {k: np.ascontiguousarray(v) for k, v in arrays.items()}
    nc = bacc.Bacc("TRN2", target_bir_lowering=False, num_devices=1)
    args = [nc.dram_tensor(k, v.shape, mybir.dt.from_np(v.dtype), kind="ExternalInput").ap() for k, v in arrays.items()]
    args.append(nc.dram_tensor("out_cm", (P, KD * L), F32, kind="ExternalOutput").ap())
    trunk(nc, *args)
    r = run_bass_kernel_spmd(nc, [arrays], core_ids=[0])
    out = r.results[0]["out_cm"].reshape(P, KD, L).transpose(2, 1, 0).reshape(1, L, D)
    return np.ascontiguousarray(out)
```
